# Optimizing a Trainium2 kernel written in Bass

```python
import jax, jax.numpy as jnp
from jax import lax
import numpy as np

D_MODEL = 2048
BATCH = 1
SEQ = 256
DEPTH = 1

ATT_HEAD_DIM = 128
ATT_HEADS = D_MODEL // ATT_HEAD_DIM
ATT_KV_HEADS = ATT_HEADS // 4
ATT_GROUP = ATT_HEADS // ATT_KV_HEADS
WINDOW = 128
BLOCK = 128
ROPE_THETA = 10000.0

RWKV_HEAD_DIM = 64
RWKV_HEADS = D_MODEL // RWKV_HEAD_DIM
RWKV_DIM = RWKV_HEADS * RWKV_HEAD_DIM
DECAY_LORA = max(32, int(round(1.8 * D_MODEL ** 0.5 / 32)) * 32)
ICLR_LORA = max(32, int(round(1.8 * D_MODEL ** 0.5 / 32)) * 32)
GATE_LORA = max(32, int(round(0.6 * D_MODEL ** 0.8 / 32)) * 32)

D_FF = 4 * D_MODEL
NORM_EPS = 1e-6
GN_EPS = 64e-5
MASK_VALUE = -1e30

Q_COLS = ATT_HEADS * ATT_HEAD_DIM
KV_COLS = ATT_KV_HEADS * ATT_HEAD_DIM
SHIFT_SIZES = [RWKV_DIM, RWKV_DIM, RWKV_DIM, DECAY_LORA, DECAY_LORA, ICLR_LORA, ICLR_LORA, GATE_LORA]
SHIFT_COLS = sum(SHIFT_SIZES)
IN_SIZES = [Q_COLS, KV_COLS, KV_COLS, SHIFT_COLS, D_MODEL, D_MODEL]
IN_COLS = sum(IN_SIZES)

kernel_name = 'hybrid_swa_rwkv7_sandwich_block'

def _split(t, sizes):
    idx = [int(i) for i in np.cumsum(sizes)[:-1]]
    return jnp.split(t, idx, axis=-1)

def rms_norm(x, gain):
    x32 = x.astype(jnp.float32)
    y = x32 * lax.rsqrt(jnp.mean(x32 * x32, axis=-1, keepdims=True) + NORM_EPS)
    return (y * gain.astype(jnp.float32)).astype(x.dtype)

def rope_tables(T):
    pos = jnp.arange(T, dtype=jnp.float32)
    inv_freq = ROPE_THETA ** (-jnp.arange(0, ATT_HEAD_DIM, 2, dtype=jnp.float32) / ATT_HEAD_DIM)
    ang = pos[:, None] * inv_freq[None, :]
    return jnp.cos(ang), jnp.sin(ang)

def apply_rope(x, cos, sin):
    x1, x2 = jnp.split(x.astype(jnp.float32), 2, axis=-1)
    return jnp.concatenate([x1 * cos - x2 * sin, x2 * cos + x1 * sin], axis=-1).astype(x.dtype)

def banded_gqa_attention(q, k, v, sink):
    B, T = q.shape[0], q.shape[1]
    nb = T // BLOCK
    qb = q.reshape(B, nb, BLOCK, ATT_KV_HEADS, ATT_GROUP, ATT_HEAD_DIM)

    def windows(t):
        tp = jnp.pad(t, ((0, 0), (BLOCK, BLOCK), (0, 0), (0, 0)))
        tp = tp.reshape(B, nb + 2, BLOCK, ATT_KV_HEADS, ATT_HEAD_DIM)
        return jnp.concatenate([tp[:, :-2], tp[:, 1:-1], tp[:, 2:]], axis=2)

    kw, vw = windows(k), windows(v)
    scale = ATT_HEAD_DIM ** -0.5
    s = jnp.einsum('bnqkgd,bnskd->bnkgqs', qb, kw, preferred_element_type=jnp.float32) * scale
    qi = jnp.arange(BLOCK)[:, None]
    sj = jnp.arange(3 * BLOCK)[None, :]
    in_window = jnp.abs(sj - BLOCK - qi) <= WINDOW
    kpos = jnp.arange(nb)[:, None] * BLOCK - BLOCK + jnp.arange(3 * BLOCK)[None, :]
    in_range = (kpos >= 0) & (kpos < T)
    valid = in_window[None, :, :] & in_range[:, None, :]
    s = jnp.where(valid[None, :, None, None], s, MASK_VALUE)
    sink_col = jnp.broadcast_to(
        sink.astype(jnp.float32).reshape(ATT_KV_HEADS, ATT_GROUP)[None, None, :, :, None, None],
        s.shape[:-1] + (1,))
    p = jax.nn.softmax(jnp.concatenate([s, sink_col], axis=-1), axis=-1)[..., :-1]
    o = jnp.einsum('bnkgqs,bnskd->bnqkgd', p.astype(vw.dtype), vw, preferred_element_type=jnp.float32)
    return o.reshape(B, T, ATT_HEADS * ATT_HEAD_DIM)

def centred_token_shift(c, mu):
    prev = jnp.pad(c[:, :-1], ((0, 0), (1, 0), (0, 0)))
    nxt = jnp.pad(c[:, 1:], ((0, 0), (0, 1), (0, 0)))
    return c + mu * (0.5 * (prev + nxt) - c)

def wkv7_scan(r, decay, k, v, a_vec, b_vec, reverse):
    B = r.shape[0]
    xs = tuple(jnp.moveaxis(t, 1, 0) for t in (r, decay, k, v, a_vec, b_vec))
    S0 = jnp.zeros((B, RWKV_HEADS, RWKV_HEAD_DIM, RWKV_HEAD_DIM), jnp.float32)

    def step(S, inp):
        r_t, w_t, k_t, v_t, a_t, b_t = inp
        sa = jnp.einsum('bhij,bhj->bhi', S, a_t)
        S = S * w_t[:, :, None, :] + sa[..., None] * b_t[:, :, None, :] + v_t[..., None] * k_t[:, :, None, :]
        y = jnp.einsum('bhij,bhj->bhi', S, r_t)
        return S, y

    _, ys = lax.scan(step, S0, xs, reverse=reverse)
    return jnp.moveaxis(ys, 0, 1)

def rwkv7_direction(r, k, v, kk, wd, ad, w0, w_up, a0, a_up, k_a, reverse):
    B, T = r.shape[0], r.shape[1]
    heads = lambda t: t.reshape(B, T, RWKV_HEADS, RWKV_HEAD_DIM)
    w_log = -jax.nn.softplus(-(w0.astype(jnp.float32) + jnp.tanh(wd) @ w_up.astype(jnp.float32))) - 0.5
    decay = jnp.exp(-jnp.exp(w_log))
    a = jax.nn.sigmoid(a0.astype(jnp.float32) + ad @ a_up.astype(jnp.float32))
    k_mod = k * (1.0 + (a - 1.0) * k_a.astype(jnp.float32))
    y = wkv7_scan(heads(r), heads(decay), heads(k_mod), heads(v), -kk, kk * heads(a), reverse)
    return y, k_mod

def rwkv7_bidirectional(cols, mu, w0_fwd, w_up_fwd, w0_bwd, w_up_bwd, a0_fwd, a_up_fwd,
                        a0_bwd, a_up_bwd, g_up, k_k, k_a, r_k, ln_x_gain, ln_x_bias):
    c = centred_token_shift(cols.astype(jnp.float32), mu.astype(jnp.float32))
    r, k, v, wd_f, wd_b, ad_f, ad_b, gd = _split(c, SHIFT_SIZES)
    B, T = r.shape[0], r.shape[1]
    heads = lambda t: t.reshape(B, T, RWKV_HEADS, RWKV_HEAD_DIM)
    kk = heads(k * k_k.astype(jnp.float32))
    kk = kk / jnp.maximum(jnp.sqrt(jnp.sum(kk * kk, axis=-1, keepdims=True)), 1e-12)
    y_f, k_f = rwkv7_direction(r, k, v, kk, wd_f, ad_f, w0_fwd, w_up_fwd, a0_fwd, a_up_fwd, k_a, False)
    y_b, k_b = rwkv7_direction(r, k, v, kk, wd_b, ad_b, w0_bwd, w_up_bwd, a0_bwd, a_up_bwd, k_a, True)
    y = y_f + y_b
    mean = jnp.mean(y, axis=-1, keepdims=True)
    var = jnp.mean(jnp.square(y - mean), axis=-1, keepdims=True)
    y = ((y - mean) * lax.rsqrt(var + GN_EPS)).reshape(B, T, RWKV_DIM)
    y = y * ln_x_gain.astype(jnp.float32) + ln_x_bias.astype(jnp.float32)
    k_bonus = heads(0.5 * (k_f + k_b))
    r_k_h = r_k.astype(jnp.float32).reshape(RWKV_HEADS, RWKV_HEAD_DIM)
    bonus = jnp.sum(heads(r) * k_bonus * r_k_h, axis=-1, keepdims=True) * heads(v)
    g = jax.nn.sigmoid(gd) @ g_up.astype(jnp.float32)
    return (y + bonus.reshape(B, T, RWKV_DIM)) * g

def setup_inputs(seed: int = 0) -> dict:
    key = jax.random.key(seed)
    ks = jax.random.split(key, 26)
    f32 = jnp.float32
    nrm = lambda k, shape, scale: scale * jax.random.normal(k, shape, f32)
    gain = lambda k: 1.0 + 0.05 * jax.random.normal(k, (DEPTH, D_MODEL), f32)
    return {
        'x': jax.random.normal(ks[0], (BATCH, SEQ, D_MODEL), f32),
        'norm_pre_mix': gain(ks[1]),
        'w_in': nrm(ks[2], (DEPTH, D_MODEL, IN_COLS), D_MODEL ** -0.5),
        'mu_shift': jax.random.uniform(ks[3], (DEPTH, SHIFT_COLS), f32),
        'attn_sink': nrm(ks[4], (DEPTH, ATT_HEADS), 0.5),
        'w0_fwd': jax.random.uniform(ks[5], (DEPTH, RWKV_DIM), f32, -4.0, 0.5),
        'w_up_fwd': nrm(ks[6], (DEPTH, DECAY_LORA, RWKV_DIM), 0.1),
        'w0_bwd': jax.random.uniform(ks[7], (DEPTH, RWKV_DIM), f32, -4.0, 0.5),
        'w_up_bwd': nrm(ks[8], (DEPTH, DECAY_LORA, RWKV_DIM), 0.1),
        'a0_fwd': nrm(ks[9], (DEPTH, RWKV_DIM), 0.1),
        'a_up_fwd': nrm(ks[10], (DEPTH, ICLR_LORA, RWKV_DIM), 0.1),
        'a0_bwd': nrm(ks[11], (DEPTH, RWKV_DIM), 0.1),
        'a_up_bwd': nrm(ks[12], (DEPTH, ICLR_LORA, RWKV_DIM), 0.1),
        'g_up': nrm(ks[13], (DEPTH, GATE_LORA, RWKV_DIM), GATE_LORA ** -0.5),
        'k_k': 0.85 + nrm(ks[14], (DEPTH, RWKV_DIM), 0.05),
        'k_a': 1.0 + nrm(ks[15], (DEPTH, RWKV_DIM), 0.05),
        'r_k': nrm(ks[16], (DEPTH, RWKV_DIM), 0.1),
        'ln_x_gain': gain(ks[17]),
        'ln_x_bias': nrm(ks[18], (DEPTH, RWKV_DIM), 0.01),
        'w_out': nrm(ks[19], (DEPTH, D_MODEL, D_MODEL), D_MODEL ** -0.5),
        'norm_post_mix': gain(ks[20]),
        'norm_pre_ffn': gain(ks[21]),
        'w_ffn_up': nrm(ks[22], (DEPTH, D_MODEL, D_FF), D_MODEL ** -0.5),
        'w_ffn_down': nrm(ks[23], (DEPTH, D_FF, D_MODEL), D_FF ** -0.5),
        'norm_post_ffn': gain(ks[24]),
    }

def reference(x, norm_pre_mix, w_in, mu_shift, attn_sink, w0_fwd, w_up_fwd, w0_bwd, w_up_bwd,
              a0_fwd, a_up_fwd, a0_bwd, a_up_bwd, g_up, k_k, k_a, r_k, ln_x_gain, ln_x_bias,
              w_out, norm_post_mix, norm_pre_ffn, w_ffn_up, w_ffn_down, norm_post_ffn):
    B, T, _ = x.shape
    cos, sin = rope_tables(T)
    h = x
    for l in range(DEPTH):
        xn = rms_norm(h, norm_pre_mix[l])
        cols = xn @ w_in[l]
        q, k, v, rw_cols, gate_attn, gate_rwkv = _split(cols, IN_SIZES)
        q = apply_rope(q.reshape(B, T, ATT_KV_HEADS, ATT_GROUP, ATT_HEAD_DIM),
                       cos[None, :, None, None, :], sin[None, :, None, None, :])
        k = apply_rope(k.reshape(B, T, ATT_KV_HEADS, ATT_HEAD_DIM),
                       cos[None, :, None, :], sin[None, :, None, :])
        v = v.reshape(B, T, ATT_KV_HEADS, ATT_HEAD_DIM)
        o_attn = banded_gqa_attention(q, k, v, attn_sink[l])
        o_rwkv = rwkv7_bidirectional(rw_cols, mu_shift[l], w0_fwd[l], w_up_fwd[l], w0_bwd[l],
                                     w_up_bwd[l], a0_fwd[l], a_up_fwd[l], a0_bwd[l], a_up_bwd[l],
                                     g_up[l], k_k[l], k_a[l], r_k[l], ln_x_gain[l], ln_x_bias[l])
        merged = (jax.nn.sigmoid(gate_attn.astype(jnp.float32)) * o_attn
                  + jax.nn.sigmoid(gate_rwkv.astype(jnp.float32)) * o_rwkv)
        mix = merged.astype(x.dtype) @ w_out[l]
        h = h + rms_norm(mix, norm_post_mix[l])
        hn = rms_norm(h, norm_pre_ffn[l])
        ff = jnp.square(jax.nn.relu(hn @ w_ffn_up[l])) @ w_ffn_down[l]
        h = h + rms_norm(ff, norm_post_ffn[l])
    return h


_drawn_inputs = setup_inputs


def setup_inputs(seed=0):
    import zlib

    import numpy as np

    out = dict(_drawn_inputs(seed))
    spreads = {}
    factors = {'attn_sink': 8.0, 'a0_fwd': 2.713, 'a0_bwd': 2.847, 'k_k': 3.049, 'ln_x_bias': 8.0}
    for name, (base, spread) in spreads.items():
        noise = np.random.default_rng([zlib.crc32(name.encode()), seed]).standard_normal(out[name].shape)
        drawn = base * np.exp(spread * noise) if base else spread * noise
        out[name] = __import__('jax').numpy.asarray(drawn.astype(out[name].dtype))
    for name, factor in factors.items():
        out[name] = (out[name] * factor).astype(out[name].dtype)
    return out
```

```python
from contextlib import ExitStack

import numpy as np

import concourse.bass as bass
from concourse import mybir

D = 2048
T = 256
P = 128
KT = D // P
HD = 128
KVH = 4
GRP = 4
PAIRS = D // P
DL = 96
GL = 256
FF = 4 * D
EPS = 1e-6
GN_EPS = 64e-5
DECAY_E = float(np.exp(-0.5))
P0SCALE = 2.0 ** 56
LV = 7

Q0, K0, V0 = 0, D, D + 512
SH0 = D + 1024
R0, RK0, RV0 = SH0, SH0 + D, SH0 + 2 * D
LO0 = SH0 + 3 * D
GA0 = LO0 + 4 * DL + GL
GR0 = GA0 + D

C_ID, C_GM, C_LM, C_MEAN, C_HALF, C_SEL = 0, 128, 128 + 512, 128 + 512 + 2 * LV * 128, 128 + 512 + 2 * LV * 128 + 128, 128 + 512 + 2 * LV * 128 + 256
C_SM = C_SEL + 2
C_END = C_SM + P
CA_COS, CA_SIN, CA_MASK, CA_END = 0, 256, 512, 1024

PARAMS_A = ["mu_shift", "w0_fwd", "w0_bwd", "a0_fwd", "a0_bwd"]
PARAMS_B = ["k_k", "k_a", "r_k", "ln_x_gain", "ln_x_bias", "norm_pre_mix", "norm_pre_ffn"]


class Sig:

    def __init__(self, sem, per=1):
        self.sem, self.per = sem, per

    def at(self, i, k=None):
        return self.per * i + (self.per if k is None else k)

    def before(self, i):
        return self.per * i


def constants():
    c = np.zeros((P, C_END), np.float32)
    s, t = np.arange(P)[:, None], np.arange(P)[None, :]
    c[:, C_ID:C_ID + P] = s == t
    c[:, C_GM:C_GM + 128] = s < t
    c[:, C_GM + 128:C_GM + 256] = s <= t
    c[:, C_GM + 256:C_GM + 384] = s > t
    c[:, C_GM + 384:C_GM + 512] = s >= t
    for l in range(LV):
        m = 1 << l
        sib = (s // m // 2) == (t // m // 2)
        fwd = sib & (t // m % 2 == 1) & (s // m % 2 == 0)
        bwd = sib & (t // m % 2 == 0) & (s // m % 2 == 1)
        c[:, C_LM + l * P:C_LM + (l + 1) * P] = fwd
        c[:, C_LM + (LV + l) * P:C_LM + (LV + l + 1) * P] = bwd
    same = (s // 64) == (t // 64)
    c[:, C_MEAN:C_MEAN + P] = same / 64.0
    c[:, C_HALF:C_HALF + P] = same * 0.5
    c[:, C_SM:C_SM + P] = same / P0SCALE
    c[:, C_SEL:C_SEL + 2] = (s // 64) == np.arange(2)[None, :]
    a = np.zeros((P, CA_END), np.float32)
    pos = np.arange(T, dtype=np.float32)
    inv = (np.float32(10000.0) ** (-np.arange(0, HD, 2, dtype=np.float32) / np.float32(HD))).astype(np.float32)
    ang = (pos[None, :] * inv[:, None]).astype(np.float32)
    a[:, CA_COS:CA_COS + T] = np.concatenate([np.cos(ang), np.cos(ang)], 0)
    a[:, CA_SIN:CA_SIN + T] = np.concatenate([-np.sin(ang), np.sin(ang)], 0)
    j = np.arange(T)[None, :]
    for qb in range(2):
        q = np.arange(P)[:, None] + qb * P
        a[:, CA_MASK + qb * T:CA_MASK + (qb + 1) * T] = np.where(np.abs(j - q) <= 128, 0.0, -1e30)
    return c, a


def block_kernel(nc, I, cst_d, csa_d, out_d):
    f32, f32r, i32 = mybir.dt.float32, mybir.dt.float32r, mybir.dt.int32
    ACT, ALU, AX = mybir.ActivationFunctionType, mybir.AluOpType, mybir.AxisListType
    w_in, w_out, w_up, w_dn = I["w_in"][0], I["w_out"][0], I["w_ffn_up"][0], I["w_ffn_down"][0]

    ctx = ExitStack()
    with ctx:
        nbuf = [0]

        def sb(name, shape, dt=f32, stack=ctx):
            return stack.enter_context(nc.sbuf_tensor(name, shape, dt))

        def sig(name, per=1):
            return Sig(ctx.enter_context(nc.semaphore(name)), per)

        raw = sb("raw", [P, 4, 2048])
        whi = sb("whi", [P, 2, 2048], f32r)
        wlo = sb("wlo", [P, 2, 2048], f32r)
        xT = sb("xT", [P, KT, 2, T], f32r)
        cst = sb("cst", [P, C_END])
        pA = sb("pA", [P, 112])
        pB = sb("pB", [P, 112])
        small = sb("small", [P, 64])
        cells = sb("cells", [P, 8])
        epsh = sb("epsh", [P, 4])
        ident = cst[:, C_ID:C_ID + P]
        ones_mean, ones_half, hsel = cst[:, C_MEAN:C_MEAN + P], cst[:, C_HALF:C_HALF + P], cst[:, C_SEL:C_SEL + 2]
        PB = [ctx.enter_context(nc.psum_tensor(f"bank{b}", [P, 512], f32)) for b in range(8)]

        mixers = ExitStack()
        mrg = sb("mrg", [P, KT, T], stack=mixers)
        lact = sb("lact", [P, 4, T], stack=mixers)
        gact = sb("gact", [P, 2, T], stack=mixers)
        muL = sb("muL", [P, 6], stack=mixers)
        raw4 = sb("raw4", [P, 4, T + 2], stack=mixers)

        att = ExitStack()
        xtok = sb("xtok", [P, 2, D], stack=att)
        csa = sb("csa", [P, CA_END], stack=att)
        xf = sb("xf", [P, 2, T], stack=att)
        prow = sb("prow", [P, 3, P], stack=att)
        tokA = sb("tokA", [P, 2, T], stack=att)
        tokB = sb("tokB", [P, 2, T], stack=att)
        kr = sb("kr", [P, T], stack=att)
        qr = sb("qr", [P, 2, T], stack=att)
        vf = sb("vf", [P, T], stack=att)
        vtok = sb("vtok", [P, 2, HD], stack=att)
        scm = sb("scm", [P, 2, T], stack=att)
        prb = sb("prb", [P, 2, 2, T], stack=att)
        prT = sb("prT", [P, 2, T], stack=att)
        sinkb = sb("sinkb", [P, 16], stack=att)
        sm = sb("sm", [P, 16], stack=att)
        att.close()

        rw = ExitStack()
        G = [sb(f"G{d}", [P, 4, 4, P], stack=rw) for d in range(2)]
        CT = [sb(f"CT{d}", [P, 4, P], f32r, stack=rw) for d in range(2)]
        W = [sb(f"W{d}", [P, 4, P], f32r, stack=rw) for d in range(2)]
        Dm = [sb(f"Dm{d}", [P, 4, P], f32r, stack=rw) for d in range(2)]
        DT = [sb(f"DT{d}", [P, 4, P], f32r, stack=rw) for d in range(2)]
        sh = sb("sh", [P, 3, T], stack=rw)
        nb = sb("nb", [P, 3, T], stack=rw)
        gt = sb("gt", [P, T], stack=rw)
        gup = sb("gup", [P, T], stack=rw)
        upw = sb("upw", [P, 4, P], stack=rw)
        upg = sb("upg", [P, 2, P], stack=rw)
        AR = [sb(f"AR{d}", [P, 2, T], stack=rw) for d in range(2)]
        bh = [sb(f"bh{d}", [P, T], stack=rw) for d in range(2)]
        kh = [sb(f"kh{d}", [P, T], stack=rw) for d in range(2)]
        Pd = [sb(f"Pd{d}", [P, 2, P + 1], stack=rw) for d in range(2)]
        ta = [sb(f"ta{d}", [P, T], stack=rw) for d in range(2)]
        dec = [sb(f"dec{d}", [P, T], stack=rw) for d in range(2)]
        tw = dec
        km = [sb(f"km{d}", [P, T], stack=rw) for d in range(2)]
        kk = sb("kk", [P, T], stack=rw)
        sq = nb[:, 0, :]
        kA = sb("kA", [P, T], stack=rw)
        kB = sb("kB", [P, T], stack=rw)
        rk = sb("rk", [P, T], stack=rw)
        rep = sb("rep", [P, 2, P], stack=rw)
        Vt = sb("Vt", [P, 2, P], stack=rw)
        KB = sb("KB", [P, 4, P], stack=rw)
        rhs = sb("rhs", [P, 4, 64], f32r, stack=rw)
        U = sb("U", [P, 2, 4, 64], stack=rw)
        Sm = sb("Sm", [P, 2, P], stack=rw)
        zero = sb("zero", [P, P], stack=rw)
        der = sb("der", [P, 96], stack=rw)
        st = sb("st", [P, 8], stack=rw)
        ysb, yc, bon, ysq = tw[0], tw[1], kA, kB
        rw.close()
        mixers.close()

        ffn = ExitStack()
        hres = sb("hres", [P, 2, D], stack=ffn)
        acc = sb("acc", [P, 2, D], stack=ffn)
        gain = sb("gain", [P, D], stack=ffn)
        ft = sb("ft", [P, 8, 2, T], f32r, stack=ffn)
        fa = sb("fa", [P, 2, T], stack=ffn)
        fs = sb("fs", [P, 2, T], stack=ffn)
        junk = sb("junk", [P, 512], stack=ffn)
        hf = sb("hf", [P, 2, T], stack=ffn)
        ffn.close()

        raw_full = [sig(f"raw_full{s}") for s in range(4)]
        w_hi, w_lo, w_used, d_evac = sig("w_hi"), sig("w_lo"), sig("w_used"), sig("d_evac")
        s = {}
        for name, per in dict(
            ld_x=1, ld_c=1, ld_p=1, n_sq=8, n_st=2, n_pow=1, x_n=1, x_tp=1, x_gain=1, x_hi=1, x_lo=1, prm_ms=1,
            prm_tp=1, prm_ev=1, exp_ms=1,
            k_r1=1, k_r=1, v_tp=1, v_tok=1, q_r1=4, q_r=4, sc=4, sc_m=4, mx=4, mx2=4, neg=4,
            ex=4, esink=4, den=4, rden=4, prn=4, p_tp=4, p_T=4, pv=4, o_ev=4,
            ga_m=4, lo_nb=1, lo_df=1, lo_sh=1, lo_act=1, lo_fin=1, drv=1, zr=1,
            up_ld=1, sh_nb=1, sh_df=1, shifted=1, gate_t=1, kkr=1, sqd=1, ss=1, ssm=1, rs=1, rrep=1, rbc=1, nkk=1,
            kAB=1, rkd=1, lw=1, la=1, lg=1, tws=1, decs=2, tas=1, gups=1, scan=2, inv=2, ar=2, tt=2, bhs=2, km1=2, km2=2,
            khs=2, kbs=1, t2=1, vtp=1, vts=1, gram=8, gmask=8, e0=2, dt0=2, d0p=2, d0=2, ctm=12, wmm=12, wev=12,
            ddm=10, dtm=12, dup=10, dtup=12, kbtp=1, kbs2=1, rhsm=2, rhsc=2, um=2, ue=2, resm=2, rese=2, dum=2, due=2,
            smm=1, sme=1, ym=1, ye=1, mean=1, ycs=1, ysqs=1, var=1, vars=1, vpow=1, vrep=1, vbc=1, bonm=1, bonv=1,
            y1=1, y2=1, y3=1, y4=2, y5=1,
            mg_hi=1, mg_lo=1, om=1, o_cp=1, ld_h=1, ld_g=1, m_n=1, m_h=1,
            h_n=1, h_tp=1, h_g=1, h_hi=1, h_lo=1, up_re=8, up_sq=8, up_hi=8, up_lo=8, dn=4, dn_acc=4, f_n=1, f_o=1, ld_g2=1, done=1, acc0=1,
        ).items():
            s[name] = sig(name, per)

        U_ATT, U_GA, U_LO, U_RW = 0, 24, 40, 46
        U_OUT = U_RW + 4 * PAIRS
        U_FF = U_OUT + 16
        FCH = 8




        block = ctx.enter_context(nc.Block())

        @block.sync
        def _(sp):
            def load(u_static, u_count, src, n=P, style="B"):
                slot = u_static % 4
                if u_static >= 4:
                    sp.wait_ge(w_lo.sem, u_count - 3)
                if style == "B":
                    dst = raw[:, slot, :].rearrange("p (k c) -> p k c", k=KT)[:, :, 0:n]
                else:
                    dst = raw[:, slot, :].rearrange("p (k c) -> p k c", k=4)
                sp.dma_start(dst, src).then_inc(raw_full[slot].sem, 16)

            def cols(c, n=P):
                return w_in[:, bass.ds(c, n)].rearrange("(k p) c -> p k c", p=P)

            sp.dma_start(xtok[:], I["x"][0].rearrange("(b p) c -> p b c", p=P)).then_inc(s["ld_x"].sem, 16)
            sp.dma_start(cst[:], cst_d).then_inc(s["ld_c"].sem, 16)
            sp.dma_start(csa[:], csa_d).then_inc(s["ld_c"].sem, 16)
            row = 0
            sp.wait_ge(s["prm_ms"].sem, 1)
            mu = I["mu_shift"][0]
            n_prm = 0
            for slot, names in ((0, PARAMS_A), (1, PARAMS_B)):
                row = 0
                for name in names:
                    v = mu[0:3 * D] if name == "mu_shift" else I[name][0]
                    n = v.shape[0] // P
                    sp.dma_start(prow[row:row + n, slot, :], v.rearrange("(t c) -> t c", c=P)).then_inc(s["ld_p"].sem, 16)
                    n_prm += 1
                    row += n
            sp.dma_start(prow[0:4, 2, 0:DL], mu[3 * D:3 * D + 4 * DL].rearrange("(t c) -> t c", c=DL)).then_inc(s["ld_p"].sem, 16)
            sp.dma_start(prow[4:6, 2, :], mu[3 * D + 4 * DL:].rearrange("(t c) -> t c", c=P)).then_inc(s["ld_p"].sem, 16)
            sp.dma_start(sinkb[:], I["attn_sink"].partition_broadcast(P)[:, 0, :]).then_inc(s["ld_p"].sem, 16)
            with sp.Fori(0, KVH // 2, 1) as i:
                for gg in range(2):
                    for j in range(6):
                        u = 6 * gg + j
                        c = [K0 + P * gg + 2 * P * i, V0 + P * gg + 2 * P * i][j] if j < 2 else \
                            Q0 + P * (4 * gg + j - 2) + 8 * P * i
                        slot = u % 4
                        if u >= 4:
                            sp.wait_ge(w_lo.sem, 12 * i + u - 3)
                        else:
                            sp.wait_ge(w_lo.sem, 12 * i)
                        sp.dma_start(raw[:, slot, :].rearrange("p (k c) -> p k c", k=KT), cols(c)).then_inc(raw_full[slot].sem, 16)
            with sp.Fori(0, 4, 1) as i:
                for j in range(4):
                    load(U_GA + j, 4 * i + U_GA + j, cols(GA0 + P * j + 4 * P * i))
            lora = [(LO0 + DL * j, DL) for j in range(4)] + [(LO0 + 4 * DL + P * j, P) for j in range(2)]
            for j, (c, n) in enumerate(lora):
                load(U_LO + j, U_LO + j, w_in[:, c:c + n].rearrange("(k p) c -> p k c", p=P), n)

            def pair_units(i):
                for j, c0 in enumerate((RK0, R0, RV0, GR0)):
                    load(U_RW + j, 4 * i + U_RW + j, cols(c0 + P * i))

            def pair_ups(i):
                if not isinstance(i, int) or i > 0:
                    sp.wait_ge(s["lg"].sem, s["lg"].before(i))
                for j, name in enumerate(("w_up_fwd", "w_up_bwd", "a_up_fwd", "a_up_bwd")):
                    sp.dma_start(upw[0:DL, j, :], I[name][0][:, bass.ds(P * i, P)]).then_inc(s["up_ld"].sem, 16)
                sp.dma_start(upg[:], I["g_up"][0][:, bass.ds(P * i, P)].rearrange("(k p) c -> p k c", p=P)).then_inc(s["up_ld"].sem, 16)

            pair_units(0)
            sp.wait_ge(s["ga_m"].sem, 16)
            sp.wait_ge(s["o_ev"].sem, 16)
            with sp.Fori(0, PAIRS - 1, 1) as i:
                pair_ups(i)
                pair_units(i + 1)
            pair_ups(PAIRS - 1)

            def out_units(i, u0, wt, rows):
                for j in range(8):
                    nblk, kc = j // 4, j % 4
                    load(u0 + j, 8 * i + u0 + j, wt[kc * 512:(kc + 1) * 512, bass.ds(512 * nblk + 1024 * i, 512)]
                         .rearrange("(k p) c -> p k c", p=P), style="A")

            with sp.Fori(0, 2, 1) as i:
                out_units(i, U_OUT, w_out, D)
            sp.wait_ge(s["mg_lo"].sem, 16)
            sp.dma_start(hres[:], I["x"][0].rearrange("(b p) c -> p b c", p=P)).then_inc(s["ld_h"].sem, 16)
            sp.dma_start(gain[:], I["norm_post_mix"].partition_broadcast(P)[:, 0, :]).then_inc(s["ld_g"].sem, 16)

            with sp.Fori(0, FCH, 1) as i:
                for j in range(8):
                    load(U_FF + j, 16 * i + U_FF + j, w_up[:, bass.ds(P * j + 1024 * i, P)].rearrange("(k p) c -> p k c", p=P))
                for j in range(8):
                    nblk, kc = j // 2, j % 2
                    load(U_FF + 8 + j, 16 * i + U_FF + 8 + j,
                         w_dn[bass.ds(512 * kc + 1024 * i, 512), 512 * nblk:512 * nblk + 512].rearrange("(k p) c -> p k c", p=P), style="A")
            sp.wait_ge(s["m_h"].sem, 2)
            sp.dma_start(gain[:], I["norm_post_ffn"].partition_broadcast(P)[:, 0, :]).then_inc(s["ld_g2"].sem, 16)
            for b in range(2):
                sp.wait_ge(s["f_o"].sem, b + 1)
                sp.dma_start(out_d[0][b * P:(b + 1) * P, :], acc[:, b, :]).then_inc(s["done"].sem, 16)
            sp.wait_ge(s["done"].sem, 32)

        @block.scalar
        def _(act):
            A = nc.scalar

            def cut_hi(u_static, u):
                slot = u_static % 4
                full = 16 * (u_static // 4 + 1)
                step = u - u_static
                act.wait_ge(raw_full[slot].sem, full + step * 4)
                if u_static >= 2:
                    act.wait_ge(w_used.sem, u - 1)
                A.activation(whi[:, u_static % 2, :], raw[:, slot, :], ACT.Copy).then_inc(w_hi.sem, 1)

            act.wait_ge(s["ld_x"].sem, 16)
            for b in range(2):
                for q in range(4):
                    A.activation(tokB[:].rearrange("p a t -> p (a t)"), xtok[:, b, 512 * q:512 * q + 512], ACT.Square,
                                 accum_out=small[:, 4 * b + q:4 * b + q + 1]).then_inc(s["n_sq"].sem, 1)
                    act.wait_ge(s["n_sq"].sem, 4 * b + q + 1)
            for k in range(KT):
                act.wait_ge(s["x_gain"].sem, k + 1)
                A.activation(xT[:, k, 0, :], xf[:, k % 2, :], ACT.Copy).then_inc(s["x_hi"].sem, 1)

            cut_hi(0, 0)
            cut_hi(1, 1)
            with act.Fori(0, KVH // 2, 1) as i:
                for gg in range(2):
                    g = 2 * i + gg
                    for j in range(8):
                        u = 6 * gg + j
                        if j < 6:
                            act.wait_ge(w_used.sem, 12 * i + u + 1)
                            bank = PB[u % 2]
                            if j == 1:
                                act.wait_ge(s["v_tp"].sem, g)
                                A.activation(vf[:], bank[:, 0:T], ACT.Copy).then_inc(d_evac.sem, 1)
                            else:
                                done = s["k_r1"].before(g) if j == 0 else s["q_r1"].at(g, j - 2)
                                act.wait_ge(s["k_r1"].sem, s["k_r1"].before(g) if j == 0 else s["k_r1"].at(g))
                                act.wait_ge(s["q_r1"].sem, s["q_r1"].before(g) if j == 0 else s["q_r1"].at(g, j - 2))
                                A.activation(tokA[:, 0, :], bank[:, 0:T], ACT.Copy)
                                A.activation(tokA[0:64, 1, :], bank[64:P, 0:T], ACT.Copy)
                                A.activation(tokA[64:P, 1, :], bank[0:64, 0:T], ACT.Copy).then_inc(d_evac.sem, 1)
                            nu = u + 2
                            if gg == 0 or j < 4:
                                act.wait_ge(raw_full[nu % 4].sem, 48 * i + 16 * (nu // 4 + 1))
                                act.wait_ge(w_used.sem, 12 * i + nu - 1)
                                A.activation(whi[:, nu % 2, :], raw[:, nu % 4, :], ACT.Copy).then_inc(w_hi.sem, 1)
                            else:
                                act.wait_ge(raw_full[nu % 4].sem, 48 * i + 16 * (nu // 4 + 1))
                                act.wait_ge(w_used.sem, 12 * i + nu - 1)
                                A.activation(whi[:, nu % 2, :], raw[:, nu % 4, :], ACT.Copy).then_inc(w_hi.sem, 1)
                        if j == 1:
                            act.wait_ge(s["v_tp"].sem, s["v_tp"].at(g))
                            A.activation(vtok[:].rearrange("p a b -> p (a b)"), PB[2][:, 0:T], ACT.Copy).then_inc(s["v_tok"].sem, 1)
                        h = j - 3
                        if 0 <= h < 4:
                            n = s["neg"].at(g, h + 1)
                            act.wait_ge(s["neg"].sem, n)
                            act.wait_ge(s["p_tp"].sem, s["p_tp"].at(g, h - 1) if h >= 2 else s["p_tp"].before(g))
                            for qb in range(2):
                                x = A.activation(prb[:, h % 2, qb, :], scm[:, qb, :], ACT.Exp, bias=sm[:, 6 + qb:7 + qb],
                                                 scale=float(HD) ** -0.5, accum_out=sm[:, 8 + qb:9 + qb])
                            x.then_inc(s["ex"].sem, 1)
                            A.activation(sm[:, 10:12], sm[:, 4:6], ACT.Exp).then_inc(s["esink"].sem, 1)
                        h = j - 4
                        if 0 <= h < 4:
                            act.wait_ge(s["p_tp"].sem, s["p_tp"].at(g, h + 1))
                            A.activation(prT[:].rearrange("p a b -> p (a b)"), PB[5][:, :], ACT.Copy).then_inc(s["p_T"].sem, 1)
                            act.wait_ge(s["pv"].sem, s["pv"].at(g, h + 1))
                            A.activation(mrg[:, bass.ds(4 * gg + h + 8 * i, 1), :].rearrange("p a t -> p (a t)"), PB[6][:, 0:T],
                                         ACT.Copy).then_inc(s["o_ev"].sem, 1)
            with act.Fori(0, 4, 1) as i:
                for j in range(4):
                    u = U_GA + j
                    act.wait_ge(w_used.sem, 4 * i + u + 1)
                    act.wait_ge(s["ga_m"].sem, s["ga_m"].at(i, j))
                    A.activation(tokA[:, j % 2, :], PB[u % 2][:, 0:T], ACT.Tanh, scale=0.5).then_inc(d_evac.sem, 1)
                    cut_hi(u + 2, 4 * i + u + 2)
            for j in range(6):
                u = U_LO + j
                n = DL if j < 4 else P
                act.wait_ge(w_used.sem, u + 1)
                if j == 0:
                    act.wait_ge(s["zr"].sem, 2)
                else:
                    act.wait_ge(s["lo_sh"].sem, j)
                A.activation(raw4[0:n, 0, 1:T + 1], PB[u % 2][0:n, 0:T], ACT.Copy).then_inc(d_evac.sem, 1)
                cut_hi(u + 2, u + 2)
                act.wait_ge(s["lo_sh"].sem, j + 1)
                if j < 2:
                    A.activation(lact[0:n, j, :], lact[0:n, j, :], ACT.Tanh).then_inc(s["lo_act"].sem, 1)
                elif j >= 4:
                    A.activation(gact[:, j - 4, :], gact[:, j - 4, :], ACT.Tanh, scale=0.5).then_inc(s["lo_act"].sem, 1)

            def dense(j, i):
                u = U_RW + j
                act.wait_ge(w_used.sem, 4 * i + u + 1)
                if not (isinstance(i, int) and i == 0):
                    act.wait_ge(s["shifted"].sem, s["shifted"].before(i))
                    act.wait_ge(s["gate_t"].sem, s["gate_t"].before(i))
                slot = (1, 0, 2, 3)[j]
                A.activation(raw4[:, slot, 1:T + 1], PB[u % 2][:, 0:T], ACT.Copy).then_inc(d_evac.sem, 1)

            def cut_pair(j, i):
                cut_hi(U_RW + j + 2, 4 * i + U_RW + j + 2)

            def pair(i, nxt):
                def filler(j):
                    if nxt is not None:
                        dense(j, nxt)
                        if not (isinstance(nxt, int) and nxt == PAIRS - 1 and j >= 2):
                            cut_pair(j, nxt)

                w = lambda n, k=None: act.wait_ge(s[n].sem, s[n].at(i, k))
                act.wait_ge(s["y5"].sem, s["y5"].before(i))
                act.wait_ge(d_evac.sem, U_RW + 4 + 4 * i)
                A.activation(gt[:], raw4[:, 3, 1:T + 1], ACT.Tanh, scale=0.5).then_inc(s["gate_t"].sem, 1)
                w("lw")
                for d in range(2):
                    x = A.activation(tw[d][:], PB[2][:, T * d:T * d + T], ACT.Tanh, scale=0.5,
                                     bias=der[:, bass.ds(16 * d + i, 1)])
                x.then_inc(s["tws"].sem, 1)
                w("tws")
                for d in range(2):
                    A.activation(dec[d][:], tw[d][:], ACT.Exp, scale=-0.5 * DECAY_E, bias=-0.5 * DECAY_E).then_inc(s["decs"].sem, 1)
                w("la")
                for d in range(2):
                    x = A.activation(ta[d][:], PB[3][:, T * d:T * d + T], ACT.Tanh, scale=0.5,
                                     bias=der[:, bass.ds(32 + 16 * d + i, 1)])
                x.then_inc(s["tas"].sem, 1)
                w("lg")
                A.activation(gup[:], PB[4][:, 0:T], ACT.Copy).then_inc(s["gups"].sem, 1)
                w("vtp")
                A.activation(Vt[:].rearrange("p a b -> p (a b)"), PB[5][:, 0:T], ACT.Copy).then_inc(s["vts"].sem, 1)
                filler(0)
                for l in range(1, LV):
                    for d in range(2):
                        n = 2 * (l - 1) + d + 1
                        w("wmm", n)
                        A.activation(W[d][:].rearrange("p a b -> p (a b)"), PB[4 - d][:, :], ACT.Copy).then_inc(s["wev"].sem, 1)
                    if l in (1, 3, 5):
                        filler((l + 1) // 2)
                w("kbtp")
                A.activation(KB[:].rearrange("p a b -> p (a b)"), PB[3][:, :], ACT.Copy).then_inc(s["kbs2"].sem, 1)
                for c in range(2):
                    w("rhsm", c + 1)
                    A.activation(rhs[:].rearrange("p a b -> p (a b)"), PB[4][:, 0:T], ACT.Copy).then_inc(s["rhsc"].sem, 1)
                    w("um", c + 1)
                    A.activation(U[:, c, :, :].rearrange("p a b -> p (a b)"), PB[5][:, 0:T], ACT.Copy).then_inc(s["ue"].sem, 1)
                w("ym")
                A.activation(ysb[:], PB[2][:, 0:T], ACT.Copy).then_inc(s["ye"].sem, 1)
                w("ycs")
                A.activation(ysq[:], yc[:], ACT.Square).then_inc(s["ysqs"].sem, 1)

            for j in range(4):
                dense(j, 0)
                cut_pair(j, 0)
            with act.Fori(0, PAIRS - 2, 1) as i:
                pair(i, i + 1)
            pair(PAIRS - 2, PAIRS - 1)
            pair(PAIRS - 1, None)

            act.wait_ge(w_used.sem, U_OUT)
            act.wait_ge(s["y5"].sem, 16)
            for k in range(KT):
                A.activation(xT[:, k, 0, :], mrg[:, k, :], ACT.Copy).then_inc(s["mg_hi"].sem, 1)
            cut_hi(U_OUT, U_OUT)
            cut_hi(U_OUT + 1, U_OUT + 1)
            with act.Fori(0, 2, 1) as i:
                for j in range(8):
                    cut_hi(U_OUT + j + 2, 8 * i + U_OUT + j + 2)
                    if j % 4 == 3:
                        n = j // 4
                        act.wait_ge(s["om"].sem, 2 * i + n + 1)
                        act.wait_ge(s["mg_lo"].sem, 16)
                        for b in range(2):
                            x = A.activation(acc[:, b, bass.ds(512 * n + 1024 * i, 512)], PB[2 * n + b][:, :], ACT.Copy)
                        x.then_inc(s["o_cp"].sem, 1)

            def sumsq(src, norm, col):
                for b in range(2):
                    for q in range(4):
                        A.activation(junk[:], src[:, b, 512 * q:512 * q + 512], ACT.Square,
                                     accum_out=small[:, col + 4 * b + q:col + 4 * b + q + 1]).then_inc(s["n_sq"].sem, 1)
                        act.wait_ge(s["n_sq"].sem, s["n_sq"].at(norm, 4 * b + q + 1))

            act.wait_ge(s["o_cp"].sem, 4)
            sumsq(acc, 1, 16)
            act.wait_ge(s["m_h"].sem, 2)
            sumsq(hres, 2, 32)
            for k in range(KT):
                act.wait_ge(s["h_g"].sem, k + 1)
                if k == 0:
                    act.wait_ge(w_used.sem, U_FF)
                A.activation(xT[:, k, 0, :], hf[:, k % 2, :], ACT.Copy).then_inc(s["h_hi"].sem, 1)
            def chunk(i, last):
                for j in range(16):
                    u = U_FF + j
                    if j < 8:
                        act.wait_ge(w_used.sem, 16 * i + u + 1)
                        act.wait_ge(s["up_sq"].sem, s["up_sq"].at(i, j - 1) if j else s["up_sq"].before(i))
                        A.activation(fa[:, j % 2, :], PB[u % 2][:, 0:T], ACT.Relu).then_inc(s["up_re"].sem, 1)
                    if not (last and j >= 14):
                        cut_hi(u + 2, 16 * i + u + 2)
                    if j < 8:
                        act.wait_ge(s["up_sq"].sem, s["up_sq"].at(i, j + 1))
                        if j == 0:
                            act.wait_ge(s["dn"].sem, s["dn"].before(i))
                        A.activation(ft[:, j, 0, :], fs[:, j % 2, :], ACT.Copy).then_inc(s["up_hi"].sem, 1)

            with act.Fori(0, FCH - 1, 1) as i:
                chunk(i, False)
            chunk(FCH - 1, True)
            act.wait_ge(s["dn_acc"].sem, 4 * FCH)
            sumsq(acc, 3, 48)

        @block.vector
        def _(dve):
            V = nc.vector

            def cut_lo(u_static, u):
                dve.wait_ge(w_hi.sem, u + 1)
                V.tensor_tensor(wlo[:, u_static % 2, :], raw[:, u_static % 4, :], whi[:, u_static % 2, :].bitcast(f32),
                                ALU.subtract).then_inc(w_lo.sem, 1)

            def rstd(col, norm, eps=EPS):
                dve.wait_ge(s["n_sq"].sem, s["n_sq"].at(norm))
                V.tensor_reduce(small[:, col + 8:col + 10], small[:, col:col + 8].rearrange("p (b q) -> p b q", b=2), AX.X, ALU.add)\
                    .then_inc(s["n_st"].sem, 1)
                dve.wait_ge(s["n_st"].sem, s["n_st"].at(norm, 1))
                V.tensor_scalar(small[:, col + 10:col + 12], small[:, col + 8:col + 10], 1.0 / D, eps, ALU.mult, ALU.add)\
                    .then_inc(s["n_st"].sem, 1)
                dve.wait_ge(s["n_pow"].sem, s["n_pow"].at(norm))

            V.memset(prow[:], 0.0).then_inc(s["prm_ms"].sem, 1)
            V.memset(epsh[:], -0.5).then_inc(s["exp_ms"].sem, 1)
            rstd(0, 0)
            for b in range(2):
                V.tensor_scalar(xtok[:, b, :], xtok[:, b, :], small[:, 12 + b:13 + b], None, ALU.mult).then_inc(s["x_n"].sem, 1)
            dve.wait_ge(s["prm_tp"].sem, 3)
            V.tensor_copy(pA[:], PB[7][:, 0:112]).then_inc(s["prm_ev"].sem, 1)
            V.tensor_copy(pB[:], PB[7][:, 128:240]).then_inc(s["prm_ev"].sem, 1)
            V.tensor_copy(muL[:], PB[7][:, 256:262]).then_inc(s["prm_ev"].sem, 1)
            dve.wait_ge(s["prm_ev"].sem, 3)
            for k in range(KT):
                dve.wait_ge(s["x_tp"].sem, k // 2 + 1)
                if k >= 2:
                    dve.wait_ge(s["x_lo"].sem, k - 1)
                V.tensor_scalar(xf[:, k % 2, :], PB[(k // 2) % 2][:, T * (k % 2):T * (k % 2) + T], pB[:, 80 + k:81 + k], None,
                                ALU.mult).then_inc(s["x_gain"].sem, 1)
                dve.wait_ge(s["x_hi"].sem, k + 1)
                V.tensor_tensor(xT[:, k, 1, :], xf[:, k % 2, :], xT[:, k, 0, :].bitcast(f32), ALU.subtract).then_inc(s["x_lo"].sem, 1)

            cut_lo(0, 0)
            cut_lo(1, 1)
            cos, sin = csa[:, CA_COS:CA_COS + T], csa[:, CA_SIN:CA_SIN + T]
            wmask = csa[:, CA_MASK:CA_MASK + 2 * T]
            with dve.Fori(0, KVH // 2, 1) as i:
                for gg in range(2):
                    g = 2 * i + gg
                    for j in range(8):
                        u = 6 * gg + j
                        if j < 6:
                            dve.wait_ge(d_evac.sem, 12 * i + u + 1)
                            if j != 1:
                                r1, r2 = (s["k_r1"], s["k_r"]) if j == 0 else (s["q_r1"], s["q_r"])
                                m = 1 if j == 0 else j - 1
                                dst = kr[:] if j == 0 else qr[:, j % 2, :]
                                if j == 0:
                                    dve.wait_ge(s["q_r"].sem, s["q_r"].before(g))
                                else:
                                    dve.wait_ge(s["k_r"].sem, s["k_r"].at(g))
                                    dve.wait_ge(s["q_r"].sem, s["q_r"].at(g, j - 2))
                                V.tensor_tensor(tokB[:, 0, :], tokA[:, 0, :], cos, ALU.mult)
                                V.tensor_tensor(tokB[:, 1, :], tokA[:, 1, :], sin, ALU.mult).then_inc(r1.sem, 1)
                                dve.wait_ge(r1.sem, r1.at(g, m))
                                if j == 0:
                                    dve.wait_ge(s["sc"].sem, s["sc"].before(g))
                                elif j >= 4:
                                    dve.wait_ge(s["sc"].sem, s["sc"].at(g, j - 3))
                                V.tensor_tensor(dst, tokB[:, 0, :], tokB[:, 1, :], ALU.add).then_inc(r2.sem, 1)
                            cut_lo(u + 2, 12 * i + u + 2)
                        h = j - 3
                        if 0 <= h < 4:
                            dve.wait_ge(s["sc"].sem, s["sc"].at(g, h + 1))
                            dve.wait_ge(s["esink"].sem, s["esink"].at(g, h) if h else s["esink"].before(g))
                            V.tensor_tensor(scm[:].rearrange("p a b -> p (a b)"), PB[3 + h % 2][:, :], wmask, ALU.add).then_inc(s["sc_m"].sem, 1)
                            dve.wait_ge(s["sc_m"].sem, s["sc_m"].at(g, h + 1))
                            V.tensor_reduce(sm[:, 0:2], scm[:], AX.X, ALU.max).then_inc(s["mx"].sem, 1)
                            dve.wait_ge(s["mx"].sem, s["mx"].at(g, h + 1))
                            sink = sinkb[:, bass.ds(4 * gg + h + 8 * i, 1)]
                            V.tensor_scalar(sm[:, 2:4], sm[:, 0:2], float(HD) ** -0.5, sink, ALU.mult, ALU.max).then_inc(s["mx2"].sem, 1)
                            dve.wait_ge(s["mx2"].sem, s["mx2"].at(g, h + 1))
                            V.tensor_scalar(sm[:, 6:8], sm[:, 2:4], -1.0, None, ALU.mult)
                            V.tensor_scalar(sm[:, 4:6], sm[:, 2:4], -1.0, sink, ALU.mult, ALU.add).then_inc(s["neg"].sem, 1)
                            dve.wait_ge(s["ex"].sem, s["ex"].at(g, h + 1))
                            dve.wait_ge(s["esink"].sem, s["esink"].at(g, h + 1))
                            V.tensor_tensor(sm[:, 12:14], sm[:, 8:10], sm[:, 10:12], ALU.add).then_inc(s["den"].sem, 1)
                            dve.wait_ge(s["den"].sem, s["den"].at(g, h + 1))
                            V.reciprocal(sm[:, 14:16], sm[:, 12:14]).then_inc(s["rden"].sem, 1)
                            dve.wait_ge(s["rden"].sem, s["rden"].at(g, h + 1))
                            for qb in range(2):
                                x = V.tensor_scalar(prb[:, h % 2, qb, :], prb[:, h % 2, qb, :], sm[:, 14 + qb:15 + qb], None, ALU.mult)
                            x.then_inc(s["prn"].sem, 1)
            with dve.Fori(0, 4, 1) as i:
                for j in range(4):
                    u = U_GA + j
                    dve.wait_ge(d_evac.sem, 4 * i + u + 1)
                    dve.wait_ge(s["o_ev"].sem, 16)
                    m = mrg[:, bass.ds(j + 4 * i, 1), :].rearrange("p a t -> p (a t)")
                    V.scalar_tensor_tensor(m, tokA[:, j % 2, :], 1.0, m, ALU.add, ALU.mult).then_inc(s["ga_m"].sem, 1)
                    cut_lo(u + 2, 4 * i + u + 2)
            dve.wait_ge(s["ga_m"].sem, 16)
            V.memset(raw4[:], 0.0).then_inc(s["zr"].sem, 1)
            V.memset(lact[:], 0.0).then_inc(s["zr"].sem, 1)
            for d in range(2):
                V.memset(G[d][:], 0.0).then_inc(s["zr"].sem, 1)
            V.memset(zero[:], 0.0).then_inc(s["zr"].sem, 1)
            V.memset(Pd[0][:, :, 0:1], P0SCALE).then_inc(s["zr"].sem, 1)
            V.memset(Pd[1][:, :, P:P + 1], P0SCALE).then_inc(s["zr"].sem, 1)
            V.tensor_scalar(der[:, 0:64], pA[:, 48:112], 0.5, None, ALU.mult).then_inc(s["drv"].sem, 1)
            V.tensor_scalar(der[:, 64:80], pB[:, 16:32], 0.5, None, ALU.mult).then_inc(s["drv"].sem, 1)
            V.tensor_scalar(der[:, 80:96], pB[:, 16:32], -0.5, 1.0, ALU.mult, ALU.add).then_inc(s["drv"].sem, 1)
            dve.wait_ge(s["zr"].sem, 7)
            dve.wait_ge(s["drv"].sem, 3)
            for j in range(6):
                u = U_LO + j
                n = DL if j < 4 else P
                dst = lact[0:n, j, :] if j < 4 else gact[:, j - 4, :]
                dve.wait_ge(d_evac.sem, u + 1)
                V.tensor_tensor(nb[0:n, 0, :], raw4[0:n, 0, 0:T], raw4[0:n, 0, 2:T + 2], ALU.add).then_inc(s["lo_nb"].sem, 1)
                dve.wait_ge(s["lo_nb"].sem, j + 1)
                V.scalar_tensor_tensor(nb[0:n, 1, :], nb[0:n, 0, :], 0.5, raw4[0:n, 0, 1:T + 1], ALU.mult, ALU.subtract).then_inc(s["lo_df"].sem, 1)
                dve.wait_ge(s["lo_df"].sem, j + 1)
                V.scalar_tensor_tensor(dst, nb[0:n, 1, :], muL[0:n, j:j + 1], raw4[0:n, 0, 1:T + 1], ALU.mult, ALU.add).then_inc(s["lo_sh"].sem, 1)
                cut_lo(u + 2, u + 2)
            dve.wait_ge(s["lo_act"].sem, 4)
            V.tensor_scalar(gact[:], gact[:], 0.5, 0.5, ALU.mult, ALU.add).then_inc(s["lo_fin"].sem, 1)

            def cut_pair(j, i):
                cut_lo(U_RW + j + 2, 4 * i + U_RW + j + 2)

            def pair(i, nxt):
                def filler(j):
                    if nxt is not None and not (isinstance(nxt, int) and nxt == PAIRS - 1 and j >= 2):
                        cut_pair(j, nxt)

                w = lambda n, k=None: dve.wait_ge(s[n].sem, s[n].at(i, k))
                inc = lambda x, n: x.then_inc(s[n].sem, 1)
                col = lambda t, c: t[:, bass.ds(c + i, 1)]
                dve.wait_ge(d_evac.sem, U_RW + 4 + 4 * i)
                inc(V.tensor_tensor(nb[:], raw4[:, 0:3, 0:T], raw4[:, 0:3, 2:T + 2], ALU.add), "sh_nb")
                w("sh_nb")
                inc(V.scalar_tensor_tensor(nb[:], nb[:], 0.5, raw4[:, 0:3, 1:T + 1], ALU.mult, ALU.subtract), "sh_df")
                w("sh_df")
                for c in (1, 0, 2):
                    x = V.scalar_tensor_tensor(sh[:, c, :], nb[:, c, :], col(pA, 16 * c), raw4[:, c, 1:T + 1], ALU.mult, ALU.add)
                inc(x, "shifted")
                w("shifted")
                r, k, v = sh[:, 0, :], sh[:, 1, :], sh[:, 2, :]
                inc(V.tensor_scalar(kk[:], k, col(pB, 0), None, ALU.mult), "kkr")
                w("kkr")
                inc(V.tensor_tensor(sq, kk[:], kk[:], ALU.mult), "sqd")
                V.tensor_scalar(kA[:], k, col(der, 64), None, ALU.mult)
                inc(V.tensor_scalar(kB[:], k, col(der, 80), None, ALU.mult), "kAB")
                inc(V.tensor_scalar(rk[:], r, col(pB, 32), None, ALU.mult), "rkd")
                w("ss")
                inc(V.tensor_scalar(st[:, 0:4], PB[7][:, 0:4], 1e-24, None, ALU.max), "ssm")
                w("rs")
                for tb in range(2):
                    x = V.tensor_copy(rep[:, tb, :].rearrange("p (h f) -> p h f", h=2),
                                      st[:, 4 + 2 * tb:6 + 2 * tb].unsqueeze(2).to_broadcast([P, 2, 64]))
                inc(x, "rrep")
                for d in range(2):
                    w("decs", d + 1)
                    for tb in range(2):
                        src = dec[d][:, P * tb:P * tb + P]
                        if d == 0:
                            x = V.tensor_tensor_scan(Pd[0][:, tb, 1:P + 1], src, zero[:], P0SCALE, ALU.mult, ALU.add)
                        else:
                            x = V.tensor_tensor_scan(Pd[1][:, tb, 0:P][:, ::-1], src[:, ::-1], zero[:], P0SCALE, ALU.mult, ALU.add)
                    inc(x, "scan")
                w("rbc")
                inc(V.scalar_tensor_tensor(kk[:], kk[:], -1.0, PB[7][:, 0:T], ALU.mult, ALU.mult), "nkk")
                w("nkk")
                w("tas")
                w("kAB")
                blocks = lambda t: t.rearrange("p (a b) -> p a b", a=2)
                for d in range(2):
                    incl = Pd[d][:, :, 1:P + 1] if d == 0 else Pd[d][:, :, 0:P]
                    excl = Pd[d][:, :, 0:P] if d == 0 else Pd[d][:, :, 1:P + 1]
                    w("scan", d + 1)
                    inc(V.reciprocal(blocks(dec[d][:]), incl), "inv")
                    V.tensor_tensor(blocks(AR[d][:, 0, :]), blocks(kk[:]), excl, ALU.mult)
                    inc(V.tensor_tensor(blocks(AR[d][:, 1, :]), blocks(r), incl, ALU.mult), "ar")
                    inc(V.tensor_tensor(km[d][:], kA[:], ta[d][:], ALU.mult), "km1")
                    inc(V.scalar_tensor_tensor(ta[d][:], ta[d][:], 1.0, kk[:], ALU.add, ALU.mult), "tt")
                    w("km1", d + 1)
                    inc(V.tensor_tensor(km[d][:], km[d][:], kB[:], ALU.add), "km2")
                    w("tt", d + 1)
                    w("inv", d + 1)
                    inc(V.scalar_tensor_tensor(bh[d][:], ta[d][:], -0.5, dec[d][:], ALU.mult, ALU.mult), "bhs")
                    w("km2", d + 1)
                    inc(V.tensor_tensor(kh[d][:], km[d][:], dec[d][:], ALU.mult), "khs")
                filler(0)
                for d in range(2):
                    for q in range(4):
                        n = 4 * d + q + 1
                        w("gram", n)
                        V.memset(cells[0:1, n - 1:n], 0.0)
                        mask = cst[:, C_GM + 256 * d:C_GM + 256 * d + 256].bitcast(i32).unsqueeze(1).to_broadcast([P, 2, 256])
                        inc(V.copy_predicated(G[d][:, q, :, :].rearrange("p (a b) c -> p a (b c)", a=2), mask,
                                              PB[2 + q % 2][:, :].rearrange("p (a b) -> p a b", a=2)), "gmask")
                    w("d0p", d + 1) if d == 0 and False else None
                for d in range(2):
                    w("d0p", d + 1)
                    inc(V.tensor_copy(Dm[d][:].rearrange("p a b -> p (a b)"), PB[5 + d][:, :]), "d0")
                for l in range(1, LV):
                    m = 1 << l
                    part = lambda t, par: t[:].rearrange("p g (n two m) -> p (g n) two m", two=2, m=m)[:, :, par, :]
                    small_ = lambda bank: bank[:, 0:T].rearrange("p (n m) -> p n m", m=m)
                    for d in range(2):
                        n = 2 * (l - 1) + d + 1
                        if l < LV - 1:
                            w("ddm", n)
                            inc(V.tensor_tensor(part(Dm[d], d), part(Dm[d], d).bitcast(f32), small_(PB[5 if d == 0 else 2]), ALU.add), "dup")
                        w("dtm", n)
                        inc(V.tensor_tensor(part(DT[d], 1 - d), part(DT[d], 1 - d).bitcast(f32), small_(PB[6 if d == 0 else 7]), ALU.add), "dtup")
                    if l in (1, 3, 5):
                        filler((l + 1) // 2)
                for c in range(2):
                    w("ue", c + 1)
                    w("resm", c + 1)
                    inc(V.tensor_tensor(rhs[:].rearrange("p a b -> p (a b)"), PB[4][:, 0:T],
                                        U[:, c, :, :].rearrange("p a b -> p (a b)"), ALU.subtract), "rese")
                    w("dum", c + 1)
                    u2 = U[:, c, :, :].rearrange("p a b -> p (a b)")
                    inc(V.tensor_tensor(u2, PB[5][:, T:2 * T], u2, ALU.add), "due")
                    if c == 0:
                        w("smm")
                        for d in range(2):
                            last = Pd[0][:, 0, P:P + 1] if d == 0 else Pd[1][:, 1, 0:1]
                            x = V.scalar_tensor_tensor(Sm[:, d, :], PB[6][:, P * d:P * d + P], last, cst[:, C_SM:C_SM + P], ALU.mult, ALU.mult)
                        inc(x, "sme")
                w("bonm")
                inc(V.tensor_tensor(bon[:], PB[6][:, 0:T], v, ALU.mult), "bonv")
                w("ye")
                w("mean")
                inc(V.tensor_tensor(yc[:], ysb[:], PB[7][:, 0:T], ALU.subtract), "ycs")
                w("var")
                inc(V.tensor_scalar(st[:, 0:4], PB[7][:, 0:4], 1.0 / 64, GN_EPS, ALU.mult, ALU.add), "vars")
                w("vpow")
                for tb in range(2):
                    x = V.tensor_copy(rep[:, tb, :].rearrange("p (h f) -> p h f", h=2),
                                      st[:, 4 + 2 * tb:6 + 2 * tb].unsqueeze(2).to_broadcast([P, 2, 64]))
                inc(x, "vrep")
                w("vbc")
                inc(V.tensor_tensor(yc[:], yc[:], PB[7][:, 0:T], ALU.mult), "y1")
                w("y1")
                inc(V.tensor_scalar(yc[:], yc[:], col(pB, 48), col(pB, 64), ALU.mult, ALU.add), "y2")
                w("y2")
                w("bonv")
                inc(V.tensor_tensor(yc[:], yc[:], bon[:], ALU.add), "y3")
                w("y3")
                inc(V.tensor_tensor(yc[:], yc[:], gup[:], ALU.mult), "y4")
                w("y4", 1)
                m = mrg[:, bass.ds(i, 1), :].rearrange("p a t -> p (a t)") if not isinstance(i, int) else mrg[:, i, :]
                inc(V.scalar_tensor_tensor(ysb[:], gt[:], 1.0, yc[:], ALU.add, ALU.mult), "y4")
                w("y4", 2)
                inc(V.tensor_tensor(m, m, ysb[:], ALU.add), "y5")

            for j in range(4):
                cut_pair(j, 0)
            with dve.Fori(0, PAIRS - 2, 1) as i:
                pair(i, i + 1)
            pair(PAIRS - 2, PAIRS - 1)
            pair(PAIRS - 1, None)

            dve.wait_ge(s["y5"].sem, 16)
            for k in range(KT):
                dve.wait_ge(s["mg_hi"].sem, k + 1)
                V.tensor_tensor(xT[:, k, 1, :], mrg[:, k, :], xT[:, k, 0, :].bitcast(f32), ALU.subtract).then_inc(s["mg_lo"].sem, 1)
            cut_lo(U_OUT, U_OUT)
            cut_lo(U_OUT + 1, U_OUT + 1)
            with dve.Fori(0, 2, 1) as i:
                for j in range(8):
                    cut_lo(U_OUT + j + 2, 8 * i + U_OUT + j + 2)

            rstd(16, 1, 4 * EPS)
            dve.wait_ge(s["ld_h"].sem, 16)
            dve.wait_ge(s["ld_g"].sem, 16)
            for b in range(2):
                V.scalar_tensor_tensor(acc[:, b, :], acc[:, b, :], small[:, 28 + b:29 + b], gain[:], ALU.mult, ALU.mult).then_inc(s["m_n"].sem, 1)
                dve.wait_ge(s["m_n"].sem, b + 1)
                V.tensor_tensor(hres[:, b, :], hres[:, b, :], acc[:, b, :], ALU.add).then_inc(s["m_h"].sem, 1)
            rstd(32, 2)
            for b in range(2):
                V.tensor_scalar(acc[:, b, :], hres[:, b, :], small[:, 44 + b:45 + b], None, ALU.mult).then_inc(s["h_n"].sem, 1)
            for k in range(KT):
                dve.wait_ge(s["h_tp"].sem, k // 2 + 1)
                if k >= 2:
                    dve.wait_ge(s["h_lo"].sem, k - 1)
                V.tensor_scalar(hf[:, k % 2, :], PB[4 + (k // 2) % 2][:, T * (k % 2):T * (k % 2) + T], pB[:, 96 + k:97 + k], None,
                                ALU.mult).then_inc(s["h_g"].sem, 1)
                dve.wait_ge(s["h_hi"].sem, k + 1)
                V.tensor_tensor(xT[:, k, 1, :], hf[:, k % 2, :], xT[:, k, 0, :].bitcast(f32), ALU.subtract).then_inc(s["h_lo"].sem, 1)
            dve.wait_ge(s["h_tp"].sem, 8)
            V.memset(acc[:], 0.0).then_inc(s["acc0"].sem, 1)
            dve.wait_ge(s["acc0"].sem, 1)

            def chunk(i, last):
                for j in range(16):
                    u = U_FF + j
                    if not (last and j >= 14):
                        cut_lo(u + 2, 16 * i + u + 2)
                    if j < 8:
                        dve.wait_ge(s["up_re"].sem, s["up_re"].at(i, j + 1))
                        V.tensor_tensor(fs[:, j % 2, :], fa[:, j % 2, :], fa[:, j % 2, :], ALU.mult).then_inc(s["up_sq"].sem, 1)
                        dve.wait_ge(s["up_sq"].sem, s["up_sq"].at(i, j + 1))
                        dve.wait_ge(s["up_hi"].sem, s["up_hi"].at(i, j + 1))
                        V.tensor_tensor(ft[:, j, 1, :], fs[:, j % 2, :], ft[:, j, 0, :].bitcast(f32), ALU.subtract).then_inc(s["up_lo"].sem, 1)
                    elif j % 2 == 1:
                        n = (j - 9) // 2
                        dve.wait_ge(s["dn"].sem, s["dn"].at(i, n + 1))
                        for b in range(2):
                            x = V.tensor_tensor(acc[:, b, 512 * n:512 * n + 512], acc[:, b, 512 * n:512 * n + 512], PB[2 + 2 * (n % 3) + b][:, :], ALU.add)
                        x.then_inc(s["dn_acc"].sem, 1)

            with dve.Fori(0, FCH - 1, 1) as i:
                chunk(i, False)
            chunk(FCH - 1, True)
            rstd(48, 3)
            dve.wait_ge(s["ld_g2"].sem, 16)
            for b in range(2):
                V.scalar_tensor_tensor(acc[:, b, :], acc[:, b, :], small[:, 60 + b:61 + b], gain[:], ALU.mult, ALU.mult).then_inc(s["f_n"].sem, 1)
                dve.wait_ge(s["f_n"].sem, b + 1)
                V.tensor_tensor(acc[:, b, :], hres[:, b, :], acc[:, b, :], ALU.add).then_inc(s["f_o"].sem, 1)

        @block.gpsimd
        def _(pool):
            Gp = nc.gpsimd

            def power(norm, col):
                pool.wait_ge(s["n_st"].sem, s["n_st"].at(norm))
                Gp.tensor_tensor(small[:, col + 12:col + 14], small[:, col + 10:col + 12], epsh[:, 0:2], ALU.pow).then_inc(s["n_pow"].sem, 1)

            pool.wait_ge(s["exp_ms"].sem, 1)
            power(0, 0)
            pool.wait_ge(s["ld_c"].sem, 32)

            def pair(i):
                w = lambda n, k=None: pool.wait_ge(s[n].sem, s[n].at(i, k))
                lm = lambda d, l: cst[:, C_LM + (LV * d + l) * P:C_LM + (LV * d + l + 1) * P].unsqueeze(1).to_broadcast([P, 4, P])
                w("ssm")
                Gp.tensor_tensor(st[:, 4:8], st[:, 0:4], epsh[:, 0:4], ALU.pow).then_inc(s["rs"].sem, 1)
                w("km2", 2)
                w("khs", 2)
                Gp.tensor_tensor(km[0][:], km[0][:], km[1][:], ALU.add).then_inc(s["kbs"].sem, 1)
                w("kbs")
                w("rkd")
                Gp.tensor_tensor(rk[:], rk[:], km[0][:], ALU.mult).then_inc(s["t2"].sem, 1)
                for d in range(2):
                    w("gmask", 4 * d + 4)
                    pool.wait_ge(s["dum"].sem, s["dum"].before(i))
                    Gp.tensor_tensor(DT[d][:], G[d][:, :, 0, :], lm(d, 0), ALU.mult).then_inc(s["e0"].sem, 1)
                    w("e0", d + 1)
                    Gp.tensor_tensor(DT[d][:], DT[d][:].bitcast(f32), ident.unsqueeze(1).to_broadcast([P, 4, P]), ALU.add).then_inc(s["dt0"].sem, 1)
                for l in range(1, LV):
                    for d in range(2):
                        if l > 1:
                            w("wmm", 2 * (l - 2) + d + 1)
                        Gp.tensor_tensor(CT[d][:], G[d][:, :, 0, :], lm(d, l), ALU.mult).then_inc(s["ctm"].sem, 1)
                w("vars")
                Gp.tensor_tensor(st[:, 4:8], st[:, 0:4], epsh[:, 0:4], ALU.pow).then_inc(s["vpow"].sem, 1)

            with pool.Fori(0, PAIRS, 1) as i:
                pair(i)
            for norm in (1, 2, 3):
                power(norm, 16 * norm)

        @block.tensor
        def _(pe):
            M = nc.tensor.matmul

            def unit_b(u_static, u, e=None):
                pe.wait_ge(w_lo.sem, u + 1)
                bank = PB[u_static % 2]
                hi, lo = whi[:, u_static % 2, :], wlo[:, u_static % 2, :]
                for k in range(KT):
                    h, l = hi[:, P * k:P * k + P], lo[:, P * k:P * k + P]
                    M(bank[:, 0:T], h, xT[:, k, 0, :], start=k == 0, stop=False)
                    M(bank[:, 0:T], h, xT[:, k, 1, :], start=False, stop=False)
                    x = M(bank[:, 0:T], l, xT[:, k, 0, :], start=False, stop=k == KT - 1)
                x.then_inc(w_used.sem, 1)

            def unit_a(u_static, u, act_tiles, banks, first, last, done=None):
                pe.wait_ge(w_lo.sem, u + 1)
                hi, lo = whi[:, u_static % 2, :], wlo[:, u_static % 2, :]
                for k in range(4):
                    t = act_tiles[k]
                    for b in range(2):
                        ah, al = t[:, 0, P * b:P * b + P], t[:, 1, P * b:P * b + P]
                        wh, wl = hi[:, 512 * k:512 * k + 512], lo[:, 512 * k:512 * k + 512]
                        f, e = first and k == 0, last and k == 3
                        M(banks[b][:, :], ah, wh, start=f, stop=False)
                        M(banks[b][:, :], ah, wl, start=False, stop=False)
                        x = M(banks[b][:, :], al, wh, start=False, stop=e)
                x.then_inc(w_used.sem, 1)
                return x

            pe.wait_ge(s["ld_c"].sem, 32)
            pe.wait_ge(s["ld_p"].sem, 16 * (len(PARAMS_A) + len(PARAMS_B) + 3))
            for q in range(3):
                nc.tensor.transpose(PB[7][:, P * q:P * q + P], prow[:, q, :], ident).then_inc(s["prm_tp"].sem, 1)

            def token_tiles(src, banks, ready, free, done):
                for k2 in range(KT // 2):
                    if k2 == 0:
                        pe.wait_ge(s[ready].sem, 2)
                    if k2 >= 2:
                        pe.wait_ge(s[free].sem, 2 * (k2 - 1))
                    for kk_ in range(2):
                        for b in range(2):
                            k = 2 * k2 + kk_
                            x = nc.tensor.transpose(banks[k2 % 2][:, T * kk_ + P * b:T * kk_ + P * b + P], src[:, b, P * k:P * k + P], ident)
                    x.then_inc(s[done].sem, 1)

            token_tiles(xtok, PB[0:2], "x_n", "x_gain", "x_tp")
            pe.wait_ge(s["x_lo"].sem, KT)

            with pe.Fori(0, KVH // 2, 1) as i:
                for gg in range(2):
                    g = 2 * i + gg
                    for j in range(8):
                        u = 6 * gg + j
                        if j < 6:
                            pe.wait_ge(d_evac.sem, 12 * i + u - 1 if u >= 2 else 12 * i)
                            unit_b(u, 12 * i + u)
                        if j == 1:
                            pe.wait_ge(d_evac.sem, 12 * i + u + 1)
                            for tb in range(2):
                                x = nc.tensor.transpose(PB[2][:, P * tb:P * tb + P], vf[:, P * tb:P * tb + P], ident)
                            x.then_inc(s["v_tp"].sem, 1)
                        h = j - 3
                        if 0 <= h < 4:
                            pe.wait_ge(s["k_r"].sem, s["k_r"].at(g))
                            pe.wait_ge(s["q_r"].sem, s["q_r"].at(g, h + 1))
                            if h >= 2:
                                pe.wait_ge(s["sc_m"].sem, s["sc_m"].at(g, h - 1))
                            else:
                                pe.wait_ge(s["sc_m"].sem, s["sc_m"].before(g))
                            for qb in range(2):
                                x = M(PB[3 + h % 2][:, T * qb:T * qb + T], qr[:, h % 2, P * qb:P * qb + P], kr[:], start=True, stop=True)
                            x.then_inc(s["sc"].sem, 1)
                        h = j - 4
                        if 0 <= h < 4:
                            pe.wait_ge(s["prn"].sem, s["prn"].at(g, h + 1))
                            pe.wait_ge(s["p_T"].sem, s["p_T"].at(g, h) if h else s["p_T"].before(g))
                            for sbk in range(2):
                                for qb in range(2):
                                    x = nc.tensor.transpose(PB[5][:, T * sbk + P * qb:T * sbk + P * qb + P], prb[:, h % 2, qb, P * sbk:P * sbk + P], ident)
                            x.then_inc(s["p_tp"].sem, 1)
                            pe.wait_ge(s["p_T"].sem, s["p_T"].at(g, h + 1))
                            pe.wait_ge(s["v_tok"].sem, s["v_tok"].at(g))
                            pe.wait_ge(s["o_ev"].sem, s["o_ev"].at(g, h) if h else s["o_ev"].before(g))
                            for sbk in range(2):
                                x = M(PB[6][:, 0:T], vtok[:, sbk, :], prT[:, sbk, :], start=sbk == 0, stop=sbk == 1)
                            x.then_inc(s["pv"].sem, 1)
            with pe.Fori(0, 4, 1) as i:
                for j in range(4):
                    pe.wait_ge(d_evac.sem, 4 * i + U_GA + j - 1)
                    unit_b(U_GA + j, 4 * i + U_GA + j)
            for j in range(6):
                pe.wait_ge(d_evac.sem, U_LO + j - 1)
                unit_b(U_LO + j, U_LO + j)

            def dense(j, i):
                pe.wait_ge(d_evac.sem, 4 * i + U_RW + j - 1)
                unit_b(U_RW + j, 4 * i + U_RW + j)

            for j in range(4):
                dense(j, 0)
            pe.wait_ge(s["lo_fin"].sem, 1)
            pe.wait_ge(s["lo_sh"].sem, 6)

            def pair(i, nxt):
                def filler(j):
                    if nxt is not None:
                        dense(j, nxt)

                w = lambda n, k=None: pe.wait_ge(s[n].sem, s[n].at(i, k))
                inc = lambda x, n: x.then_inc(s[n].sem, 1)
                pe.wait_ge(s["up_ld"].sem, 16 * 5 * i + 80)
                pe.wait_ge(s["y5"].sem, s["y5"].before(i))
                for q in range(4):
                    x = M(PB[2 + q // 2][:, T * (q % 2):T * (q % 2) + T], upw[0:DL, q, :], lact[0:DL, q, :], start=True, stop=True)
                    if q == 1:
                        inc(x, "lw")
                inc(x, "la")
                for q in range(2):
                    x = M(PB[4][:, 0:T], upg[:, q, :], gact[:, q, :], start=q == 0, stop=q == 1)
                inc(x, "lg")
                w("sqd")
                for tb in range(2):
                    x = M(PB[7][:, 2 * tb:2 * tb + 2], sq[:, P * tb:P * tb + P], hsel, start=True, stop=True)
                inc(x, "ss")
                w("shifted")
                for tb in range(2):
                    x = nc.tensor.transpose(PB[5][:, P * tb:P * tb + P], sh[:, 2, P * tb:P * tb + P], ident)
                inc(x, "vtp")
                w("rrep")
                for tb in range(2):
                    x = M(PB[7][:, P * tb:P * tb + P], rep[:, tb, :], ident, start=True, stop=True)
                inc(x, "rbc")
                filler(0)
                for d in range(2):
                    for q in range(4):
                        tb, h = q // 2, q % 2
                        n = 4 * d + q
                        w("khs", d + 1)
                        w("bhs", d + 1)
                        w("ar", d + 1)
                        if n >= 2:
                            w("gmask", n - 1)
                        else:
                            w("tws")
                            w("tas")
                        hp, ts = slice(64 * h, 64 * h + 64), slice(P * tb, P * tb + P)
                        for a, src in enumerate((bh[d], kh[d])):
                            x = M(PB[2 + q % 2][:, T * a:T * a + T], src[hp, ts], AR[d][hp, :, ts], start=True, stop=True)
                        inc(x, "gram")
                for d in range(2):
                    w("dt0", d + 1)
                    if d == 0:
                        w("vts")
                    for q in range(4):
                        x = nc.tensor.transpose(PB[5 + d][:, P * q:P * q + P], DT[d][:, q, :].bitcast(f32), ident)
                    inc(x, "d0p")
                for l in range(1, LV):
                    m = 1 << l
                    part = lambda t, q, par: t[:, q, :].rearrange("p (n two m) -> p n two m", two=2, m=m)[:, :, par, :]
                    for d in range(2):
                        n = 2 * (l - 1) + d + 1
                        w("ctm", n)
                        if l == 1:
                            w("d0", d + 1)
                            w("gups")
                            w("gmask", 8)
                        else:
                            w("dup", n - 2)
                            w("wev", n - 2)
                        for q in range(4):
                            x = M(PB[4 - d][:, P * q:P * q + P], CT[d][:, q, :], Dm[d][:, q, :], start=True, stop=True)
                        inc(x, "wmm")
                    for d in range(2):
                        n = 2 * (l - 1) + d + 1
                        w("wev", n)
                        if l == 1:
                            w("d0", 2)
                        else:
                            w("dtup", n - 2)
                        bd, bt = (PB[5], PB[6]) if d == 0 else (PB[2], PB[7])
                        if l < LV - 1:
                            for q in range(4):
                                x = M(bd[:, 64 * q:64 * q + 64].rearrange("p (n m) -> p n m", m=m), DT[d][:, q, :], part(W[d], q, d), start=True, stop=True)
                            inc(x, "ddm")
                        for q in range(4):
                            x = M(bt[:, 64 * q:64 * q + 64].rearrange("p (n m) -> p n m", m=m), W[d][:, q, :], part(DT[d], q, 1 - d), start=True, stop=True)
                        inc(x, "dtm")
                    if l in (1, 3, 5):
                        filler((l + 1) // 2)
                for d in range(2):
                    ts = slice(P * d, P * d + P)
                    for a, src in enumerate((kh[d], bh[d])):
                        x = nc.tensor.transpose(PB[3][:, P * (2 * d + a):P * (2 * d + a) + P], src[:, ts], ident)
                inc(x, "kbtp")
                w("dtup")
                w("vts")
                for c in range(2):
                    if c == 1:
                        w("rese", 1)
                        w("due", 1)
                        w("sme")
                    first = True
                    for d in range(2):
                        tb = c if d == 0 else 1 - c
                        if c == 1:
                            M(PB[4][:, P * d:P * d + P], AR[d][:, 0, P * tb:P * tb + P], Sm[:, d, :], start=first, stop=False, skip_group_check=True)
                            first = False
                        for h in range(2):
                            q, o = 2 * tb + h, slice(64 * (2 * d + h), 64 * (2 * d + h) + 64)
                            x = M(PB[4][:, o], G[d][:, q, 2, :], Vt[:, tb, 64 * h:64 * h + 64], start=first, stop=False, skip_group_check=True)
                            first = False
                    inc(x, "rhsm")
                    w("rhsc", c + 1)
                    for d in range(2):
                        tb = c if d == 0 else 1 - c
                        for h in range(2):
                            q, e = 2 * tb + h, 2 * d + h
                            x = M(PB[5][:, 64 * e:64 * e + 64], DT[d][:, q, :], rhs[:, e, :], start=True, stop=True)
                    inc(x, "um")
                    w("ue", c + 1)
                    for d in range(2):
                        tb = c if d == 0 else 1 - c
                        for h in range(2):
                            q, e = 2 * tb + h, 2 * d + h
                            x = M(PB[4][:, 64 * e:64 * e + 64], G[d][:, q, 0, :], U[:, c, e, :], start=False, stop=True, skip_group_check=True)
                    inc(x, "resm")
                    w("rese", c + 1)
                    for d in range(2):
                        tb = c if d == 0 else 1 - c
                        for h in range(2):
                            q, e = 2 * tb + h, 2 * d + h
                            x = M(PB[5][:, T + 64 * e:T + 64 * e + 64], DT[d][:, q, :], rhs[:, e, :], start=True, stop=True)
                    inc(x, "dum")
                    w("due", c + 1)
                    if c == 0:
                        w("kbs2")
                        for d in range(2):
                            o = PB[6][:, P * d:P * d + P]
                            M(o, KB[:, 2 * d, :], Vt[:, d, :], start=True, stop=False)
                            x = M(o, KB[:, 2 * d + 1, :], U[:, 0, 2 * d:2 * d + 2, :].rearrange("p a b -> p (a b)"), start=False, stop=True)
                        inc(x, "smm")
                w("t2")
                x = M(PB[6][:, 0:T], ones_half, rk[:], start=True, stop=True)
                inc(x, "bonm")
                for tb in range(2):
                    ts = slice(P * tb, P * tb + P)
                    d2 = 1 if tb == 0 else 0
                    M(PB[2][:, ts], Sm[:, d2, :], AR[d2][:, 1, ts], start=True, stop=False, skip_group_check=True)
                    for h in range(2):
                        hp, q = slice(64 * h, 64 * h + 64), 2 * tb + h
                        for d in range(2):
                            c = tb if d == 0 else 1 - tb
                            M(PB[2][hp, ts], Vt[:, tb, hp], G[d][:, q, 3, :], start=False, stop=False, skip_group_check=True)
                            x = M(PB[2][hp, ts], U[:, c, 2 * d + h, :], G[d][:, q, 1, :], start=False, stop=d == 1, skip_group_check=True)
                inc(x, "ym")
                w("ye")
                x = M(PB[7][:, 0:T], ones_mean, ysb[:], start=True, stop=True)
                inc(x, "mean")
                w("ysqs")
                for tb in range(2):
                    x = M(PB[7][:, 2 * tb:2 * tb + 2], ysq[:, P * tb:P * tb + P], hsel, start=True, stop=True)
                inc(x, "var")
                w("vrep")
                for tb in range(2):
                    x = M(PB[7][:, P * tb:P * tb + P], rep[:, tb, :], ident, start=True, stop=True)
                inc(x, "vbc")

            with pe.Fori(0, PAIRS - 2, 1) as i:
                pair(i, i + 1)
            pair(PAIRS - 2, PAIRS - 1)
            pair(PAIRS - 1, None)

            pe.wait_ge(s["mg_lo"].sem, 16)
            with pe.Fori(0, 2, 1) as i:
                for j in range(8):
                    n, kc = j // 4, j % 4
                    if kc == 0:
                        pe.wait_ge(s["o_cp"].sem, 2 * i)
                    x = unit_a(U_OUT + j, 8 * i + U_OUT + j, [xT[:, 4 * kc + k, :, :] for k in range(4)], PB[2 * n:2 * n + 2], kc == 0, kc == 3)
                    if kc == 3:
                        pe.wait_ge(w_used.sem, 8 * i + U_OUT + j + 1)
                        pe.sem_inc(s["om"].sem, 1)
            token_tiles(acc, PB[4:6], "h_n", "h_g", "h_tp")
            pe.wait_ge(s["h_lo"].sem, KT)
            with pe.Fori(0, FCH, 1) as i:
                for j in range(8):
                    pe.wait_ge(s["up_re"].sem, s["up_re"].at(i, j - 1) if j >= 2 else s["up_re"].before(i))
                    if j < 2:
                        pe.wait_ge(s["o_cp"].sem, 4)
                    unit_b(U_FF + j, 16 * i + U_FF + j)
                for j in range(8):
                    n, kc = j // 2, j % 2
                    pe.wait_ge(s["up_lo"].sem, s["up_lo"].at(i, 4 * kc + 4))
                    if kc == 0:
                        pe.wait_ge(s["dn_acc"].sem, s["dn_acc"].at(i, n - 2) if n >= 3 else s["dn_acc"].before(i))
                    x = unit_a(U_FF + 8 + j, 16 * i + U_FF + 8 + j, [ft[:, 4 * kc + k, :, :] for k in range(4)],
                               PB[2 + 2 * (n % 3):4 + 2 * (n % 3)], kc == 0, kc == 1)
                    if kc == 1:
                        pe.wait_ge(w_used.sem, 16 * i + U_FF + 8 + j + 1)
                        pe.sem_inc(s["dn"].sem, 1)


INS = ["x", "norm_pre_mix", "w_in", "mu_shift", "attn_sink", "w0_fwd", "w_up_fwd", "w0_bwd", "w_up_bwd", "a0_fwd", "a_up_fwd",
       "a0_bwd", "a_up_bwd", "g_up", "k_k", "k_a", "r_k", "ln_x_gain", "ln_x_bias", "w_out", "norm_post_mix", "norm_pre_ffn",
       "w_ffn_up", "w_ffn_down", "norm_post_ffn"]


def kernel(**inputs):
    import numpy as _np
    import concourse.bacc as _bacc
    from concourse import mybir as _mybir
    from concourse.bass_utils import run_bass_kernel_spmd as _run

    nc = _bacc.Bacc("TRN2", target_bir_lowering=False, num_devices=1)
    arrays, aps = {}, {}
    c, a = constants()
    for name, arr in [(n, _np.ascontiguousarray(inputs[n])) for n in INS] + [("constants", c), ("attn_constants", a)]:
        arrays[f"in_{name}"] = arr
        aps[name] = nc.dram_tensor(f"in_{name}", arr.shape, _mybir.dt.from_np(arr.dtype), kind="ExternalInput").ap()
    out = nc.dram_tensor("out", (1, T, D), _mybir.dt.float32, kind="ExternalOutput").ap()
    block_kernel(nc, aps, aps["constants"], aps["attn_constants"], out)
    r = _run(nc, [arrays], core_ids=[0])
    return r.results[0]["out"]
```

```python
from contextlib import ExitStack

import numpy as np

import concourse.bass as bass
from concourse import mybir

D = 2048
T = 256
P = 128
KT = D // P
HD = 128
KVH = 4
GRP = 4
PAIRS = D // P
DL = 96
GL = 256
FF = 4 * D
EPS = 1e-6
GN_EPS = 64e-5
DECAY_E = float(np.exp(-0.5))
P0SCALE = 2.0 ** 56
LV = 7

Q0, K0, V0 = 0, D, D + 512
SH0 = D + 1024
R0, RK0, RV0 = SH0, SH0 + D, SH0 + 2 * D
LO0 = SH0 + 3 * D
GA0 = LO0 + 4 * DL + GL
GR0 = GA0 + D

C_ID, C_GM, C_MEAN, C_HALF, C_SEL = 0, 128, 640, 768, 896
C_SM = C_SEL + 2
C_END = C_SM + P
CA_COS, CA_SIN, CA_MASK, CA_END = 0, 256, 512, 1024

PARAMS_A = ["mu_shift", "w0_fwd", "w0_bwd", "a0_fwd", "a0_bwd"]
PARAMS_B = ["k_k", "k_a", "r_k", "ln_x_gain", "ln_x_bias", "norm_pre_mix", "norm_pre_ffn"]


class Sig:

    def __init__(self, sem, per=1, base=0):
        self.sem, self.per, self.base = sem, per, base

    def n(self, count):
        return self.base + count

    def at(self, i, k=None):
        return self.base + self.per * i + (self.per if k is None else k)

    def before(self, i):
        return self.base + self.per * i


def constants():
    c = np.zeros((P, C_END), np.float32)
    s, t = np.arange(P)[:, None], np.arange(P)[None, :]
    c[:, C_ID:C_ID + P] = s == t
    c[:, C_GM:C_GM + 128] = s < t
    c[:, C_GM + 128:C_GM + 256] = s <= t
    c[:, C_GM + 256:C_GM + 384] = s > t
    c[:, C_GM + 384:C_GM + 512] = s >= t
    lm = np.zeros((P, 2, LV, P), np.float16)
    for l in range(LV):
        m = 1 << l
        sib = (s // m // 2) == (t // m // 2)
        fwd = sib & (t // m % 2 == 1) & (s // m % 2 == 0)
        bwd = sib & (t // m % 2 == 0) & (s // m % 2 == 1)
        lm[:, 0, l], lm[:, 1, l] = fwd, bwd
    same = (s // 64) == (t // 64)
    c[:, C_MEAN:C_MEAN + P] = same / 64.0
    c[:, C_HALF:C_HALF + P] = same * 0.5
    c[:, C_SM:C_SM + P] = same / P0SCALE
    c[:, C_SEL:C_SEL + 2] = (s // 64) == np.arange(2)[None, :]
    a = np.zeros((P, CA_END), np.float32)
    pos = np.arange(T, dtype=np.float32)
    inv = (np.float32(10000.0) ** (-np.arange(0, HD, 2, dtype=np.float32) / np.float32(HD))).astype(np.float32)
    ang = (pos[None, :] * inv[:, None]).astype(np.float32)
    a[:, CA_COS:CA_COS + T] = np.concatenate([np.cos(ang), np.cos(ang)], 0)
    a[:, CA_SIN:CA_SIN + T] = np.concatenate([-np.sin(ang), np.sin(ang)], 0)
    j = np.arange(T)[None, :]
    for qb in range(2):
        q = np.arange(P)[:, None] + qb * P
        a[:, CA_MASK + qb * T:CA_MASK + (qb + 1) * T] = np.where(np.abs(j - q) <= 128, 0.0, -1e30)
    return c, a, lm


def block_kernel(nc, I, cst_d, csa_d, lm_d, out_d):
    f32, f32r, i32 = mybir.dt.float32, mybir.dt.float32r, mybir.dt.int32
    ACT, ALU, AX = mybir.ActivationFunctionType, mybir.AluOpType, mybir.AxisListType
    w_in, w_out, w_up, w_dn = I["w_in"][0], I["w_out"][0], I["w_ffn_up"][0], I["w_ffn_down"][0]

    ctx = ExitStack()
    with ctx:
        nbuf = [0]

        def sb(name, shape, dt=f32, stack=ctx):
            return stack.enter_context(nc.sbuf_tensor(name, shape, dt))

        def sig(name, per=1):
            return Sig(ctx.enter_context(nc.semaphore(name)), per)

        raw = sb("raw", [P, 4, 2048])
        whi = sb("whi", [P, 2, 2048], f32r)
        wlo = sb("wlo", [P, 2, 2048], f32r)
        xT = sb("xT", [P, KT, 2, T], f32r)
        cst = sb("cst", [P, C_END])
        lmk = sb("lmk", [P, 2, LV, P], mybir.dt.float16)
        pA = sb("pA", [P, 112])
        pB = sb("pB", [P, 112])
        small = sb("small", [P, 64])
        cells = sb("cells", [P, 8])
        epsh = sb("epsh", [P, 4])
        ident = cst[:, C_ID:C_ID + P]
        ones_mean, ones_half, hsel = cst[:, C_MEAN:C_MEAN + P], cst[:, C_HALF:C_HALF + P], cst[:, C_SEL:C_SEL + 2]
        PB = [ctx.enter_context(nc.psum_tensor(f"bank{b}", [P, 512], f32)) for b in range(8)]

        mixers = ExitStack()
        mrg = sb("mrg", [P, KT, T], stack=mixers)
        lact = sb("lact", [P, 4, T], stack=mixers)
        gact = sb("gact", [P, 2, T], stack=mixers)
        muL = sb("muL", [P, 6], stack=mixers)
        raw4 = sb("raw4", [P, 4, T + 2], stack=mixers)

        att = ExitStack()
        xtok = sb("xtok", [P, 2, D], stack=att)
        csa = sb("csa", [P, CA_END], stack=att)
        xf = sb("xf", [P, 2, T], stack=att)
        prow = sb("prow", [P, 3, P], stack=att)
        tokA = sb("tokA", [P, 2, T], stack=att)
        tokB = sb("tokB", [P, 2, T], stack=att)
        kr = sb("kr", [P, T], stack=att)
        qr = sb("qr", [P, 2, T], stack=att)
        vf = sb("vf", [P, T], stack=att)
        vtok = sb("vtok", [P, 2, HD], stack=att)
        scm = sb("scm", [P, 2, T], stack=att)
        prb = sb("prb", [P, 2, 2, T], stack=att)
        prT = sb("prT", [P, 2, T], stack=att)
        sinkb = sb("sinkb", [P, 16], stack=att)
        sm = sb("sm", [P, 16], stack=att)
        att.close()

        rw = ExitStack()
        G = [sb(f"G{d}", [P, 4, 4, P], stack=rw) for d in range(2)]
        CT = [sb(f"CT{d}", [P, 4, P], f32r, stack=rw) for d in range(2)]
        W = [sb(f"W{d}", [P, 4, P], f32r, stack=rw) for d in range(2)]
        Dm = [sb(f"Dm{d}", [P, 4, P], f32r, stack=rw) for d in range(2)]
        DT = [sb(f"DT{d}", [P, 4, P], f32r, stack=rw) for d in range(2)]
        sh = sb("sh", [P, 3, T], stack=rw)
        nb = sb("nb", [P, 3, T], stack=rw)
        gt = sb("gt", [P, T], stack=rw)
        gup = sb("gup", [P, T], stack=rw)
        upw = sb("upw", [P, 4, P], stack=rw)
        upg = sb("upg", [P, 2, P], stack=rw)
        AR = [sb(f"AR{d}", [P, 2, T], stack=rw) for d in range(2)]
        kh = [sb(f"kh{d}", [P, T], stack=rw) for d in range(2)]
        Pd = [sb(f"Pd{d}", [P, 2, P + 1], stack=rw) for d in range(2)]
        ta = [sb(f"ta{d}", [P, T], stack=rw) for d in range(2)]
        dec = [sb(f"dec{d}", [P, T], stack=rw) for d in range(2)]
        tw = dec
        km = kh
        bh = ta
        kk = sb("kk", [P, T], stack=rw)
        sq = nb[:, 0, :]
        kA = sb("kA", [P, T], stack=rw)
        kB = sb("kB", [P, T], stack=rw)
        rk = sb("rk", [P, T], stack=rw)
        rep = sb("rep", [P, 2, P], stack=rw)
        Vt = sb("Vt", [P, 2, P], stack=rw)
        KB = sb("KB", [P, 4, P], stack=rw)
        rhs = sb("rhs", [P, 4, 64], f32r, stack=rw)
        U = sb("U", [P, 2, 4, 64], stack=rw)
        Sm = sb("Sm", [P, 2, P], stack=rw)
        zero = sb("zero", [P, P], stack=rw)
        der = sb("der", [P, 96], stack=rw)
        st = sb("st", [P, 8], stack=rw)
        ysb = sb("ysb", [P, T], stack=rw)
        yc = sb("yc", [P, T], stack=rw)
        ysq = sb("ysq", [P, T], stack=rw)
        bon = sb("bon", [P, T], stack=rw)
        AS = sb("AS", [P, 2, 2, P], stack=rw)
        pl = sb("pl", [P, 2], stack=rw)
        rw.close()
        mixers.close()

        ffn = ExitStack()
        hres = sb("hres", [P, 2, D], stack=ffn)
        acc = sb("acc", [P, 2, D], stack=ffn)
        gain = sb("gain", [P, D], stack=ffn)
        ft = sb("ft", [P, 8, 2, T], f32r, stack=ffn)
        fa = sb("fa", [P, 2, T], stack=ffn)
        fs = sb("fs", [P, 2, T], stack=ffn)
        junk = sb("junk", [P, 512], stack=ffn)
        hf = sb("hf", [P, 2, T], stack=ffn)
        ffn.close()

        raw_full = [sig(f"raw_full{s}") for s in range(4)]
        w_hi, w_lo, w_used, d_evac = sig("w_hi"), sig("w_lo"), sig("w_used"), sig("d_evac")
        s = {}
        for name, per in dict(
            ld_x=1, ld_c=1, ld_p=1, n_sq=8, n_st=2, n_pow=1, x_n=1, x_tp=1, x_gain=1, x_hi=1, x_lo=1, prm_ms=1,
            prm_tp=1, prm_ev=1, exp_ms=1,
            k_r1=1, k_r=1, v_tp=1, v_tok=1, q_r1=4, q_r=4, sc=4, sc_m=4, mx=4, mx2=4, neg=4,
            ex=4, esink=4, den=4, rden=4, prn=4, p_tp=4, p_T=4, pv=4, o_ev=4,
            ga_m=4, lo_nb=1, lo_df=1, lo_sh=1, lo_act=1, lo_fin=1, drv=1, zr=1,
            up_ld=1, sh_nb=1, sh_df=1, shifted=1, gate_t=1, kkr=1, sqd=1, ss=1, ssm=1, rs=1, rrep=1, rbc=1, nkk=1,
            kAB=1, rkd=1, lw=1, la=1, lg=1, tws=1, decs=2, tas=1, gups=1, scan=2, inv=2, ar=2, tt=2, bhs=2, km1=2, km2=2,
            khs=2, kbs=1, t2=1, vtp=1, vts=1, gram=8, gmask=8, e0=2, dt0=2, d0p=2, d0=2, ctm=12, wmm=12, wev=12,
            ddm=10, dtm=12, dup=10, dtup=12, kbtp=1, kbs2=1, rhsm=2, rhsc=2, um=2, ue=2, resm=2, rese=2, dum=2, due=2,
            smm=1, sme=1, ym=1, ye=1, mean=1, ycs=1, ysqs=1, var=1, vars=1, vpow=1, vrep=1, vbc=1, bonm=1, bonv=1, asc=1, plc=1,
            y1=1, y2=1, y3=1, y4=2, y5=1,
            mg_hi=1, mg_lo=1, om=1, o_cp=1, ld_h=1, ld_g=1, m_n=1, m_h=1,
            h_n=1, h_tp=1, h_g=1, h_hi=1, h_lo=1, up_re=8, up_sq=8, up_hi=8, up_lo=8, dn=4, dn_acc=4, f_n=1, f_o=1, ld_g2=1, done=1, acc0=1,
        ).items():
            s[name] = sig(name, per)
        CHARGED = [w_lo, d_evac] + [s[n] for n in (
            "k_r1", "q_r1", "k_r", "q_r", "v_tp", "sc", "sc_m", "esink", "p_tp", "p_T", "o_ev", "ga_m", "lg", "y5", "due", "dum",
            "ye", "rese", "y1", "ym", "y3", "sme", "asc", "kbtp", "gate_t", "shifted", "up_sq", "up_re", "dn", "dn_acc", "o_cp")]
        for x in CHARGED:
            x.base = 1

        U_ATT, U_GA, U_LO, U_RW = 0, 24, 40, 46
        U_OUT = U_RW + 4 * PAIRS
        U_FF = U_OUT + 16
        FCH = 8




        block = ctx.enter_context(nc.Block())

        @block.sync
        def _(sp):
            def load(u_static, u_count, src, n=P, style="B"):
                slot = u_static % 4
                if u_static >= 4:
                    sp.wait_ge(w_lo.sem, w_lo.n(u_count - 3))
                if style == "B":
                    dst = raw[:, slot, :].rearrange("p (k c) -> p k c", k=KT)[:, :, 0:n]
                else:
                    dst = raw[:, slot, :].rearrange("p (k c) -> p k c", k=4)
                sp.dma_start(dst, src).then_inc(raw_full[slot].sem, 16)

            def cols(c, n=P):
                return w_in[:, bass.ds(c, n)].rearrange("(k p) c -> p k c", p=P)

            for x in CHARGED:
                sp.sem_inc(x.sem, 1)
            sp.dma_start(xtok[:], I["x"][0].rearrange("(b p) c -> p b c", p=P)).then_inc(s["ld_x"].sem, 16)
            sp.dma_start(cst[:], cst_d).then_inc(s["ld_c"].sem, 16)
            sp.dma_start(csa[:], csa_d).then_inc(s["ld_c"].sem, 16)
            sp.dma_start(lmk[:], lm_d).then_inc(s["ld_c"].sem, 16)
            row = 0
            sp.wait_ge(s["prm_ms"].sem, s["prm_ms"].n(1))
            mu = I["mu_shift"][0]
            n_prm = 0
            for slot, names in ((0, PARAMS_A), (1, PARAMS_B)):
                row = 0
                for name in names:
                    v = mu[0:3 * D] if name == "mu_shift" else I[name][0]
                    n = v.shape[0] // P
                    sp.dma_start(prow[row:row + n, slot, :], v.rearrange("(t c) -> t c", c=P)).then_inc(s["ld_p"].sem, 16)
                    n_prm += 1
                    row += n
            sp.dma_start(prow[0:4, 2, 0:DL], mu[3 * D:3 * D + 4 * DL].rearrange("(t c) -> t c", c=DL)).then_inc(s["ld_p"].sem, 16)
            sp.dma_start(prow[4:6, 2, :], mu[3 * D + 4 * DL:].rearrange("(t c) -> t c", c=P)).then_inc(s["ld_p"].sem, 16)
            sp.dma_start(sinkb[:], I["attn_sink"].partition_broadcast(P)[:, 0, :]).then_inc(s["ld_p"].sem, 16)
            with sp.Fori(0, KVH // 2, 1) as i:
                for gg in range(2):
                    for j in range(6):
                        u = 6 * gg + j
                        c = [K0 + P * gg + 2 * P * i, V0 + P * gg + 2 * P * i][j] if j < 2 else \
                            Q0 + P * (4 * gg + j - 2) + 8 * P * i
                        slot = u % 4
                        if u >= 4:
                            sp.wait_ge(w_lo.sem, w_lo.n(12 * i + u - 3))
                        else:
                            sp.wait_ge(w_lo.sem, w_lo.n(12 * i))
                        sp.dma_start(raw[:, slot, :].rearrange("p (k c) -> p k c", k=KT), cols(c)).then_inc(raw_full[slot].sem, 16)
            with sp.Fori(0, 4, 1) as i:
                for j in range(4):
                    load(U_GA + j, 4 * i + U_GA + j, cols(GA0 + P * j + 4 * P * i))
            lora = [(LO0 + DL * j, DL) for j in range(4)] + [(LO0 + 4 * DL + P * j, P) for j in range(2)]
            for j, (c, n) in enumerate(lora):
                load(U_LO + j, U_LO + j, w_in[:, c:c + n].rearrange("(k p) c -> p k c", p=P), n)

            def pair_units(i):
                for j, c0 in enumerate((RK0, R0, RV0, GR0)):
                    load(U_RW + j, 4 * i + U_RW + j, cols(c0 + P * i))

            def pair_ups(i):
                if not isinstance(i, int) or i > 0:
                    sp.wait_ge(s["lg"].sem, s["lg"].before(i))
                for j, name in enumerate(("w_up_fwd", "w_up_bwd", "a_up_fwd", "a_up_bwd")):
                    sp.dma_start(upw[0:DL, j, :], I[name][0][:, bass.ds(P * i, P)]).then_inc(s["up_ld"].sem, 16)
                sp.dma_start(upg[:], I["g_up"][0][:, bass.ds(P * i, P)].rearrange("(k p) c -> p k c", p=P)).then_inc(s["up_ld"].sem, 16)

            pair_units(0)
            sp.wait_ge(s["ga_m"].sem, s["ga_m"].n(16))
            sp.wait_ge(s["o_ev"].sem, s["o_ev"].n(16))
            pair_ups(0)
            pair_units(1)
            with sp.Fori(0, PAIRS - 2, 1) as i:
                pair_units(i + 2)
                pair_ups(i + 1)
            pair_ups(PAIRS - 1)

            def out_units(i, u0, wt, rows):
                for j in range(8):
                    nblk, kc = j // 4, j % 4
                    load(u0 + j, 8 * i + u0 + j, wt[kc * 512:(kc + 1) * 512, bass.ds(512 * nblk + 1024 * i, 512)]
                         .rearrange("(k p) c -> p k c", p=P), style="A")

            with sp.Fori(0, 2, 1) as i:
                out_units(i, U_OUT, w_out, D)
            sp.wait_ge(s["mg_lo"].sem, s["mg_lo"].n(16))
            sp.dma_start(hres[:], I["x"][0].rearrange("(b p) c -> p b c", p=P)).then_inc(s["ld_h"].sem, 16)
            sp.dma_start(gain[:], I["norm_post_mix"].partition_broadcast(P)[:, 0, :]).then_inc(s["ld_g"].sem, 16)

            with sp.Fori(0, FCH, 1) as i:
                for j in range(8):
                    load(U_FF + j, 16 * i + U_FF + j, w_up[:, bass.ds(P * j + 1024 * i, P)].rearrange("(k p) c -> p k c", p=P))
                for j in range(8):
                    nblk, kc = j // 2, j % 2
                    load(U_FF + 8 + j, 16 * i + U_FF + 8 + j,
                         w_dn[bass.ds(512 * kc + 1024 * i, 512), 512 * nblk:512 * nblk + 512].rearrange("(k p) c -> p k c", p=P), style="A")
            sp.wait_ge(s["m_h"].sem, s["m_h"].n(2))
            sp.dma_start(gain[:], I["norm_post_ffn"].partition_broadcast(P)[:, 0, :]).then_inc(s["ld_g2"].sem, 16)
            for b in range(2):
                sp.wait_ge(s["f_o"].sem, s["f_o"].n(b + 1))
                sp.dma_start(out_d[0][b * P:(b + 1) * P, :], acc[:, b, :]).then_inc(s["done"].sem, 16)
            sp.wait_ge(s["done"].sem, s["done"].n(32))

        @block.scalar
        def _(act):
            A = nc.scalar

            def cut_hi(u_static, u, half=None):
                if half == 1:
                    A.activation(whi[:, u_static % 2, 1024:], raw[:, u_static % 4, 1024:], ACT.Copy).then_inc(w_hi.sem, 1)
                    return
                slot = u_static % 4
                full = 16 * (u_static // 4 + 1)
                step = u - u_static
                act.wait_ge(raw_full[slot].sem, raw_full[slot].n(full + step * 4))
                if u_static >= 2:
                    act.wait_ge(w_used.sem, w_used.n(u - 1))
                if half is None:
                    A.activation(whi[:, u_static % 2, :], raw[:, slot, :], ACT.Copy).then_inc(w_hi.sem, 1)
                else:
                    A.activation(whi[:, u_static % 2, 0:1024], raw[:, slot, 0:1024], ACT.Copy)

            act.wait_ge(s["ld_x"].sem, s["ld_x"].n(16))
            for b in range(2):
                for q in range(4):
                    A.activation(tokB[:].rearrange("p a t -> p (a t)"), xtok[:, b, 512 * q:512 * q + 512], ACT.Square,
                                 accum_out=small[:, 4 * b + q:4 * b + q + 1]).then_inc(s["n_sq"].sem, 1)
                    act.wait_ge(s["n_sq"].sem, s["n_sq"].n(4 * b + q + 1))
            for k in range(KT):
                act.wait_ge(s["x_gain"].sem, s["x_gain"].n(k + 1))
                A.activation(xT[:, k, 0, :], xf[:, k % 2, :], ACT.Copy).then_inc(s["x_hi"].sem, 1)

            cut_hi(0, 0)
            cut_hi(1, 1)
            with act.Fori(0, KVH // 2, 1) as i:
                for gg in range(2):
                    g = 2 * i + gg
                    for j in range(8):
                        u = 6 * gg + j
                        if j < 6:
                            act.wait_ge(w_used.sem, w_used.n(12 * i + u + 1))
                            bank = PB[u % 2]
                            if j == 1:
                                act.wait_ge(s["v_tp"].sem, s["v_tp"].n(g))
                                A.activation(vf[:], bank[:, 0:T], ACT.Copy).then_inc(d_evac.sem, 1)
                            else:
                                done = s["k_r1"].before(g) if j == 0 else s["q_r1"].at(g, j - 2)
                                act.wait_ge(s["k_r1"].sem, s["k_r1"].before(g) if j == 0 else s["k_r1"].at(g))
                                act.wait_ge(s["q_r1"].sem, s["q_r1"].before(g) if j == 0 else s["q_r1"].at(g, j - 2))
                                A.activation(tokA[:, 0, :], bank[:, 0:T], ACT.Copy)
                                A.activation(tokA[0:64, 1, :], bank[64:P, 0:T], ACT.Copy)
                                A.activation(tokA[64:P, 1, :], bank[0:64, 0:T], ACT.Copy).then_inc(d_evac.sem, 1)
                            nu = u + 2
                            if gg == 0 or j < 4:
                                act.wait_ge(raw_full[nu % 4].sem, raw_full[nu % 4].n(48 * i + 16 * (nu // 4 + 1)))
                                act.wait_ge(w_used.sem, w_used.n(12 * i + nu - 1))
                                A.activation(whi[:, nu % 2, :], raw[:, nu % 4, :], ACT.Copy).then_inc(w_hi.sem, 1)
                            else:
                                act.wait_ge(raw_full[nu % 4].sem, raw_full[nu % 4].n(48 * i + 16 * (nu // 4 + 1)))
                                act.wait_ge(w_used.sem, w_used.n(12 * i + nu - 1))
                                A.activation(whi[:, nu % 2, :], raw[:, nu % 4, :], ACT.Copy).then_inc(w_hi.sem, 1)
                        if j == 1:
                            act.wait_ge(s["v_tp"].sem, s["v_tp"].at(g))
                            A.activation(vtok[:].rearrange("p a b -> p (a b)"), PB[2][:, 0:T], ACT.Copy).then_inc(s["v_tok"].sem, 1)
                        h = j - 3
                        if 0 <= h < 4:
                            n = s["neg"].at(g, h + 1)
                            act.wait_ge(s["neg"].sem, n)
                            act.wait_ge(s["p_tp"].sem, s["p_tp"].at(g, h - 1) if h >= 2 else s["p_tp"].before(g))
                            for qb in range(2):
                                x = A.activation(prb[:, h % 2, qb, :], scm[:, qb, :], ACT.Exp, bias=sm[:, 6 + qb:7 + qb],
                                                 scale=float(HD) ** -0.5, accum_out=sm[:, 8 + qb:9 + qb])
                            x.then_inc(s["ex"].sem, 1)
                            A.activation(sm[:, 10:12], sm[:, 4:6], ACT.Exp).then_inc(s["esink"].sem, 1)
                        h = j - 4
                        if 0 <= h < 4:
                            act.wait_ge(s["p_tp"].sem, s["p_tp"].at(g, h + 1))
                            A.activation(prT[:].rearrange("p a b -> p (a b)"), PB[5][:, :], ACT.Copy).then_inc(s["p_T"].sem, 1)
                            act.wait_ge(s["pv"].sem, s["pv"].at(g, h + 1))
                            A.activation(mrg[:, bass.ds(4 * gg + h + 8 * i, 1), :].rearrange("p a t -> p (a t)"), PB[6][:, 0:T],
                                         ACT.Copy).then_inc(s["o_ev"].sem, 1)
            with act.Fori(0, 4, 1) as i:
                for j in range(4):
                    u = U_GA + j
                    act.wait_ge(w_used.sem, w_used.n(4 * i + u + 1))
                    act.wait_ge(s["ga_m"].sem, s["ga_m"].at(i, j))
                    A.activation(tokA[:, j % 2, :], PB[u % 2][:, 0:T], ACT.Tanh, scale=0.5).then_inc(d_evac.sem, 1)
                    cut_hi(u + 2, 4 * i + u + 2)
            for j in range(6):
                u = U_LO + j
                n = DL if j < 4 else P
                act.wait_ge(w_used.sem, w_used.n(u + 1))
                if j == 0:
                    act.wait_ge(s["zr"].sem, s["zr"].n(2))
                else:
                    act.wait_ge(s["lo_sh"].sem, s["lo_sh"].n(j))
                A.activation(raw4[0:n, 0, 1:T + 1], PB[u % 2][0:n, 0:T], ACT.Copy).then_inc(d_evac.sem, 1)
                cut_hi(u + 2, u + 2)
                act.wait_ge(s["lo_sh"].sem, s["lo_sh"].n(j + 1))
                if j < 2:
                    A.activation(lact[0:n, j, :], lact[0:n, j, :], ACT.Tanh).then_inc(s["lo_act"].sem, 1)
                elif j >= 4:
                    A.activation(gact[:, j - 4, :], gact[:, j - 4, :], ACT.Tanh, scale=0.5).then_inc(s["lo_act"].sem, 1)

            def dense(j, i):
                u = U_RW + j
                act.wait_ge(w_used.sem, w_used.n(4 * i + u + 1))
                if j < 3:
                    act.wait_ge(s["shifted"].sem, s["shifted"].before(i))
                else:
                    act.wait_ge(s["gate_t"].sem, s["gate_t"].before(i))
                slot = (1, 0, 2, 3)[j]
                A.activation(raw4[:, slot, 1:T + 1], PB[u % 2][:, 0:T], ACT.Copy).then_inc(d_evac.sem, 1)

            def cut_pair(j, i, half=None):
                if i is not None:
                    cut_hi(U_RW + j + 2, 4 * i + U_RW + j + 2, half)

            def decays(n):
                act.wait_ge(s["kbtp"].sem, s["kbtp"].before(n))
                act.wait_ge(s["lw"].sem, s["lw"].at(n))
                for d in range(2):
                    x = A.activation(tw[d][:], PB[2][:, T * d:T * d + T], ACT.Tanh, scale=0.5,
                                     bias=der[:, bass.ds(16 * d + n, 1)])
                x.then_inc(s["tws"].sem, 1)

            def decays_exp(n):
                act.wait_ge(s["tws"].sem, s["tws"].at(n))
                for d in range(2):
                    A.activation(dec[d][:], tw[d][:], ACT.Exp, scale=-0.5 * DECAY_E, bias=-0.5 * DECAY_E).then_inc(s["decs"].sem, 1)

            def rates(n):
                act.wait_ge(s["la"].sem, s["la"].at(n))
                for d in range(2):
                    x = A.activation(ta[d][:], PB[3][:, T * d:T * d + T], ACT.Tanh, scale=0.5,
                                     bias=der[:, bass.ds(32 + 16 * d + n, 1)])
                x.then_inc(s["tas"].sem, 1)

            def values(n):
                act.wait_ge(s["ym"].sem, s["ym"].before(n))
                act.wait_ge(s["vtp"].sem, s["vtp"].at(n))
                A.activation(Vt[:].rearrange("p a b -> p (a b)"), PB[5][:, 0:T], ACT.Copy).then_inc(s["vts"].sem, 1)

            def pair(i, n, d1, d2):
                w = lambda name, k=None: act.wait_ge(s[name].sem, s[name].at(i, k))
                act.wait_ge(s["y5"].sem, s["y5"].before(i))
                w("lg")
                A.activation(gup[:], PB[4][:, 0:T], ACT.Copy).then_inc(s["gups"].sem, 1)
                A.activation(gt[:], raw4[:, 3, 1:T + 1], ACT.Tanh, scale=0.5).then_inc(s["gate_t"].sem, 1)
                cut_pair(1, d1, 0)
                cut_pair(1, d1, 1)
                for l in range(1, LV):
                    for d in range(2):
                        w("wmm", 2 * (l - 1) + d + 1)
                        A.activation(W[d][:].rearrange("p a b -> p (a b)"), PB[4 - d][:, :], ACT.Copy).then_inc(s["wev"].sem, 1)
                        if l == 3 and d == 0 and d1 is not None:
                            dense(2, d1)
                        if l in (3, 4) and d == 1 and d2 is not None:
                            cut_pair(2, d1, l - 3)
                w("kbtp")
                A.activation(KB[:].rearrange("p a b -> p (a b)"), PB[3][:, :], ACT.Copy).then_inc(s["kbs2"].sem, 1)
                if d1 is not None:
                    dense(3, d1)
                for c in range(2):
                    w("rhsm", c + 1)
                    A.activation(rhs[:].rearrange("p a b -> p (a b)"), PB[4][:, 0:T], ACT.Copy).then_inc(s["rhsc"].sem, 1)
                    if c == 0 and n is not None:
                        decays(n)
                    w("um", c + 1)
                    A.activation(U[:, c, :, :].rearrange("p a b -> p (a b)"), PB[5][:, 0:T], ACT.Copy).then_inc(s["ue"].sem, 1)
                    if c == 0:
                        if n is not None:
                            decays_exp(n)
                        if d2 is not None:
                            cut_pair(3, d1, 0)
                        if n is not None:
                            rates(n)
                        if d2 is not None:
                            cut_pair(3, d1, 1)
                            dense(0, d2)
                    else:
                        cut_pair(0, d2, 0)
                        cut_pair(0, d2, 1)
                act.wait_ge(s["y3"].sem, s["y3"].before(i))
                w("ym")
                A.activation(ysb[:], PB[2][:, 0:T], ACT.Copy).then_inc(s["ye"].sem, 1)
                if n is not None:
                    values(n)
                w("ycs")
                A.activation(ysq[:], yc[:], ACT.Square).then_inc(s["ysqs"].sem, 1)
                if d2 is not None:
                    dense(1, d2)

            for j in range(4):
                dense(j, 0)
                cut_pair(j, 0)
            decays(0)
            decays_exp(0)
            rates(0)
            act.wait_ge(s["vtp"].sem, s["vtp"].at(0))
            A.activation(Vt[:].rearrange("p a b -> p (a b)"), PB[5][:, 0:T], ACT.Copy).then_inc(s["vts"].sem, 1)
            dense(0, 1)
            cut_pair(0, 1)
            dense(1, 1)
            with act.Fori(0, PAIRS - 2, 1) as i:
                pair(i, i + 1, i + 1, i + 2)
            pair(PAIRS - 2, PAIRS - 1, PAIRS - 1, None)
            pair(PAIRS - 1, None, None, None)

            act.wait_ge(w_used.sem, w_used.n(U_OUT))
            act.wait_ge(s["y5"].sem, s["y5"].n(16))
            for k in range(KT):
                A.activation(xT[:, k, 0, :], mrg[:, k, :], ACT.Copy).then_inc(s["mg_hi"].sem, 1)
            cut_hi(U_OUT, U_OUT)
            cut_hi(U_OUT + 1, U_OUT + 1)
            with act.Fori(0, 2, 1) as i:
                for j in range(8):
                    cut_hi(U_OUT + j + 2, 8 * i + U_OUT + j + 2)
                    if j % 4 == 3:
                        n = j // 4
                        act.wait_ge(s["om"].sem, s["om"].n(2 * i + n + 1))
                        act.wait_ge(s["mg_lo"].sem, s["mg_lo"].n(16))
                        for b in range(2):
                            x = A.activation(acc[:, b, bass.ds(512 * n + 1024 * i, 512)], PB[2 * n + b][:, :], ACT.Copy)
                        x.then_inc(s["o_cp"].sem, 1)

            def sumsq(src, norm, col):
                for b in range(2):
                    for q in range(4):
                        A.activation(junk[:], src[:, b, 512 * q:512 * q + 512], ACT.Square,
                                     accum_out=small[:, col + 4 * b + q:col + 4 * b + q + 1]).then_inc(s["n_sq"].sem, 1)
                        act.wait_ge(s["n_sq"].sem, s["n_sq"].at(norm, 4 * b + q + 1))

            act.wait_ge(s["o_cp"].sem, s["o_cp"].n(4))
            sumsq(acc, 1, 16)
            act.wait_ge(s["m_h"].sem, s["m_h"].n(2))
            sumsq(hres, 2, 32)
            for k in range(KT):
                act.wait_ge(s["h_g"].sem, s["h_g"].n(k + 1))
                if k == 0:
                    act.wait_ge(w_used.sem, w_used.n(U_FF))
                A.activation(xT[:, k, 0, :], hf[:, k % 2, :], ACT.Copy).then_inc(s["h_hi"].sem, 1)
            def chunk(i, last):
                for j in range(16):
                    u = U_FF + j
                    if j < 8:
                        act.wait_ge(w_used.sem, w_used.n(16 * i + u + 1))
                        act.wait_ge(s["up_sq"].sem, s["up_sq"].at(i, j - 1) if j else s["up_sq"].before(i))
                        A.activation(fa[:, j % 2, :], PB[u % 2][:, 0:T], ACT.Relu).then_inc(s["up_re"].sem, 1)
                    if not (last and j >= 14):
                        cut_hi(u + 2, 16 * i + u + 2)
                    if j < 8:
                        act.wait_ge(s["up_sq"].sem, s["up_sq"].at(i, j + 1))
                        if j == 0:
                            act.wait_ge(s["dn"].sem, s["dn"].before(i))
                        A.activation(ft[:, j, 0, :], fs[:, j % 2, :], ACT.Copy).then_inc(s["up_hi"].sem, 1)

            with act.Fori(0, FCH - 1, 1) as i:
                chunk(i, False)
            chunk(FCH - 1, True)
            act.wait_ge(s["dn_acc"].sem, s["dn_acc"].n(4 * FCH))
            sumsq(acc, 3, 48)

        @block.vector
        def _(dve):
            V = nc.vector

            def cut_lo(u_static, u, half=None):
                if half != 1:
                    dve.wait_ge(w_hi.sem, w_hi.n(u + 1))
                part = {None: slice(0, 2048), 0: slice(0, 1024), 1: slice(1024, 2048)}[half]
                x = V.tensor_tensor(wlo[:, u_static % 2, part], raw[:, u_static % 4, part], whi[:, u_static % 2, part].bitcast(f32),
                                    ALU.subtract)
                if half != 0:
                    x.then_inc(w_lo.sem, 1)

            def rstd(col, norm, eps=EPS):
                dve.wait_ge(s["n_sq"].sem, s["n_sq"].at(norm))
                V.tensor_reduce(small[:, col + 8:col + 10], small[:, col:col + 8].rearrange("p (b q) -> p b q", b=2), AX.X, ALU.add)\
                    .then_inc(s["n_st"].sem, 1)
                dve.wait_ge(s["n_st"].sem, s["n_st"].at(norm, 1))
                V.tensor_scalar(small[:, col + 10:col + 12], small[:, col + 8:col + 10], 1.0 / D, eps, ALU.mult, ALU.add)\
                    .then_inc(s["n_st"].sem, 1)
                dve.wait_ge(s["n_pow"].sem, s["n_pow"].at(norm))

            V.memset(prow[:], 0.0).then_inc(s["prm_ms"].sem, 1)
            V.memset(epsh[:], -0.5).then_inc(s["exp_ms"].sem, 1)
            rstd(0, 0)
            for b in range(2):
                V.tensor_scalar(xtok[:, b, :], xtok[:, b, :], small[:, 12 + b:13 + b], None, ALU.mult).then_inc(s["x_n"].sem, 1)
            dve.wait_ge(s["prm_tp"].sem, s["prm_tp"].n(3))
            V.tensor_copy(pA[:], PB[7][:, 0:112]).then_inc(s["prm_ev"].sem, 1)
            V.tensor_copy(pB[:], PB[7][:, 128:240]).then_inc(s["prm_ev"].sem, 1)
            V.tensor_copy(muL[:], PB[7][:, 256:262]).then_inc(s["prm_ev"].sem, 1)
            dve.wait_ge(s["prm_ev"].sem, s["prm_ev"].n(3))
            for k in range(KT):
                dve.wait_ge(s["x_tp"].sem, s["x_tp"].n(k // 2 + 1))
                if k >= 2:
                    dve.wait_ge(s["x_lo"].sem, s["x_lo"].n(k - 1))
                V.tensor_scalar(xf[:, k % 2, :], PB[(k // 2) % 2][:, T * (k % 2):T * (k % 2) + T], pB[:, 80 + k:81 + k], None,
                                ALU.mult).then_inc(s["x_gain"].sem, 1)
                dve.wait_ge(s["x_hi"].sem, s["x_hi"].n(k + 1))
                V.tensor_tensor(xT[:, k, 1, :], xf[:, k % 2, :], xT[:, k, 0, :].bitcast(f32), ALU.subtract).then_inc(s["x_lo"].sem, 1)

            cut_lo(0, 0)
            cut_lo(1, 1)
            cos, sin = csa[:, CA_COS:CA_COS + T], csa[:, CA_SIN:CA_SIN + T]
            wmask = csa[:, CA_MASK:CA_MASK + 2 * T]
            with dve.Fori(0, KVH // 2, 1) as i:
                for gg in range(2):
                    g = 2 * i + gg
                    for j in range(8):
                        u = 6 * gg + j
                        if j < 6:
                            dve.wait_ge(d_evac.sem, d_evac.n(12 * i + u + 1))
                            if j != 1:
                                r1, r2 = (s["k_r1"], s["k_r"]) if j == 0 else (s["q_r1"], s["q_r"])
                                m = 1 if j == 0 else j - 1
                                dst = kr[:] if j == 0 else qr[:, j % 2, :]
                                if j == 0:
                                    dve.wait_ge(s["q_r"].sem, s["q_r"].before(g))
                                else:
                                    dve.wait_ge(s["k_r"].sem, s["k_r"].at(g))
                                    dve.wait_ge(s["q_r"].sem, s["q_r"].at(g, j - 2))
                                V.tensor_tensor(tokB[:, 0, :], tokA[:, 0, :], cos, ALU.mult)
                                V.tensor_tensor(tokB[:, 1, :], tokA[:, 1, :], sin, ALU.mult).then_inc(r1.sem, 1)
                                dve.wait_ge(r1.sem, r1.at(g, m))
                                if j == 0:
                                    dve.wait_ge(s["sc"].sem, s["sc"].before(g))
                                elif j >= 4:
                                    dve.wait_ge(s["sc"].sem, s["sc"].at(g, j - 3))
                                V.tensor_tensor(dst, tokB[:, 0, :], tokB[:, 1, :], ALU.add).then_inc(r2.sem, 1)
                            cut_lo(u + 2, 12 * i + u + 2)
                        h = j - 3
                        if 0 <= h < 4:
                            dve.wait_ge(s["sc"].sem, s["sc"].at(g, h + 1))
                            dve.wait_ge(s["esink"].sem, s["esink"].at(g, h) if h else s["esink"].before(g))
                            V.tensor_tensor(scm[:].rearrange("p a b -> p (a b)"), PB[3 + h % 2][:, :], wmask, ALU.add).then_inc(s["sc_m"].sem, 1)
                            dve.wait_ge(s["sc_m"].sem, s["sc_m"].at(g, h + 1))
                            V.tensor_reduce(sm[:, 0:2], scm[:], AX.X, ALU.max).then_inc(s["mx"].sem, 1)
                            dve.wait_ge(s["mx"].sem, s["mx"].at(g, h + 1))
                            sink = sinkb[:, bass.ds(4 * gg + h + 8 * i, 1)]
                            V.tensor_scalar(sm[:, 2:4], sm[:, 0:2], float(HD) ** -0.5, sink, ALU.mult, ALU.max).then_inc(s["mx2"].sem, 1)
                            dve.wait_ge(s["mx2"].sem, s["mx2"].at(g, h + 1))
                            V.tensor_scalar(sm[:, 6:8], sm[:, 2:4], -1.0, None, ALU.mult)
                            V.tensor_scalar(sm[:, 4:6], sm[:, 2:4], -1.0, sink, ALU.mult, ALU.add).then_inc(s["neg"].sem, 1)
                            dve.wait_ge(s["ex"].sem, s["ex"].at(g, h + 1))
                            dve.wait_ge(s["esink"].sem, s["esink"].at(g, h + 1))
                            V.tensor_tensor(sm[:, 12:14], sm[:, 8:10], sm[:, 10:12], ALU.add).then_inc(s["den"].sem, 1)
                            dve.wait_ge(s["den"].sem, s["den"].at(g, h + 1))
                            V.reciprocal(sm[:, 14:16], sm[:, 12:14]).then_inc(s["rden"].sem, 1)
                            dve.wait_ge(s["rden"].sem, s["rden"].at(g, h + 1))
                            for qb in range(2):
                                x = V.tensor_scalar(prb[:, h % 2, qb, :], prb[:, h % 2, qb, :], sm[:, 14 + qb:15 + qb], None, ALU.mult)
                            x.then_inc(s["prn"].sem, 1)
            with dve.Fori(0, 4, 1) as i:
                for j in range(4):
                    u = U_GA + j
                    dve.wait_ge(d_evac.sem, d_evac.n(4 * i + u + 1))
                    dve.wait_ge(s["o_ev"].sem, s["o_ev"].n(16))
                    m = mrg[:, bass.ds(j + 4 * i, 1), :].rearrange("p a t -> p (a t)")
                    V.scalar_tensor_tensor(m, tokA[:, j % 2, :], 1.0, m, ALU.add, ALU.mult).then_inc(s["ga_m"].sem, 1)
                    cut_lo(u + 2, 4 * i + u + 2)
            dve.wait_ge(s["ga_m"].sem, s["ga_m"].n(16))
            V.memset(raw4[:], 0.0).then_inc(s["zr"].sem, 1)
            V.memset(lact[:], 0.0).then_inc(s["zr"].sem, 1)
            for d in range(2):
                V.memset(G[d][:], 0.0).then_inc(s["zr"].sem, 1)
            V.memset(zero[:], 0.0).then_inc(s["zr"].sem, 1)
            V.memset(Pd[0][:, :, 0:1], P0SCALE).then_inc(s["zr"].sem, 1)
            V.memset(Pd[1][:, :, P:P + 1], P0SCALE).then_inc(s["zr"].sem, 1)
            V.tensor_scalar(der[:, 0:64], pA[:, 48:112], 0.5, None, ALU.mult).then_inc(s["drv"].sem, 1)
            V.tensor_scalar(der[:, 64:80], pB[:, 16:32], 0.5, None, ALU.mult).then_inc(s["drv"].sem, 1)
            V.tensor_scalar(der[:, 80:96], pB[:, 16:32], -0.5, 1.0, ALU.mult, ALU.add).then_inc(s["drv"].sem, 1)
            dve.wait_ge(s["zr"].sem, s["zr"].n(7))
            dve.wait_ge(s["drv"].sem, s["drv"].n(3))
            for j in range(6):
                u = U_LO + j
                n = DL if j < 4 else P
                dst = lact[0:n, j, :] if j < 4 else gact[:, j - 4, :]
                dve.wait_ge(d_evac.sem, d_evac.n(u + 1))
                V.tensor_tensor(nb[0:n, 0, :], raw4[0:n, 0, 0:T], raw4[0:n, 0, 2:T + 2], ALU.add).then_inc(s["lo_nb"].sem, 1)
                dve.wait_ge(s["lo_nb"].sem, s["lo_nb"].n(j + 1))
                V.scalar_tensor_tensor(nb[0:n, 1, :], nb[0:n, 0, :], 0.5, raw4[0:n, 0, 1:T + 1], ALU.mult, ALU.subtract).then_inc(s["lo_df"].sem, 1)
                dve.wait_ge(s["lo_df"].sem, s["lo_df"].n(j + 1))
                V.scalar_tensor_tensor(dst, nb[0:n, 1, :], muL[0:n, j:j + 1], raw4[0:n, 0, 1:T + 1], ALU.mult, ALU.add).then_inc(s["lo_sh"].sem, 1)
                cut_lo(u + 2, u + 2)
            dve.wait_ge(s["lo_act"].sem, s["lo_act"].n(4))
            V.tensor_scalar(gact[:], gact[:], 0.5, 0.5, ALU.mult, ALU.add).then_inc(s["lo_fin"].sem, 1)

            def cut_pair(j, i, half=None):
                if i is not None:
                    cut_lo(U_RW + j + 2, 4 * i + U_RW + j + 2, half)

            blocks = lambda t: t.rearrange("p (a b) -> p a b", a=2)
            r, k, v = sh[:, 0, :], sh[:, 1, :], sh[:, 2, :]
            inc = lambda x, name: x.then_inc(s[name].sem, 1)

            class Prep:

                def __init__(self, n):
                    self.n = n
                    self.w = lambda name, k=None: dve.wait_ge(s[name].sem, s[name].at(n, k))
                    self.col = lambda t, c: t[:, bass.ds(c + n, 1)]

                def neighbours(self):
                    n, w = self.n, self.w
                    dve.wait_ge(d_evac.sem, d_evac.n(U_RW + 3 + 4 * n))
                    inc(V.tensor_tensor(nb[:], raw4[:, 0:3, 0:T], raw4[:, 0:3, 2:T + 2], ALU.add), "sh_nb")
                    w("sh_nb")
                    inc(V.scalar_tensor_tensor(nb[:], nb[:], 0.5, raw4[:, 0:3, 1:T + 1], ALU.mult, ALU.subtract), "sh_df")

                def shift(self):
                    w, col = self.w, self.col
                    w("sh_df")
                    for c in (1, 0, 2):
                        x = V.scalar_tensor_tensor(sh[:, c, :], nb[:, c, :], col(pA, 16 * c), raw4[:, c, 1:T + 1], ALU.mult, ALU.add)
                    inc(x, "shifted")
                    w("shifted")
                    inc(V.tensor_scalar(kk[:], k, col(pB, 0), None, ALU.mult), "kkr")
                    w("kkr")
                    inc(V.tensor_tensor(sq, kk[:], kk[:], ALU.mult), "sqd")

                def keys(self):
                    w, col = self.w, self.col
                    V.tensor_scalar(kA[:], k, col(der, 64), None, ALU.mult)
                    inc(V.tensor_scalar(kB[:], k, col(der, 80), None, ALU.mult), "kAB")
                    inc(V.tensor_scalar(rk[:], r, col(pB, 32), None, ALU.mult), "rkd")
                    w("ss")
                    inc(V.tensor_scalar(st[:, 0:4], PB[7][:, 0:4], 1e-24, None, ALU.max), "ssm")

                def norm(self):
                    w = self.w
                    w("rs")
                    for tb in range(2):
                        x = V.tensor_copy(rep[:, tb, :].rearrange("p (h f) -> p h f", h=2),
                                          st[:, 4 + 2 * tb:6 + 2 * tb].unsqueeze(2).to_broadcast([P, 2, 64]))
                    inc(x, "rrep")

                def products(self, d):
                    w = self.w
                    w("decs", d + 1)
                    for tb in range(2):
                        src = dec[d][:, P * tb:P * tb + P]
                        if d == 0:
                            x = V.tensor_tensor_scan(Pd[0][:, tb, 1:P + 1], src, zero[:], P0SCALE, ALU.mult, ALU.add)
                        else:
                            x = V.tensor_tensor_scan(Pd[1][:, tb, 0:P][:, ::-1], src[:, ::-1], zero[:], P0SCALE, ALU.mult, ALU.add)
                    inc(x, "scan")

                def modified(self):
                    w = self.w
                    w("rbc")
                    inc(V.scalar_tensor_tensor(kk[:], kk[:], -1.0, PB[7][:, 0:T], ALU.mult, ALU.mult), "nkk")
                    w("tas")
                    w("kAB")
                    for d in range(2):
                        inc(V.tensor_tensor(km[d][:], kA[:], ta[d][:], ALU.mult), "km1")
                    w("nkk")
                    for d in range(2):
                        w("km1", d + 1)
                        inc(V.tensor_tensor(km[d][:], km[d][:], kB[:], ALU.add), "km2")
                        inc(V.scalar_tensor_tensor(ta[d][:], ta[d][:], 1.0, kk[:], ALU.add, ALU.mult), "tt")

                def hats(self, d):
                    w = self.w
                    incl = Pd[d][:, :, 1:P + 1] if d == 0 else Pd[d][:, :, 0:P]
                    excl = Pd[d][:, :, 0:P] if d == 0 else Pd[d][:, :, 1:P + 1]
                    w("scan", d + 1)
                    inc(V.reciprocal(blocks(dec[d][:]), incl), "inv")
                    V.tensor_tensor(blocks(AR[d][:, 0, :]), blocks(kk[:]), excl, ALU.mult)
                    inc(V.tensor_tensor(blocks(AR[d][:, 1, :]), blocks(r), incl, ALU.mult), "ar")
                    w("tt", d + 1)
                    w("inv", d + 1)
                    inc(V.scalar_tensor_tensor(bh[d][:], ta[d][:], -0.5, dec[d][:], ALU.mult, ALU.mult), "bhs")
                    w("km2", d + 1)
                    w("kbs")
                    inc(V.tensor_tensor(kh[d][:], km[d][:], dec[d][:], ALU.mult), "khs")

            class Gram:

                def __init__(self, n):
                    self.n = n
                    self.w = lambda name, k=None: dve.wait_ge(s[name].sem, s[name].at(n, k))

                def keep(self, m):
                    d, q = m // 4, m % 4
                    self.w("gram", m + 1)
                    V.memset(cells[0:1, m:m + 1], 0.0)
                    mask = cst[:, C_GM + 256 * d:C_GM + 256 * d + 256].bitcast(i32).unsqueeze(1).to_broadcast([P, 2, 256])
                    inc(V.copy_predicated(G[d][:, q, :, :].rearrange("p (a b) c -> p a (b c)", a=2), mask,
                                          PB[3 - q % 2][:, :].rearrange("p (a b) -> p a b", a=2)), "gmask")

                def lasts(self):
                    V.tensor_copy(pl[:, 0:1], Pd[0][:, 0, P:P + 1])
                    inc(V.tensor_copy(pl[:, 1:2], Pd[1][:, 1, 0:1]), "plc")

                def bonus(self):
                    dve.wait_ge(s["y3"].sem, s["y3"].before(self.n))
                    self.w("bonm")
                    inc(V.tensor_tensor(bon[:], PB[6][:, 0:T], v, ALU.mult), "bonv")

            class Tail:

                def __init__(self, i):
                    self.i = i
                    self.w = lambda name, k=None: dve.wait_ge(s[name].sem, s[name].at(i, k))
                    self.col = lambda t, c: t[:, bass.ds(c + i, 1)]

                def centre(self):
                    self.w("ye")
                    self.w("mean")
                    inc(V.tensor_tensor(yc[:], ysb[:], PB[7][:, 0:T], ALU.subtract), "ycs")

                def variance(self):
                    self.w("var")
                    inc(V.tensor_scalar(st[:, 0:4], PB[7][:, 0:4], 1.0 / 64, GN_EPS, ALU.mult, ALU.add), "vars")

                def spread(self):
                    self.w("vpow")
                    for tb in range(2):
                        x = V.tensor_copy(rep[:, tb, :].rearrange("p (h f) -> p h f", h=2),
                                          st[:, 4 + 2 * tb:6 + 2 * tb].unsqueeze(2).to_broadcast([P, 2, 64]))
                    inc(x, "vrep")

                def scale(self):
                    w, col = self.w, self.col
                    w("vbc")
                    inc(V.tensor_tensor(yc[:], yc[:], PB[7][:, 0:T], ALU.mult), "y1")
                    w("y1")
                    inc(V.tensor_scalar(yc[:], yc[:], col(pB, 48), col(pB, 64), ALU.mult, ALU.add), "y2")
                    w("y2")
                    w("bonv")
                    inc(V.tensor_tensor(yc[:], yc[:], bon[:], ALU.add), "y3")

                def gate(self):
                    i, w = self.i, self.w
                    w("y3")
                    w("gups")
                    inc(V.tensor_tensor(yc[:], yc[:], gup[:], ALU.mult), "y4")
                    w("y4", 1)
                    w("gate_t")
                    m = mrg[:, bass.ds(i, 1), :].rearrange("p a t -> p (a t)") if not isinstance(i, int) else mrg[:, i, :]
                    inc(V.scalar_tensor_tensor(ysb[:], gt[:], 1.0, yc[:], ALU.add, ALU.mult), "y4")
                    w("y4", 2)
                    inc(V.tensor_tensor(m, m, ysb[:], ALU.add), "y5")

            def pair(i, n, d1, d2):
                w = lambda name, k=None: dve.wait_ge(s[name].sem, s[name].at(i, k))
                nx = Prep(n) if n is not None else None
                for d in range(2):
                    w("d0p", d + 1)
                    inc(V.tensor_copy(Dm[d][:].rearrange("p a b -> p (a b)"), PB[5 + d][:, :]), "d0")
                    if d == 0:
                        cut_pair(1, d1, 0)
                for l in range(1, LV):
                    m = 1 << l
                    part = lambda t, par: t[:].rearrange("p g (n two m) -> p (g n) two m", two=2, m=m)[:, :, par, :]
                    small_ = lambda bank: bank[:, 0:T].rearrange("p (n m) -> p n m", m=m)
                    for d in range(2):
                        nn = 2 * (l - 1) + d + 1
                        if l < LV - 1:
                            w("ddm", nn)
                            inc(V.tensor_tensor(part(Dm[d], d), part(Dm[d], d).bitcast(f32), small_(PB[5 if d == 0 else 2]), ALU.add), "dup")
                        w("dtm", nn)
                        inc(V.tensor_tensor(part(DT[d], 1 - d), part(DT[d], 1 - d).bitcast(f32), small_(PB[6 if d == 0 else 7]), ALU.add), "dtup")
                        if l == 1 and d == 0:
                            cut_pair(1, d1, 1)
                        if l in (4, 5) and d == 1 and d2 is not None:
                            cut_pair(2, d1, l - 4)
                for c in range(2):
                    if nx and c == 0:
                        nx.neighbours()
                    w("ue", c + 1)
                    w("resm", c + 1)
                    inc(V.tensor_tensor(rhs[:].rearrange("p a b -> p (a b)"), PB[4][:, 0:T],
                                        U[:, c, :, :].rearrange("p a b -> p (a b)"), ALU.subtract), "rese")
                    if nx:
                        if c == 0:
                            nx.shift()
                        else:
                            nx.modified()
                    w("dum", c + 1)
                    u2 = U[:, c, :, :].rearrange("p a b -> p (a b)")
                    inc(V.tensor_tensor(u2, PB[5][:, T:2 * T], u2, ALU.add), "due")
                    if c == 0:
                        if nx:
                            nx.keys()
                        w("smm")
                        for d in range(2):
                            x = V.scalar_tensor_tensor(Sm[:, d, :], PB[6][:, P * d:P * d + P], pl[:, d:d + 1], cst[:, C_SM:C_SM + P], ALU.mult, ALU.mult)
                        inc(x, "sme")
                        if nx:
                            nx.norm()
                        if d2 is not None:
                            cut_pair(3, d1, 0)
                        if nx:
                            nx.products(0)
                            nx.products(1)
                        if d2 is not None:
                            cut_pair(3, d1, 1)
                if nx:
                    nx.hats(0)
                tail = Tail(i)
                if nx is None:
                    tail.centre()
                    tail.variance()
                    tail.spread()
                    tail.scale()
                    tail.gate()
                    return
                gram = Gram(n)
                nx.hats(1)
                tail.centre()
                gram.keep(0)
                cut_pair(0, d2, 0)
                tail.variance()
                gram.lasts()
                gram.keep(1)
                gram.keep(2)
                tail.spread()
                gram.keep(3)
                cut_pair(0, d2, 1)
                gram.keep(4)
                tail.scale()
                gram.bonus()
                gram.keep(5)
                tail.gate()
                gram.keep(6)
                gram.keep(7)

            for j in range(4):
                cut_pair(j, 0)
            p0 = Prep(0)
            p0.neighbours()
            p0.shift()
            p0.keys()
            p0.norm()
            p0.products(0)
            p0.products(1)
            p0.modified()
            p0.hats(0)
            p0.hats(1)
            g0 = Gram(0)
            g0.lasts()
            for m in range(8):
                g0.keep(m)
                if m == 3:
                    g0.bonus()
            cut_pair(0, 1)
            with dve.Fori(0, PAIRS - 2, 1) as i:
                pair(i, i + 1, i + 1, i + 2)
            pair(PAIRS - 2, PAIRS - 1, PAIRS - 1, None)
            pair(PAIRS - 1, None, None, None)

            dve.wait_ge(s["y5"].sem, s["y5"].n(16))
            for k in range(KT):
                dve.wait_ge(s["mg_hi"].sem, s["mg_hi"].n(k + 1))
                V.tensor_tensor(xT[:, k, 1, :], mrg[:, k, :], xT[:, k, 0, :].bitcast(f32), ALU.subtract).then_inc(s["mg_lo"].sem, 1)
            cut_lo(U_OUT, U_OUT)
            cut_lo(U_OUT + 1, U_OUT + 1)
            with dve.Fori(0, 2, 1) as i:
                for j in range(8):
                    cut_lo(U_OUT + j + 2, 8 * i + U_OUT + j + 2)

            rstd(16, 1, 4 * EPS)
            dve.wait_ge(s["ld_h"].sem, s["ld_h"].n(16))
            dve.wait_ge(s["ld_g"].sem, s["ld_g"].n(16))
            for b in range(2):
                V.scalar_tensor_tensor(acc[:, b, :], acc[:, b, :], small[:, 28 + b:29 + b], gain[:], ALU.mult, ALU.mult).then_inc(s["m_n"].sem, 1)
                dve.wait_ge(s["m_n"].sem, s["m_n"].n(b + 1))
                V.tensor_tensor(hres[:, b, :], hres[:, b, :], acc[:, b, :], ALU.add).then_inc(s["m_h"].sem, 1)
            rstd(32, 2)
            for b in range(2):
                V.tensor_scalar(acc[:, b, :], hres[:, b, :], small[:, 44 + b:45 + b], None, ALU.mult).then_inc(s["h_n"].sem, 1)
            for k in range(KT):
                dve.wait_ge(s["h_tp"].sem, s["h_tp"].n(k // 2 + 1))
                if k >= 2:
                    dve.wait_ge(s["h_lo"].sem, s["h_lo"].n(k - 1))
                V.tensor_scalar(hf[:, k % 2, :], PB[4 + (k // 2) % 2][:, T * (k % 2):T * (k % 2) + T], pB[:, 96 + k:97 + k], None,
                                ALU.mult).then_inc(s["h_g"].sem, 1)
                dve.wait_ge(s["h_hi"].sem, s["h_hi"].n(k + 1))
                V.tensor_tensor(xT[:, k, 1, :], hf[:, k % 2, :], xT[:, k, 0, :].bitcast(f32), ALU.subtract).then_inc(s["h_lo"].sem, 1)
            dve.wait_ge(s["h_tp"].sem, s["h_tp"].n(8))
            V.memset(acc[:], 0.0).then_inc(s["acc0"].sem, 1)
            dve.wait_ge(s["acc0"].sem, s["acc0"].n(1))

            def chunk(i, last):
                for j in range(16):
                    u = U_FF + j
                    if not (last and j >= 14):
                        cut_lo(u + 2, 16 * i + u + 2)
                    if j < 8:
                        dve.wait_ge(s["up_re"].sem, s["up_re"].at(i, j + 1))
                        V.tensor_tensor(fs[:, j % 2, :], fa[:, j % 2, :], fa[:, j % 2, :], ALU.mult).then_inc(s["up_sq"].sem, 1)
                        dve.wait_ge(s["up_sq"].sem, s["up_sq"].at(i, j + 1))
                        dve.wait_ge(s["up_hi"].sem, s["up_hi"].at(i, j + 1))
                        V.tensor_tensor(ft[:, j, 1, :], fs[:, j % 2, :], ft[:, j, 0, :].bitcast(f32), ALU.subtract).then_inc(s["up_lo"].sem, 1)
                    elif j % 2 == 1:
                        n = (j - 9) // 2
                        dve.wait_ge(s["dn"].sem, s["dn"].at(i, n + 1))
                        for b in range(2):
                            x = V.tensor_tensor(acc[:, b, 512 * n:512 * n + 512], acc[:, b, 512 * n:512 * n + 512], PB[2 + 2 * (n % 3) + b][:, :], ALU.add)
                        x.then_inc(s["dn_acc"].sem, 1)

            with dve.Fori(0, FCH - 1, 1) as i:
                chunk(i, False)
            chunk(FCH - 1, True)
            rstd(48, 3)
            dve.wait_ge(s["ld_g2"].sem, s["ld_g2"].n(16))
            for b in range(2):
                V.scalar_tensor_tensor(acc[:, b, :], acc[:, b, :], small[:, 60 + b:61 + b], gain[:], ALU.mult, ALU.mult).then_inc(s["f_n"].sem, 1)
                dve.wait_ge(s["f_n"].sem, s["f_n"].n(b + 1))
                V.tensor_tensor(acc[:, b, :], hres[:, b, :], acc[:, b, :], ALU.add).then_inc(s["f_o"].sem, 1)

        @block.gpsimd
        def _(pool):
            Gp = nc.gpsimd

            def power(norm, col):
                pool.wait_ge(s["n_st"].sem, s["n_st"].at(norm))
                Gp.tensor_tensor(small[:, col + 12:col + 14], small[:, col + 10:col + 12], epsh[:, 0:2], ALU.pow).then_inc(s["n_pow"].sem, 1)

            pool.wait_ge(s["exp_ms"].sem, s["exp_ms"].n(1))
            power(0, 0)
            pool.wait_ge(s["ld_c"].sem, s["ld_c"].n(48))

            def prep(n):
                w = lambda name, k=None: pool.wait_ge(s[name].sem, s[name].at(n, k))
                w("ssm")
                Gp.tensor_tensor(st[:, 4:8], st[:, 0:4], epsh[:, 0:4], ALU.pow).then_inc(s["rs"].sem, 1)
                w("km2", 2)
                w("ss")
                Gp.tensor_tensor(nb[:, 1, :], km[0][:], km[1][:], ALU.add).then_inc(s["kbs"].sem, 1)
                w("kbs")
                w("rkd")
                Gp.tensor_tensor(rk[:], rk[:], nb[:, 1, :], ALU.mult).then_inc(s["t2"].sem, 1)

            def pair(i, n):
                w = lambda name, k=None: pool.wait_ge(s[name].sem, s[name].at(i, k))
                lm = lambda d, l: lmk[:, d, l, :].unsqueeze(1).to_broadcast([P, 4, P])
                for d in range(2):
                    w("gmask", 4 * d + 4)
                    pool.wait_ge(s["dum"].sem, s["dum"].before(i))
                    Gp.tensor_tensor(DT[d][:], G[d][:, :, 0, :], lm(d, 0), ALU.mult).then_inc(s["e0"].sem, 1)
                    w("e0", d + 1)
                    Gp.tensor_tensor(DT[d][:], DT[d][:].bitcast(f32), ident.unsqueeze(1).to_broadcast([P, 4, P]), ALU.add).then_inc(s["dt0"].sem, 1)
                    Gp.tensor_tensor(CT[d][:], G[d][:, :, 0, :], lm(d, 1), ALU.mult).then_inc(s["ctm"].sem, 1)
                for l in range(2, LV):
                    for d in range(2):
                        w("wmm", 2 * (l - 2) + d + 1)
                        Gp.tensor_tensor(CT[d][:], G[d][:, :, 0, :], lm(d, l), ALU.mult).then_inc(s["ctm"].sem, 1)
                    if l == 2:
                        pool.wait_ge(s["ym"].sem, s["ym"].before(i))
                        for d in range(2):
                            x = Gp.tensor_tensor(AS[:, d, :, :], AR[d][:, :, P * (1 - d):P * (1 - d) + P],
                                                 zero[:].unsqueeze(1).to_broadcast([P, 2, P]), ALU.add)
                        x.then_inc(s["asc"].sem, 1)
                if n is not None:
                    prep(n)
                w("vars")
                Gp.tensor_tensor(st[:, 4:8], st[:, 0:4], epsh[:, 0:4], ALU.pow).then_inc(s["vpow"].sem, 1)

            prep(0)
            with pool.Fori(0, PAIRS - 1, 1) as i:
                pair(i, i + 1)
            pair(PAIRS - 1, None)
            for norm in (1, 2, 3):
                power(norm, 16 * norm)

        @block.tensor
        def _(pe):
            M = nc.tensor.matmul

            def unit_b(u_static, u, k0=0, k1=KT):
                if k0 == 0:
                    pe.wait_ge(w_lo.sem, w_lo.n(u + 1))
                bank = PB[u_static % 2]
                hi, lo = whi[:, u_static % 2, :], wlo[:, u_static % 2, :]
                for k in range(k0, k1):
                    h, l = hi[:, P * k:P * k + P], lo[:, P * k:P * k + P]
                    M(bank[:, 0:T], h, xT[:, k, 0, :], start=k == 0, stop=False)
                    M(bank[:, 0:T], h, xT[:, k, 1, :], start=False, stop=False)
                    x = M(bank[:, 0:T], l, xT[:, k, 0, :], start=False, stop=k == KT - 1)
                if k1 == KT:
                    x.then_inc(w_used.sem, 1)

            def unit_a(u_static, u, act_tiles, banks, first, last, done=None):
                pe.wait_ge(w_lo.sem, w_lo.n(u + 1))
                hi, lo = whi[:, u_static % 2, :], wlo[:, u_static % 2, :]
                for k in range(4):
                    t = act_tiles[k]
                    for b in range(2):
                        ah, al = t[:, 0, P * b:P * b + P], t[:, 1, P * b:P * b + P]
                        wh, wl = hi[:, 512 * k:512 * k + 512], lo[:, 512 * k:512 * k + 512]
                        f, e = first and k == 0, last and k == 3
                        M(banks[b][:, :], ah, wh, start=f, stop=False)
                        M(banks[b][:, :], ah, wl, start=False, stop=False)
                        x = M(banks[b][:, :], al, wh, start=False, stop=e)
                x.then_inc(w_used.sem, 1)
                return x

            pe.wait_ge(s["ld_c"].sem, s["ld_c"].n(48))
            pe.wait_ge(s["ld_p"].sem, s["ld_p"].n(16 * (len(PARAMS_A) + len(PARAMS_B) + 3)))
            for q in range(3):
                nc.tensor.transpose(PB[7][:, P * q:P * q + P], prow[:, q, :], ident).then_inc(s["prm_tp"].sem, 1)

            def token_tiles(src, banks, ready, free, done):
                for k2 in range(KT // 2):
                    if k2 == 0:
                        pe.wait_ge(s[ready].sem, 2)
                    if k2 >= 2:
                        pe.wait_ge(s[free].sem, 2 * (k2 - 1))
                    for kk_ in range(2):
                        for b in range(2):
                            k = 2 * k2 + kk_
                            x = nc.tensor.transpose(banks[k2 % 2][:, T * kk_ + P * b:T * kk_ + P * b + P], src[:, b, P * k:P * k + P], ident)
                    x.then_inc(s[done].sem, 1)

            token_tiles(xtok, PB[0:2], "x_n", "x_gain", "x_tp")
            pe.wait_ge(s["x_lo"].sem, s["x_lo"].n(KT))

            with pe.Fori(0, KVH // 2, 1) as i:
                for gg in range(2):
                    g = 2 * i + gg
                    for j in range(8):
                        u = 6 * gg + j
                        if j < 6:
                            pe.wait_ge(d_evac.sem, d_evac.n(12 * i + u - 1 if u >= 2 else 12 * i))
                            unit_b(u, 12 * i + u)
                        if j == 1:
                            pe.wait_ge(d_evac.sem, d_evac.n(12 * i + u + 1))
                            for tb in range(2):
                                x = nc.tensor.transpose(PB[2][:, P * tb:P * tb + P], vf[:, P * tb:P * tb + P], ident)
                            x.then_inc(s["v_tp"].sem, 1)
                        h = j - 3
                        if 0 <= h < 4:
                            pe.wait_ge(s["k_r"].sem, s["k_r"].at(g))
                            pe.wait_ge(s["q_r"].sem, s["q_r"].at(g, h + 1))
                            if h >= 2:
                                pe.wait_ge(s["sc_m"].sem, s["sc_m"].at(g, h - 1))
                            else:
                                pe.wait_ge(s["sc_m"].sem, s["sc_m"].before(g))
                            for qb in range(2):
                                x = M(PB[3 + h % 2][:, T * qb:T * qb + T], qr[:, h % 2, P * qb:P * qb + P], kr[:], start=True, stop=True)
                            x.then_inc(s["sc"].sem, 1)
                        h = j - 4
                        if 0 <= h < 4:
                            pe.wait_ge(s["prn"].sem, s["prn"].at(g, h + 1))
                            pe.wait_ge(s["p_T"].sem, s["p_T"].at(g, h) if h else s["p_T"].before(g))
                            for sbk in range(2):
                                for qb in range(2):
                                    x = nc.tensor.transpose(PB[5][:, T * sbk + P * qb:T * sbk + P * qb + P], prb[:, h % 2, qb, P * sbk:P * sbk + P], ident)
                            x.then_inc(s["p_tp"].sem, 1)
                            pe.wait_ge(s["p_T"].sem, s["p_T"].at(g, h + 1))
                            pe.wait_ge(s["v_tok"].sem, s["v_tok"].at(g))
                            pe.wait_ge(s["o_ev"].sem, s["o_ev"].at(g, h) if h else s["o_ev"].before(g))
                            for sbk in range(2):
                                x = M(PB[6][:, 0:T], vtok[:, sbk, :], prT[:, sbk, :], start=sbk == 0, stop=sbk == 1)
                            x.then_inc(s["pv"].sem, 1)
            with pe.Fori(0, 4, 1) as i:
                for j in range(4):
                    pe.wait_ge(d_evac.sem, d_evac.n(4 * i + U_GA + j - 1))
                    unit_b(U_GA + j, 4 * i + U_GA + j)
            for j in range(6):
                pe.wait_ge(d_evac.sem, d_evac.n(U_LO + j - 1))
                unit_b(U_LO + j, U_LO + j)

            def dense(j, n, k0=0, k1=KT):
                if n is None:
                    return
                if k0 == 0:
                    pe.wait_ge(d_evac.sem, d_evac.n(4 * n + U_RW + j - 1))
                unit_b(U_RW + j, 4 * n + U_RW + j, k0, k1)

            inc = lambda x, name: x.then_inc(s[name].sem, 1)

            class Prep:

                def __init__(self, n):
                    self.n = n
                    self.w = lambda name, k=None: pe.wait_ge(s[name].sem, s[name].at(n, k))

                def lora_w(self):
                    n = self.n
                    pe.wait_ge(s["up_ld"].sem, s["up_ld"].n(16 * 5 * n + 80))
                    for q in range(2):
                        x = M(PB[2][:, T * q:T * q + T], upw[0:DL, q, :], lact[0:DL, q, :], start=True, stop=True)
                    inc(x, "lw")

                def lora_a(self):
                    for q in range(2):
                        x = M(PB[3][:, T * q:T * q + T], upw[0:DL, 2 + q, :], lact[0:DL, 2 + q, :], start=True, stop=True)
                    inc(x, "la")

                def squares(self):
                    self.w("sqd")
                    for tb in range(2):
                        x = M(PB[7][:, 2 * tb:2 * tb + 2], sq[:, P * tb:P * tb + P], hsel, start=True, stop=True)
                    inc(x, "ss")

                def norms(self):
                    self.w("rrep")
                    for tb in range(2):
                        x = M(PB[7][:, P * tb:P * tb + P], rep[:, tb, :], ident, start=True, stop=True)
                    inc(x, "rbc")

            class Gram:

                def __init__(self, n):
                    self.n = n
                    self.w = lambda name, k=None: pe.wait_ge(s[name].sem, s[name].at(n, k))

                def values(self):
                    pe.wait_ge(s["due"].sem, s["due"].before(self.n))
                    self.w("shifted")
                    for tb in range(2):
                        x = nc.tensor.transpose(PB[5][:, P * tb:P * tb + P], sh[:, 2, P * tb:P * tb + P], ident)
                    inc(x, "vtp")

                def gate(self):
                    pe.wait_ge(s["rese"].sem, s["rese"].before(self.n))
                    for q in range(2):
                        x = M(PB[4][:, 0:T], upg[:, q, :], gact[:, q, :], start=q == 0, stop=q == 1)
                    inc(x, "lg")

                def gram(self, m):
                    w = self.w
                    d, q = m // 4, m % 4
                    tb, h = q // 2, q % 2
                    if q == 0:
                        w("khs", d + 1)
                        w("bhs", d + 1)
                        w("ar", d + 1)
                    if m >= 2:
                        w("gmask", m - 1)
                    elif m == 0:
                        w("tas")
                    else:
                        w("tws")
                        pe.wait_ge(s["ye"].sem, s["ye"].before(self.n))
                    hp, ts = slice(64 * h, 64 * h + 64), slice(P * tb, P * tb + P)
                    for a, src in enumerate((bh[d], kh[d])):
                        x = M(PB[3 - q % 2][:, T * a:T * a + T], src[hp, ts], AR[d][hp, :, ts], start=True, stop=True)
                    inc(x, "gram")

                def bonus(self):
                    self.w("t2")
                    pe.wait_ge(s["sme"].sem, s["sme"].before(self.n))
                    x = M(PB[6][:, 0:T], ones_half, rk[:], start=True, stop=True)
                    inc(x, "bonm")

            def pair(i, n, d1, d2):
                w = lambda name, k=None: pe.wait_ge(s[name].sem, s[name].at(i, k))
                nx = Prep(n) if n is not None else None
                at = [0]

                def filler(count):
                    k = at[0]
                    at[0] = k + count
                    if k < KT:
                        dense(2, d1, k, min(k + count, KT))
                    if k + count > KT:
                        dense(3, d1, max(k - KT, 0), k + count - KT)

                filler(3)
                for d in range(2):
                    w("dt0", d + 1)
                    if d == 0:
                        w("vts")
                    else:
                        w("bonv")
                    for q in range(4):
                        x = nc.tensor.transpose(PB[5 + d][:, P * q:P * q + P], DT[d][:, q, :].bitcast(f32), ident)
                    inc(x, "d0p")
                    filler(4 if d == 0 else 2)

                def blocks_w(l, d):
                    nn = 2 * (l - 1) + d + 1
                    w("ctm", nn)
                    if l == 1:
                        w("d0", d + 1)
                        if d == 0:
                            w("gups")
                            w("gmask", 8)
                    else:
                        w("dup", nn - 2)
                        w("wev", nn - 2)
                    for q in range(4):
                        x = M(PB[4 - d][:, P * q:P * q + P], CT[d][:, q, :], Dm[d][:, q, :], start=True, stop=True)
                    inc(x, "wmm")

                def blocks_d(l, d):
                    m = 1 << l
                    part = lambda t, q, par: t[:, q, :].rearrange("p (n two m) -> p n two m", two=2, m=m)[:, :, par, :]
                    nn = 2 * (l - 1) + d + 1
                    w("wev", nn)
                    if l == 1:
                        w("d0", 2)
                        if d == 1:
                            pe.wait_ge(s["y1"].sem, s["y1"].before(i))
                    else:
                        w("dtup", nn - 2)
                    bd, bt = (PB[5], PB[6]) if d == 0 else (PB[2], PB[7])
                    if l < LV - 1:
                        for q in range(4):
                            x = M(bd[:, 64 * q:64 * q + 64].rearrange("p (n m) -> p n m", m=m), DT[d][:, q, :], part(W[d], q, d), start=True, stop=True)
                        inc(x, "ddm")
                    for q in range(4):
                        x = M(bt[:, 64 * q:64 * q + 64].rearrange("p (n m) -> p n m", m=m), W[d][:, q, :], part(DT[d], q, 1 - d), start=True, stop=True)
                    inc(x, "dtm")

                for l in range(1, LV):
                    blocks_w(l, 0)
                    if l > 1:
                        blocks_d(l - 1, 1)
                    filler(1 if l == LV - 1 else 2)
                    blocks_d(l, 0)
                    blocks_w(l, 1)
                    filler(2)
                blocks_d(LV - 1, 1)
                w("wev")
                for d in range(2):
                    ts = slice(P * d, P * d + P)
                    for a, src in enumerate((kh[d], bh[d])):
                        x = nc.tensor.transpose(PB[3][:, P * (2 * d + a):P * (2 * d + a) + P], src[:, ts], ident)
                inc(x, "kbtp")
                w("dup")
                w("asc")
                if nx:
                    nx.lora_w()
                for c in range(2):
                    if c == 1:
                        w("rese", 1)
                        w("due", 1)
                        w("sme")
                    first = True
                    for d in range(2):
                        tb = c if d == 0 else 1 - c
                        if c == 1:
                            M(PB[4][:, P * d:P * d + P], AS[:, d, 0, :], Sm[:, d, :], start=first, stop=False, skip_group_check=True)
                            first = False
                        for h in range(2):
                            q, o = 2 * tb + h, slice(64 * (2 * d + h), 64 * (2 * d + h) + 64)
                            x = M(PB[4][:, o], G[d][:, q, 2, :], Vt[:, tb, 64 * h:64 * h + 64], start=first, stop=False, skip_group_check=True)
                            first = False
                    inc(x, "rhsm")
                    dense(c, d2, 0, 3)
                    w("rhsc", c + 1)
                    if c == 0:
                        w("dtup")
                    for d in range(2):
                        tb = c if d == 0 else 1 - c
                        for h in range(2):
                            q, e = 2 * tb + h, 2 * d + h
                            x = M(PB[5][:, 64 * e:64 * e + 64], DT[d][:, q, :], rhs[:, e, :], start=True, stop=True)
                    inc(x, "um")
                    dense(c, d2, 3, 6)
                    w("ue", c + 1)
                    for d in range(2):
                        tb = c if d == 0 else 1 - c
                        for h in range(2):
                            q, e = 2 * tb + h, 2 * d + h
                            x = M(PB[4][:, 64 * e:64 * e + 64], G[d][:, q, 0, :], U[:, c, e, :], start=False, stop=True, skip_group_check=True)
                    inc(x, "resm")
                    if nx and c == 0:
                        w("kbs2")
                        nx.lora_a()
                    dense(c, d2, 6, 9)
                    w("rese", c + 1)
                    for d in range(2):
                        tb = c if d == 0 else 1 - c
                        for h in range(2):
                            q, e = 2 * tb + h, 2 * d + h
                            x = M(PB[5][:, T + 64 * e:T + 64 * e + 64], DT[d][:, q, :], rhs[:, e, :], start=True, stop=True)
                    inc(x, "dum")
                    if c == 0:
                        dense(c, d2, 9, 12)
                        if nx:
                            nx.squares()
                        w("due", c + 1)
                        w("kbs2")
                        for d in range(2):
                            o = PB[6][:, P * d:P * d + P]
                            M(o, KB[:, 2 * d, :], Vt[:, d, :], start=True, stop=False)
                            x = M(o, KB[:, 2 * d + 1, :], U[:, 0, 2 * d:2 * d + 2, :].rearrange("p a b -> p (a b)"), start=False, stop=True)
                        inc(x, "smm")
                        dense(c, d2, 12, KT)
                        if nx:
                            nx.norms()
                    else:
                        dense(c, d2, 9, 11)
                        w("due", 2)
                gram = Gram(n) if n is not None else None
                if gram:
                    gram.values()
                    nx.w("tws")
                for tb in range(2):
                    ts = slice(P * tb, P * tb + P)
                    d2nd = 1 if tb == 0 else 0
                    M(PB[2][:, ts], Sm[:, d2nd, :], AS[:, d2nd, 1, :], start=True, stop=False, skip_group_check=True)
                    for h in range(2):
                        hp, q = slice(64 * h, 64 * h + 64), 2 * tb + h
                        for d in range(2):
                            c = tb if d == 0 else 1 - tb
                            M(PB[2][hp, ts], Vt[:, tb, hp], G[d][:, q, 3, :], start=False, stop=False, skip_group_check=True)
                            x = M(PB[2][hp, ts], U[:, c, 2 * d + h, :], G[d][:, q, 1, :], start=False, stop=d == 1, skip_group_check=True)
                inc(x, "ym")
                if gram:
                    gram.gate()
                    gram.gram(0)
                    nx.w("nkk")
                w("ye")
                x = M(PB[7][:, 0:T], ones_mean, ysb[:], start=True, stop=True)
                inc(x, "mean")
                if gram:
                    gram.gram(1)
                    dense(1, d2, 11, 13)
                    gram.gram(2)
                w("ysqs")
                for tb in range(2):
                    x = M(PB[7][:, 2 * tb:2 * tb + 2], ysq[:, P * tb:P * tb + P], hsel, start=True, stop=True)
                inc(x, "var")
                if gram:
                    gram.gram(3)
                    dense(1, d2, 13, KT)
                    gram.gram(4)
                    gram.bonus()
                w("vrep")
                for tb in range(2):
                    x = M(PB[7][:, P * tb:P * tb + P], rep[:, tb, :], ident, start=True, stop=True)
                inc(x, "vbc")
                if gram:
                    for m in range(5, 8):
                        gram.gram(m)

            for j in range(4):
                dense(j, 0)
            pe.wait_ge(s["lo_fin"].sem, s["lo_fin"].n(1))
            pe.wait_ge(s["lo_sh"].sem, s["lo_sh"].n(6))
            p0 = Prep(0)
            p0.lora_w()
            p0.lora_a()
            p0.squares()
            p0.norms()
            g0 = Gram(0)
            g0.values()
            g0.gate()
            for m in range(8):
                g0.gram(m)
                if m == 3:
                    g0.bonus()
            for j in range(2):
                dense(j, 1)
            with pe.Fori(0, PAIRS - 2, 1) as i:
                pair(i, i + 1, i + 1, i + 2)
            pair(PAIRS - 2, PAIRS - 1, PAIRS - 1, None)
            pair(PAIRS - 1, None, None, None)

            pe.wait_ge(s["mg_lo"].sem, s["mg_lo"].n(16))
            with pe.Fori(0, 2, 1) as i:
                for j in range(8):
                    n, kc = j // 4, j % 4
                    if kc == 0:
                        pe.wait_ge(s["o_cp"].sem, s["o_cp"].n(2 * i))
                    x = unit_a(U_OUT + j, 8 * i + U_OUT + j, [xT[:, 4 * kc + k, :, :] for k in range(4)], PB[2 * n:2 * n + 2], kc == 0, kc == 3)
                    if kc == 3:
                        pe.wait_ge(w_used.sem, w_used.n(8 * i + U_OUT + j + 1))
                        pe.sem_inc(s["om"].sem, 1)
            token_tiles(acc, PB[4:6], "h_n", "h_g", "h_tp")
            pe.wait_ge(s["h_lo"].sem, s["h_lo"].n(KT))
            with pe.Fori(0, FCH, 1) as i:
                for j in range(8):
                    pe.wait_ge(s["up_re"].sem, s["up_re"].at(i, j - 1) if j >= 2 else s["up_re"].before(i))
                    if j < 2:
                        pe.wait_ge(s["o_cp"].sem, s["o_cp"].n(4))
                    unit_b(U_FF + j, 16 * i + U_FF + j)
                for j in range(8):
                    n, kc = j // 2, j % 2
                    pe.wait_ge(s["up_lo"].sem, s["up_lo"].at(i, 4 * kc + 4))
                    if kc == 0:
                        pe.wait_ge(s["dn_acc"].sem, s["dn_acc"].at(i, n - 2) if n >= 3 else s["dn_acc"].before(i))
                    x = unit_a(U_FF + 8 + j, 16 * i + U_FF + 8 + j, [ft[:, 4 * kc + k, :, :] for k in range(4)],
                               PB[2 + 2 * (n % 3):4 + 2 * (n % 3)], kc == 0, kc == 1)
                    if kc == 1:
                        pe.wait_ge(w_used.sem, w_used.n(16 * i + U_FF + 8 + j + 1))
                        pe.sem_inc(s["dn"].sem, 1)


INS = ["x", "norm_pre_mix", "w_in", "mu_shift", "attn_sink", "w0_fwd", "w_up_fwd", "w0_bwd", "w_up_bwd", "a0_fwd", "a_up_fwd",
       "a0_bwd", "a_up_bwd", "g_up", "k_k", "k_a", "r_k", "ln_x_gain", "ln_x_bias", "w_out", "norm_post_mix", "norm_pre_ffn",
       "w_ffn_up", "w_ffn_down", "norm_post_ffn"]


def kernel(**inputs):
    import numpy as _np
    import concourse.bacc as _bacc
    from concourse import mybir as _mybir
    from concourse.bass_utils import run_bass_kernel_spmd as _run

    nc = _bacc.Bacc("TRN2", target_bir_lowering=False, num_devices=1)
    arrays, aps = {}, {}
    c, a, lm = constants()
    for name, arr in [(n, _np.ascontiguousarray(inputs[n])) for n in INS] + [("constants", c), ("attn_constants", a), ("level_masks", lm)]:
        arrays[f"in_{name}"] = arr
        aps[name] = nc.dram_tensor(f"in_{name}", arr.shape, _mybir.dt.from_np(arr.dtype), kind="ExternalInput").ap()
    out = nc.dram_tensor("out", (1, T, D), _mybir.dt.float32, kind="ExternalOutput").ap()
    block_kernel(nc, aps, aps["constants"], aps["attn_constants"], aps["level_masks"], out)
    r = _run(nc, [arrays], core_ids=[0])
    return r.results[0]["out"]
```

```python
from contextlib import ExitStack

import numpy as np

import concourse.bass as bass
from concourse import mybir

D = 2048
T = 256
P = 128
KT = D // P
HD = 128
KVH = 4
GRP = 4
PAIRS = D // P
DL = 96
GL = 256
FF = 4 * D
EPS = 1e-6
GN_EPS = 64e-5
DECAY_E = float(np.exp(-0.5))
P0SCALE = 2.0 ** 56
LV = 7

Q0, K0, V0 = 0, D, D + 512
SH0 = D + 1024
R0, RK0, RV0 = SH0, SH0 + D, SH0 + 2 * D
LO0 = SH0 + 3 * D
GA0 = LO0 + 4 * DL + GL
GR0 = GA0 + D

C_ID, C_GM, C_MEAN, C_HALF, C_SEL = 0, 128, 640, 768, 896
C_SM = C_SEL + 2
C_END = C_SM + P
CA_COS, CA_SIN, CA_MASK, CA_END = 0, 256, 512, 1024

PARAMS_A = ["mu_shift", "w0_fwd", "w0_bwd", "a0_fwd", "a0_bwd"]
PARAMS_B = ["k_k", "k_a", "r_k", "ln_x_gain", "ln_x_bias", "norm_pre_mix", "norm_pre_ffn"]


class Sig:

    def __init__(self, sem, per=1, base=0):
        self.sem, self.per, self.base = sem, per, base

    def n(self, count):
        return self.base + count

    def at(self, i, k=None):
        return self.base + self.per * i + (self.per if k is None else k)

    def before(self, i):
        return self.base + self.per * i


def constants():
    c = np.zeros((P, C_END), np.float32)
    s, t = np.arange(P)[:, None], np.arange(P)[None, :]
    c[:, C_ID:C_ID + P] = s == t
    c[:, C_GM:C_GM + 128] = s < t
    c[:, C_GM + 128:C_GM + 256] = s <= t
    c[:, C_GM + 256:C_GM + 384] = s > t
    c[:, C_GM + 384:C_GM + 512] = s >= t
    lm = np.zeros((P, 2, LV, P), np.float16)
    for l in range(LV):
        m = 1 << l
        sib = (s // m // 2) == (t // m // 2)
        fwd = sib & (t // m % 2 == 1) & (s // m % 2 == 0)
        bwd = sib & (t // m % 2 == 0) & (s // m % 2 == 1)
        lm[:, 0, l], lm[:, 1, l] = fwd, bwd
    lm[:, :, 0] += np.eye(P, dtype=np.float16)[:, None, :]
    same = (s // 64) == (t // 64)
    c[:, C_MEAN:C_MEAN + P] = same / 64.0
    c[:, C_HALF:C_HALF + P] = same * 0.5
    c[:, C_SM:C_SM + P] = same / P0SCALE
    c[:, C_SEL:C_SEL + 2] = (s // 64) == np.arange(2)[None, :]
    a = np.zeros((P, CA_END), np.float32)
    pos = np.arange(T, dtype=np.float32)
    inv = (np.float32(10000.0) ** (-np.arange(0, HD, 2, dtype=np.float32) / np.float32(HD))).astype(np.float32)
    ang = (pos[None, :] * inv[:, None]).astype(np.float32)
    a[:, CA_COS:CA_COS + T] = np.concatenate([np.cos(ang), np.cos(ang)], 0)
    a[:, CA_SIN:CA_SIN + T] = np.concatenate([-np.sin(ang), np.sin(ang)], 0)
    j = np.arange(T)[None, :]
    for qb in range(2):
        q = np.arange(P)[:, None] + qb * P
        a[:, CA_MASK + qb * T:CA_MASK + (qb + 1) * T] = np.where(np.abs(j - q) <= 128, 0.0, -1e30)
    return c, a, lm


def block_kernel(nc, I, cst_d, csa_d, lm_d, out_d):
    f32, f32r, i32 = mybir.dt.float32, mybir.dt.float32r, mybir.dt.int32
    ACT, ALU, AX = mybir.ActivationFunctionType, mybir.AluOpType, mybir.AxisListType
    w_in, w_out, w_up, w_dn = I["w_in"][0], I["w_out"][0], I["w_ffn_up"][0], I["w_ffn_down"][0]

    ctx = ExitStack()
    with ctx:
        nbuf = [0]

        def sb(name, shape, dt=f32, stack=ctx):
            return stack.enter_context(nc.sbuf_tensor(name, shape, dt))

        def sig(name, per=1):
            return Sig(ctx.enter_context(nc.semaphore(name)), per)

        raw = sb("raw", [P, 4, 2048])
        whi = sb("whi", [P, 2, 2048], f32r)
        wlo = sb("wlo", [P, 2, 2048], f32r)
        xT = sb("xT", [P, KT, 2, T], f32r)
        cst = sb("cst", [P, C_END])
        lmk = sb("lmk", [P, 2, LV, P], mybir.dt.float16)
        pA = sb("pA", [P, 112])
        pB = sb("pB", [P, 112])
        small = sb("small", [P, 64])
        cells = sb("cells", [P, 8])
        epsh = sb("epsh", [P, 4])
        diag = sb("diag", [P, 2, P])
        ident = cst[:, C_ID:C_ID + P]
        ones_mean, ones_half, hsel = cst[:, C_MEAN:C_MEAN + P], cst[:, C_HALF:C_HALF + P], cst[:, C_SEL:C_SEL + 2]
        PB = [ctx.enter_context(nc.psum_tensor(f"bank{b}", [P, 512], f32)) for b in range(8)]

        mixers = ExitStack()
        mrg = sb("mrg", [P, KT, T], stack=mixers)
        lact = sb("lact", [P, 4, T], stack=mixers)
        gact = sb("gact", [P, 2, T], stack=mixers)
        muL = sb("muL", [P, 6], stack=mixers)
        raw4 = sb("raw4", [P, 4, T + 2], stack=mixers)

        att = ExitStack()
        xtok = sb("xtok", [P, 2, D], stack=att)
        csa = sb("csa", [P, CA_END], stack=att)
        prow = sb("prow", [P, 3, P], stack=att)
        tokA = sb("tokA", [P, 2, T], stack=att)
        tokB = sb("tokB", [P, 2, T], stack=att)
        kr = sb("kr", [P, T], stack=att)
        qr = sb("qr", [P, 2, T], stack=att)
        vf = sb("vf", [P, T], stack=att)
        vtok = sb("vtok", [P, 2, HD], stack=att)
        scm = sb("scm", [P, 2, T], stack=att)
        prb = sb("prb", [P, 2, 2, T], stack=att)
        prT = sb("prT", [P, 2, T], stack=att)
        sinkb = sb("sinkb", [P, 16], stack=att)
        sm = sb("sm", [P, 16], stack=att)
        att.close()

        rw = ExitStack()
        G = [sb(f"G{d}", [P, 4, 4, P], stack=rw) for d in range(2)]
        CT = [sb(f"CT{d}", [P, 4, P], f32r, stack=rw) for d in range(2)]
        W = [sb(f"W{d}", [P, 4, P], f32r, stack=rw) for d in range(2)]
        Dm = [sb(f"Dm{d}", [P, 4, P], f32r, stack=rw) for d in range(2)]
        DT = [sb(f"DT{d}", [P, 4, P], f32r, stack=rw) for d in range(2)]
        sh = sb("sh", [P, 3, T], stack=rw)
        nb = sb("nb", [P, 3, T], stack=rw)
        gt = sb("gt", [P, T], stack=rw)
        gup = sb("gup", [P, T], stack=rw)
        upw = sb("upw", [P, 4, P], stack=rw)
        upg = sb("upg", [P, 2, P], stack=rw)
        AR = [sb(f"AR{d}", [P, 2, T], stack=rw) for d in range(2)]
        kh = [sb(f"kh{d}", [P, T], stack=rw) for d in range(2)]
        Pd = [sb(f"Pd{d}", [P, 2, P + 1], stack=rw) for d in range(2)]
        ta = [sb(f"ta{d}", [P, T], stack=rw) for d in range(2)]
        dec = [sb(f"dec{d}", [P, T], stack=rw) for d in range(2)]
        tw = dec
        km = kh
        bh = ta
        kk = sb("kk", [P, T], stack=rw)
        sq = nb[:, 0, :]
        kA = sb("kA", [P, T], stack=rw)
        kB = sb("kB", [P, T], stack=rw)
        rk = sb("rk", [P, T], stack=rw)
        rep = sb("rep", [P, 2, P], stack=rw)
        Vt = sb("Vt", [P, 2, P], stack=rw)
        KB = sb("KB", [P, 4, P], stack=rw)
        rhs = sb("rhs", [P, 4, 64], f32r, stack=rw)
        U = sb("U", [P, 2, 4, 64], stack=rw)
        Sm = sb("Sm", [P, 2, P], stack=rw)
        zero = sb("zero", [P, P], stack=rw)
        der = sb("der", [P, 112], stack=rw)
        st = sb("st", [P, 8], stack=rw)
        ysb = sb("ysb", [P, T], stack=rw)
        yc = sb("yc", [P, T], stack=rw)
        ysq = sb("ysq", [P, T], stack=rw)
        bon = sb("bon", [P, T], stack=rw)
        AS = sb("AS", [P, 2, 2, P], stack=rw)
        pl = sb("pl", [P, 2], stack=rw)
        rw.close()
        mixers.close()

        ffn = ExitStack()
        hres = sb("hres", [P, 2, D], stack=ffn)
        acc = sb("acc", [P, 2, D], stack=ffn)
        gain = sb("gain", [P, D], stack=ffn)
        ft = sb("ft", [P, 8, 2, T], f32r, stack=ffn)
        fa = sb("fa", [P, 2, T], stack=ffn)
        fs = sb("fs", [P, 2, T], stack=ffn)
        junk = sb("junk", [P, 8, 512], stack=ffn)
        ffn.close()

        raw_full = [sig(f"raw_full{s}") for s in range(4)]
        w_hi, w_lo, w_used, d_evac = sig("w_hi"), sig("w_lo"), sig("w_used"), sig("d_evac")
        s = {}
        for name, per in dict(
            ld_x=1, ld_c=1, ld_c2=1, ld_p=1, n_sq=8, n_st=2, n_pow=1, x_n=2, x_tp=1, x_hi=1, x_lo=1, prm_ms=1,
            prm_tp=1, prm_ev=1, exp_ms=1,
            k_r1=1, k_r=1, v_tp=1, v_tok=1, q_r1=4, q_r=4, sc=4, sc_m=4, mx=4, mx2=4, neg=4,
            ex=4, esink=4, den=4, rden=4, prn=4, p_tp=4, p_T=4, pv=4, o_ev=4,
            ga_m=4, lo_nb=1, lo_df=1, lo_sh=1, lo_act=1, lo_fin=1, drv=1, zr=1,
            up_ld=1, sh_nb=1, sh_df=1, shifted=1, gate_t=1, sqd=1, ss=1, ssm=1, rs=1, rrep=1, rbc=1, nkk=1, gg=2,
            kAB=1, rkd=1, lw=1, la=1, lg=1, tws=1, decs=2, tas=1, gups=1, scan=2, inv=2, ar=2, tt=2, bhs=2, km1=2, km2=2,
            khs=2, kbs=1, t2=1, vtp=1, vts=1, gram=8, gmask=8, dt0=2, d0p=2, d0=2, ctm=12, wmm=12, wev=12,
            ddm=10, dtm=12, dup=10, dtup=12, kbtp=1, kbs2=1, rhsm=2, rhsc=2, um=2, ue=2, resm=2, rese=2, dum=2, due=2,
            smm=1, sme=1, ym=1, ye=1, mean=1, ycs=1, ysqs=1, var=1, vars=1, vpow=1, vrep=1, vbc=1, bonm=1, bonv=1, asc=1, plc=1,
            y1=1, y2=1, y3=1, y4=1, y5=1,
            mg_hi=1, mg_lo=1, om=1, o_cp=1, ld_h=1, ld_g=1, m_h=1,
            h_n=2, h_tp=1, h_hi=1, h_lo=1, up_re=8, up_sq=8, up_hi=8, up_lo=8, dn=4, dn_acc=4, f_n=1, f_o=1, ld_g2=1, done=1, acc0=1,
        ).items():
            s[name] = sig(name, per)
        CHARGED = [w_lo, d_evac] + [s[n] for n in (
            "k_r1", "q_r1", "k_r", "q_r", "v_tp", "sc", "sc_m", "esink", "p_tp", "p_T", "o_ev", "ga_m", "lg", "y5", "due", "dum",
            "ye", "rese", "y1", "ym", "y3", "sme", "asc", "kbtp", "gate_t", "shifted", "up_sq", "up_re", "dn", "dn_acc", "o_cp")]
        for x in CHARGED:
            x.base = 1

        U_ATT, U_GA, U_LO, U_RW = 0, 24, 40, 46
        U_OUT = U_RW + 4 * PAIRS
        U_FF = U_OUT + 16
        FCH = 8




        def raw_count(u_static):
            if u_static < U_GA:
                return 16 * (u_static // 3 + 1)
            return 16 * ((u_static - U_GA) // 4 + 1) + (16 * U_GA // 3 if u_static % 4 < 3 else 0)

        block = ctx.enter_context(nc.Block())

        @block.sync
        def _(sp):
            def load(u_static, u_count, src, n=P, style="B"):
                slot = u_static % 4
                first_gates = isinstance(u_count, int) and u_count < U_GA + 4
                sp.wait_ge(w_lo.sem, w_lo.n(u_count - (2 if first_gates else 3)))
                if style == "B":
                    dst = raw[:, slot, :].rearrange("p (k c) -> p k c", k=KT)[:, :, 0:n]
                else:
                    dst = raw[:, slot, :].rearrange("p (k c) -> p k c", k=4)
                sp.dma_start(dst, src).then_inc(raw_full[slot].sem, 16)

            def cols(c, n=P):
                return w_in[:, bass.ds(c, n)].rearrange("(k p) c -> p k c", p=P)

            for x in CHARGED:
                sp.sem_inc(x.sem, 1)
            for b in range(2):
                sp.dma_start(xtok[:, b, :], I["x"][0][P * b:P * b + P, :]).then_inc(s["ld_x"].sem, 16)
            sp.dma_start(cst[:], cst_d).then_inc(s["ld_c"].sem, 16)
            row = 0
            sp.wait_ge(s["prm_ms"].sem, s["prm_ms"].n(1))
            mu = I["mu_shift"][0]
            n_prm = 0
            for slot, names in ((0, PARAMS_A), (1, PARAMS_B)):
                row = 0
                for name in names:
                    v = mu[0:3 * D] if name == "mu_shift" else I[name][0]
                    n = v.shape[0] // P
                    sp.dma_start(prow[row:row + n, slot, :], v.rearrange("(t c) -> t c", c=P)).then_inc(s["ld_p"].sem, 16)
                    n_prm += 1
                    row += n
            sp.dma_start(prow[0:4, 2, 0:DL], mu[3 * D:3 * D + 4 * DL].rearrange("(t c) -> t c", c=DL)).then_inc(s["ld_p"].sem, 16)
            sp.dma_start(prow[4:6, 2, :], mu[3 * D + 4 * DL:].rearrange("(t c) -> t c", c=P)).then_inc(s["ld_p"].sem, 16)
            sp.dma_start(sinkb[:], I["attn_sink"].partition_broadcast(P)[:, 0, :]).then_inc(s["ld_p"].sem, 16)
            for j in range(3):
                c = (K0, V0, Q0)[j]
                sp.dma_start(raw[:, j, :].rearrange("p (k c) -> p k c", k=KT), w_in[:, c:c + P].rearrange("(k p) c -> p k c", p=P))\
                    .then_inc(raw_full[j].sem, 16)
            sp.dma_start(csa[:], csa_d).then_inc(s["ld_c2"].sem, 16)
            sp.dma_start(lmk[:], lm_d).then_inc(s["ld_c2"].sem, 16)
            def attention_load(j, g, u, slot):
                c = (K0 + P * g, V0 + P * g)[j] if j < 2 else Q0 + P * (j - 2) + 4 * P * g
                sp.wait_ge(w_lo.sem, w_lo.n(u - 2))
                sp.dma_start(raw[:, slot, :].rearrange("p (k c) -> p k c", k=KT), cols(c)).then_inc(raw_full[slot].sem, 16)

            with sp.Fori(0, KVH - 1, 1) as i:
                for j in (3, 4, 5):
                    attention_load(j, i, 6 * i + j, j % 3)
                for j in (0, 1, 2):
                    attention_load(j, i + 1, 6 * i + 6 + j, j % 3)
            for j in (3, 4, 5):
                attention_load(j, KVH - 1, 6 * (KVH - 1) + j, j % 3)
            for j in range(4):
                load(U_GA + j, U_GA + j, cols(GA0 + P * j))
            with sp.Fori(0, 3, 1) as i:
                for j in range(4):
                    load(U_GA + j, 4 * i + 4 + U_GA + j, cols(GA0 + P * j + 4 * P + 4 * P * i))
            lora = [(LO0 + DL * j, DL) for j in range(4)] + [(LO0 + 4 * DL + P * j, P) for j in range(2)]
            for j, (c, n) in enumerate(lora):
                load(U_LO + j, U_LO + j, w_in[:, c:c + n].rearrange("(k p) c -> p k c", p=P), n)

            def pair_units(i):
                for j, c0 in enumerate((RK0, R0, RV0, GR0)):
                    load(U_RW + j, 4 * i + U_RW + j, cols(c0 + P * i))

            def pair_ups(i):
                if not isinstance(i, int) or i > 0:
                    sp.wait_ge(s["lg"].sem, s["lg"].before(i))
                for j, name in enumerate(("w_up_fwd", "w_up_bwd", "a_up_fwd", "a_up_bwd")):
                    sp.dma_start(upw[0:DL, j, :], I[name][0][:, bass.ds(P * i, P)]).then_inc(s["up_ld"].sem, 16)
                sp.dma_start(upg[:], I["g_up"][0][:, bass.ds(P * i, P)].rearrange("(k p) c -> p k c", p=P)).then_inc(s["up_ld"].sem, 16)

            pair_units(0)
            sp.wait_ge(s["ga_m"].sem, s["ga_m"].n(16))
            sp.wait_ge(s["o_ev"].sem, s["o_ev"].n(16))
            pair_ups(0)
            pair_units(1)
            with sp.Fori(0, PAIRS - 2, 1) as i:
                pair_units(i + 2)
                pair_ups(i + 1)
            pair_ups(PAIRS - 1)

            def out_units(i, u0, wt, rows):
                for j in range(8):
                    nblk, kc = j // 4, j % 4
                    load(u0 + j, 8 * i + u0 + j, wt[kc * 512:(kc + 1) * 512, bass.ds(512 * nblk + 1024 * i, 512)]
                         .rearrange("(k p) c -> p k c", p=P), style="A")

            with sp.Fori(0, 2, 1) as i:
                out_units(i, U_OUT, w_out, D)

            with sp.Fori(0, FCH, 1) as i:
                for j in range(8):
                    load(U_FF + j, 16 * i + U_FF + j, w_up[:, bass.ds(P * j + 1024 * i, P)].rearrange("(k p) c -> p k c", p=P))
                for j in range(8):
                    nblk, kc = j // 2, j % 2
                    load(U_FF + 8 + j, 16 * i + U_FF + 8 + j,
                         w_dn[bass.ds(512 * kc + 1024 * i, 512), 512 * nblk:512 * nblk + 512].rearrange("(k p) c -> p k c", p=P), style="A")
            sp.wait_ge(s["m_h"].sem, s["m_h"].n(4))
            sp.dma_start(gain[:], I["norm_post_ffn"].partition_broadcast(P)[:, 0, :]).then_inc(s["ld_g2"].sem, 16)
            for b in range(2):
                sp.wait_ge(s["f_o"].sem, s["f_o"].n(b + 1))
                sp.dma_start(out_d[0][b * P:(b + 1) * P, :], acc[:, b, :]).then_inc(s["done"].sem, 16)
            sp.wait_ge(s["done"].sem, s["done"].n(32))

        @block.scalar
        def _(act):
            A = nc.scalar

            def cut_hi(u_static, u, half=None):
                if half == 1:
                    A.activation(whi[:, u_static % 2, 1024:], raw[:, u_static % 4, 1024:], ACT.Copy).then_inc(w_hi.sem, 1)
                    return
                slot = u_static % 4
                step = u - u_static
                act.wait_ge(raw_full[slot].sem, raw_full[slot].n(raw_count(u_static) + step * 4))
                if u_static >= 2:
                    act.wait_ge(w_used.sem, w_used.n(u - 1))
                if half is None:
                    A.activation(whi[:, u_static % 2, :], raw[:, slot, :], ACT.Copy).then_inc(w_hi.sem, 1)
                else:
                    A.activation(whi[:, u_static % 2, 0:1024], raw[:, slot, 0:1024], ACT.Copy)

            squares_out = mrg[:].rearrange("p k t -> p (k t)")
            act.wait_ge(s["ld_x"].sem, s["ld_x"].n(32))
            for b in range(2):
                for q in range(4):
                    c = 4 * b + q
                    A.activation(squares_out[:, 512 * c:512 * c + 512], xtok[:, b, 512 * q:512 * q + 512], ACT.Square,
                                 accum_out=small[:, c:c + 1]).then_inc(s["n_sq"].sem, 1)

            def hi_parts(turned, hi, banks, col):
                for k in range(KT):
                    act.wait_ge(s[turned].sem, k // 2 + 1)
                    A.activation(xT[:, k, 0, :], banks[(k // 2) % 4][:, T * (k % 2):T * (k % 2) + T], ACT.Copy,
                                 scale=pB[:, col + k:col + k + 1]).then_inc(s[hi].sem, 1)


            def cut_attention(u_static, i=0):
                slot = u_static % 3 if u_static < U_GA else u_static % 4
                act.wait_ge(raw_full[slot].sem, raw_full[slot].n(raw_count(u_static) + 32 * i))
                if u_static >= 2:
                    act.wait_ge(w_used.sem, w_used.n(u_static + 6 * i - 1))
                A.activation(whi[:, u_static % 2, :], raw[:, slot, :], ACT.Copy).then_inc(w_hi.sem, 1)

            def evacuate(j, g, u_static, u):
                act.wait_ge(w_used.sem, w_used.n(u + 1))
                bank = PB[u_static % 2]
                if j == 1:
                    act.wait_ge(s["v_tp"].sem, s["v_tp"].before(g))
                    A.activation(vf[:], bank[:, 0:T], ACT.Copy).then_inc(d_evac.sem, 1)
                    return
                if j == 0:
                    act.wait_ge(s["q_r1"].sem, s["q_r1"].before(g))
                else:
                    act.wait_ge(s["k_r1"].sem, s["k_r1"].at(g))
                    act.wait_ge(s["q_r1"].sem, s["q_r1"].at(g, j - 2))
                A.activation(tokA[:, 0, :], bank[:, 0:T], ACT.Copy)
                A.activation(tokA[0:64, 1, :], bank[64:P, 0:T], ACT.Copy)
                A.activation(tokA[64:P, 1, :], bank[0:64, 0:T], ACT.Copy).then_inc(d_evac.sem, 1)

            def gate_tanh(j, i):
                u = U_GA + j
                act.wait_ge(w_used.sem, w_used.n(4 * i + u + 1))
                act.wait_ge(s["ga_m"].sem, s["ga_m"].at(i, j))
                A.activation(tokA[:, j % 2, :], PB[u % 2][:, 0:T], ACT.Tanh, scale=0.5).then_inc(d_evac.sem, 1)

            def turned(g, h):
                act.wait_ge(s["p_tp"].sem, s["p_tp"].at(g, h + 1))
                A.activation(prT[:].rearrange("p a b -> p (a b)"), PB[5][:, :], ACT.Copy).then_inc(s["p_T"].sem, 1)

            def output(g, h):
                act.wait_ge(s["pv"].sem, s["pv"].at(g, h + 1))
                A.activation(mrg[:, bass.ds(4 * g + h, 1), :].rearrange("p a t -> p (a t)"), PB[6][:, 0:T], ACT.Copy)\
                    .then_inc(s["o_ev"].sem, 1)

            def exponentials(g, h):
                act.wait_ge(s["neg"].sem, s["neg"].at(g, h + 1))
                act.wait_ge(s["p_tp"].sem, s["p_tp"].at(g, h - 1) if h >= 2 else s["p_tp"].before(g))
                for qb in range(2):
                    x = A.activation(prb[:, h % 2, qb, :], scm[:, qb, :], ACT.Exp, bias=sm[:, 6 + qb:7 + qb],
                                     scale=float(HD) ** -0.5, accum_out=sm[:, 8 + qb:9 + qb])
                x.then_inc(s["ex"].sem, 1)
                A.activation(sm[:, 10:12], sm[:, 4:6], ACT.Exp).then_inc(s["esink"].sem, 1)

            def step(j, g, hg, u_static, i=0):
                u = u_static + 6 * i
                if g is None:
                    gate_tanh(j, 0)
                else:
                    evacuate(j, g, u_static, u)
                h = (j + 1) % 6
                if hg is not None and h < 4:
                    output(hg, h)
                h = (j + 2) % 6
                if hg is not None and h < 4:
                    turned(hg, h)
                if j == 2 and g is not None:
                    act.wait_ge(s["v_tp"].sem, s["v_tp"].at(g))
                    A.activation(vtok[:].rearrange("p a b -> p (a b)"), PB[2][:, 0:T], ACT.Copy).then_inc(s["v_tok"].sem, 1)
                cut_attention(u_static + 2, i)
                h = (j + 3) % 6
                if hg is not None and h < 4:
                    exponentials(hg, h)

            cut_attention(0)
            cut_attention(1)
            act.wait_ge(s["prm_ev"].sem, s["prm_ev"].n(3))
            hi_parts("x_tp", "x_hi", PB[2:6], 80)
            for j in (0, 1, 2):
                step(j, 0, None, j)
            with act.Fori(0, KVH - 1, 1) as i:
                for j in (3, 4, 5):
                    step(j, i, i, j, i)
                for j in (0, 1, 2):
                    step(j, i + 1, i, 6 + j, i)
            for j in (3, 4, 5):
                step(j, KVH - 1, KVH - 1, 18 + j)
            for j in (0, 1, 2):
                step(j, None, KVH - 1, U_GA + j)
            gate_tanh(3, 0)
            cut_hi(U_GA + 5, U_GA + 5)
            with act.Fori(0, 3, 1) as i:
                for j in range(4):
                    gate_tanh(j, i + 1)
                    cut_hi(U_GA + j + 2, 4 * i + 4 + U_GA + j + 2)
            for j in range(6):
                u = U_LO + j
                n = DL if j < 4 else P
                act.wait_ge(w_used.sem, w_used.n(u + 1))
                if j == 0:
                    act.wait_ge(s["zr"].sem, s["zr"].n(2))
                else:
                    act.wait_ge(s["lo_sh"].sem, s["lo_sh"].n(j))
                A.activation(raw4[0:n, 0, 1:T + 1], PB[u % 2][0:n, 0:T], ACT.Copy).then_inc(d_evac.sem, 1)
                cut_hi(u + 2, u + 2)
                act.wait_ge(s["lo_sh"].sem, s["lo_sh"].n(j + 1))
                if j < 2:
                    A.activation(lact[0:n, j, :], lact[0:n, j, :], ACT.Tanh).then_inc(s["lo_act"].sem, 1)
                elif j >= 4:
                    A.activation(gact[:, j - 4, :], gact[:, j - 4, :], ACT.Tanh, scale=0.5).then_inc(s["lo_act"].sem, 1)

            def dense(j, i):
                u = U_RW + j
                act.wait_ge(w_used.sem, w_used.n(4 * i + u + 1))
                if j < 3:
                    act.wait_ge(s["shifted"].sem, s["shifted"].before(i))
                else:
                    act.wait_ge(s["gate_t"].sem, s["gate_t"].before(i))
                slot = (1, 0, 2, 3)[j]
                A.activation(raw4[:, slot, 1:T + 1], PB[u % 2][:, 0:T], ACT.Copy).then_inc(d_evac.sem, 1)

            def cut_pair(j, i, half=None):
                if i is not None:
                    cut_hi(U_RW + j + 2, 4 * i + U_RW + j + 2, half)

            def decays(n):
                act.wait_ge(s["kbtp"].sem, s["kbtp"].before(n))
                act.wait_ge(s["lw"].sem, s["lw"].at(n))
                for d in range(2):
                    x = A.activation(tw[d][:], PB[2][:, T * d:T * d + T], ACT.Tanh, scale=0.5,
                                     bias=der[:, bass.ds(16 * d + n, 1)])
                x.then_inc(s["tws"].sem, 1)

            def decays_exp(n):
                act.wait_ge(s["tws"].sem, s["tws"].at(n))
                for d in range(2):
                    A.activation(dec[d][:], tw[d][:], ACT.Exp, scale=-0.5 * DECAY_E, bias=-0.5 * DECAY_E).then_inc(s["decs"].sem, 1)

            def rates(n):
                act.wait_ge(s["la"].sem, s["la"].at(n))
                for d in range(2):
                    x = A.activation(ta[d][:], PB[3][:, T * d:T * d + T], ACT.Tanh, scale=0.5,
                                     bias=der[:, bass.ds(32 + 16 * d + n, 1)])
                x.then_inc(s["tas"].sem, 1)

            def squares(n):
                act.wait_ge(s["shifted"].sem, s["shifted"].at(n))
                A.activation(sq, sh[:, 1, :], ACT.Square, scale=pB[:, bass.ds(n, 1)]).then_inc(s["sqd"].sem, 1)

            def key_parts(n):
                A.activation(kA[:], sh[:, 1, :], ACT.Copy, scale=der[:, bass.ds(64 + n, 1)])
                A.activation(kB[:], sh[:, 1, :], ACT.Copy, scale=der[:, bass.ds(80 + n, 1)]).then_inc(s["kAB"].sem, 1)
                A.activation(rk[:], sh[:, 0, :], ACT.Copy, scale=pB[:, bass.ds(32 + n, 1)]).then_inc(s["rkd"].sem, 1)

            def values(n):
                act.wait_ge(s["ym"].sem, s["ym"].before(n))
                act.wait_ge(s["vtp"].sem, s["vtp"].at(n))
                A.activation(Vt[:].rearrange("p a b -> p (a b)"), PB[5][:, 0:T], ACT.Copy).then_inc(s["vts"].sem, 1)

            def pair(i, n, d1, d2):
                w = lambda name, k=None: act.wait_ge(s[name].sem, s[name].at(i, k))
                act.wait_ge(s["y5"].sem, s["y5"].before(i))
                w("lg")
                A.activation(gup[:], PB[4][:, 0:T], ACT.Copy).then_inc(s["gups"].sem, 1)
                A.activation(gt[:], raw4[:, 3, 1:T + 1], ACT.Tanh, scale=0.5).then_inc(s["gate_t"].sem, 1)
                for d in range(2):
                    w("d0p", d + 1)
                    A.activation(Dm[d][:].rearrange("p a b -> p (a b)"), PB[5 + d][:, :], ACT.Copy).then_inc(s["d0"].sem, 1)
                    cut_pair(1, d1, d)
                for l in range(1, LV):
                    for d in range(2):
                        w("wmm", 2 * (l - 1) + d + 1)
                        A.activation(W[d][:].rearrange("p a b -> p (a b)"), PB[4 - d][:, :], ACT.Copy).then_inc(s["wev"].sem, 1)
                        if l == 3 and d == 0 and d1 is not None:
                            dense(2, d1)
                        if l in (3, 4) and d == 1:
                            cut_pair(2, d1, l - 3)
                w("kbtp")
                A.activation(KB[:].rearrange("p a b -> p (a b)"), PB[3][:, :], ACT.Copy).then_inc(s["kbs2"].sem, 1)
                if d1 is not None:
                    dense(3, d1)
                for c in range(2):
                    w("rhsm", c + 1)
                    A.activation(rhs[:].rearrange("p a b -> p (a b)"), PB[4][:, 0:T], ACT.Copy).then_inc(s["rhsc"].sem, 1)
                    if c == 0 and n is not None:
                        decays(n)
                    w("um", c + 1)
                    A.activation(U[:, c, :, :].rearrange("p a b -> p (a b)"), PB[5][:, 0:T], ACT.Copy).then_inc(s["ue"].sem, 1)
                    if c == 0:
                        if n is not None:
                            decays_exp(n)
                        cut_pair(3, d1, 0)
                        if n is not None:
                            rates(n)
                            squares(n)
                        cut_pair(3, d1, 1)
                        if n is not None:
                            key_parts(n)
                        if d2 is not None:
                            dense(0, d2)
                    else:
                        cut_pair(0, d2, 0)
                        cut_pair(0, d2, 1)
                act.wait_ge(s["y3"].sem, s["y3"].before(i))
                w("ym")
                A.activation(ysb[:], PB[2][:, 0:T], ACT.Copy).then_inc(s["ye"].sem, 1)
                if n is not None:
                    values(n)
                w("ycs")
                A.activation(ysq[:], yc[:], ACT.Square).then_inc(s["ysqs"].sem, 1)
                if d2 is not None:
                    dense(1, d2)
                w("y1")
                A.activation(yc[:], yc[:], ACT.Identity, scale=pB[:, bass.ds(48 + i, 1)],
                             bias=pB[:, bass.ds(64 + i, 1)]).then_inc(s["y2"].sem, 1)

            for j in range(4):
                dense(j, 0)
                cut_pair(j, 0)
            decays(0)
            decays_exp(0)
            rates(0)
            squares(0)
            key_parts(0)
            act.wait_ge(s["vtp"].sem, s["vtp"].at(0))
            A.activation(Vt[:].rearrange("p a b -> p (a b)"), PB[5][:, 0:T], ACT.Copy).then_inc(s["vts"].sem, 1)
            dense(0, 1)
            cut_pair(0, 1)
            dense(1, 1)
            with act.Fori(0, PAIRS - 2, 1) as i:
                pair(i, i + 1, i + 1, i + 2)
            pair(PAIRS - 2, PAIRS - 1, PAIRS - 1, None)
            pair(PAIRS - 1, None, None, None)

            act.wait_ge(w_used.sem, w_used.n(U_OUT))
            act.wait_ge(s["y5"].sem, s["y5"].n(16))
            for k in range(KT):
                A.activation(xT[:, k, 0, :], mrg[:, k, :], ACT.Copy).then_inc(s["mg_hi"].sem, 1)
            act.wait_ge(s["mg_lo"].sem, s["mg_lo"].n(16))
            act.dma_start(gain[:], I["norm_post_mix"].partition_broadcast(P)[:, 0, :]).then_inc(s["ld_g"].sem, 16)
            act.dma_start(hres[:], I["x"][0].rearrange("(b p) c -> p b c", p=P)).then_inc(s["ld_h"].sem, 16)
            with act.Fori(0, 2, 1) as i:
                for j in range(8):
                    cut_hi(U_OUT + j + 2, 8 * i + U_OUT + j + 2)
                    if j % 4 == 3:
                        n = j // 4
                        act.wait_ge(s["om"].sem, s["om"].n(2 * i + n + 1))
                        act.wait_ge(s["mg_lo"].sem, s["mg_lo"].n(16))
                        act.wait_ge(s["n_sq"].sem, s["n_sq"].n(8 + 4 * i))
                        for b in range(2):
                            A.activation(junk[:, 2 * n + b, :], PB[2 * n + b][:, :], ACT.Square,
                                         accum_out=small[:, bass.ds(16 + 4 * b + n + 2 * i, 1)]).then_inc(s["n_sq"].sem, 1)

            def sumsq(src, norm, col):
                act.wait_ge(s["n_sq"].sem, s["n_sq"].before(norm))
                for b in range(2):
                    for q in range(4):
                        if norm == 2 and q % 2 == 0:
                            act.wait_ge(s["m_h"].sem, s["m_h"].n(2 * b + q // 2 + 1))
                        A.activation(junk[:, 4 * b + q, :], src[:, b, 512 * q:512 * q + 512], ACT.Square,
                                     accum_out=small[:, col + 4 * b + q:col + 4 * b + q + 1]).then_inc(s["n_sq"].sem, 1)

            sumsq(hres, 2, 32)
            act.wait_ge(w_used.sem, w_used.n(U_FF))
            hi_parts("h_tp", "h_hi", PB[4:8], 96)
            def chunk(i, last):
                for j in range(16):
                    u = U_FF + j
                    if j < 8:
                        act.wait_ge(w_used.sem, w_used.n(16 * i + u + 1))
                        act.wait_ge(s["up_sq"].sem, s["up_sq"].at(i, j - 1) if j else s["up_sq"].before(i))
                        A.activation(fa[:, j % 2, :], PB[u % 2][:, 0:T], ACT.Relu).then_inc(s["up_re"].sem, 1)
                    if not (last and j >= 14):
                        cut_hi(u + 2, 16 * i + u + 2)
                    if j < 8:
                        act.wait_ge(s["up_sq"].sem, s["up_sq"].at(i, j + 1))
                        if j == 0:
                            act.wait_ge(s["dn"].sem, s["dn"].before(i))
                        A.activation(ft[:, j, 0, :], fs[:, j % 2, :], ACT.Copy).then_inc(s["up_hi"].sem, 1)

            with act.Fori(0, FCH - 1, 1) as i:
                chunk(i, False)
            chunk(FCH - 1, True)
            act.wait_ge(s["dn_acc"].sem, s["dn_acc"].n(4 * FCH))
            sumsq(acc, 3, 48)

        @block.vector
        def _(dve):
            V = nc.vector

            def cut_lo(u_static, u, half=None):
                if half != 1:
                    dve.wait_ge(w_hi.sem, w_hi.n(u + 1))
                part = {None: slice(0, 2048), 0: slice(0, 1024), 1: slice(1024, 2048)}[half]
                x = V.tensor_tensor(wlo[:, u_static % 2, part], raw[:, u_static % 4, part], whi[:, u_static % 2, part].bitcast(f32),
                                    ALU.subtract)
                if half != 0:
                    x.then_inc(w_lo.sem, 1)

            def rstd(col, norm, eps=EPS):
                dve.wait_ge(s["n_sq"].sem, s["n_sq"].at(norm))
                V.tensor_reduce(small[:, col + 8:col + 10], small[:, col:col + 8].rearrange("p (b q) -> p b q", b=2), AX.X, ALU.add)\
                    .then_inc(s["n_st"].sem, 1)
                dve.wait_ge(s["n_st"].sem, s["n_st"].at(norm, 1))
                V.tensor_scalar(small[:, col + 10:col + 12], small[:, col + 8:col + 10], 1.0 / D, eps, ALU.mult, ALU.add)\
                    .then_inc(s["n_st"].sem, 1)

            V.memset(prow[:], 0.0).then_inc(s["prm_ms"].sem, 1)
            V.memset(epsh[:], -0.5).then_inc(s["exp_ms"].sem, 1)
            rstd(0, 0)
            dve.wait_ge(s["prm_tp"].sem, s["prm_tp"].n(3))
            V.tensor_copy(pA[:], PB[7][:, 0:112]).then_inc(s["prm_ev"].sem, 1)
            V.tensor_copy(pB[:], PB[7][:, 128:240]).then_inc(s["prm_ev"].sem, 1)
            V.tensor_copy(muL[:], PB[7][:, 256:262]).then_inc(s["prm_ev"].sem, 1)
            dve.wait_ge(s["prm_ev"].sem, s["prm_ev"].n(3))

            def diagonals(norm, col, name):
                dve.wait_ge(s["n_pow"].sem, s["n_pow"].at(norm))
                for b in range(2):
                    V.tensor_scalar(diag[:, b, :], ident, small[:, col + 12 + b:col + 13 + b], None, ALU.mult).then_inc(s[name].sem, 1)

            def lo_parts(hi, lo, banks, col):
                for k in range(KT):
                    if k % 2 == 0:
                        dve.wait_ge(s[hi].sem, k + 2)
                    V.scalar_tensor_tensor(xT[:, k, 1, :], banks[(k // 2) % 4][:, T * (k % 2):T * (k % 2) + T], pB[:, col + k:col + k + 1],
                                           xT[:, k, 0, :].bitcast(f32), ALU.mult, ALU.subtract).then_inc(s[lo].sem, 1)

            diagonals(0, 0, "x_n")
            cut_lo(0, 0)
            cut_lo(1, 1)
            lo_parts("x_hi", "x_lo", PB[2:6], 80)
            dve.wait_ge(s["ld_c2"].sem, s["ld_c2"].n(32))
            cos, sin = csa[:, CA_COS:CA_COS + T], csa[:, CA_SIN:CA_SIN + T]
            wmask = csa[:, CA_MASK:CA_MASK + 2 * T]
            def rotate(j, g):
                r1, r2 = (s["k_r1"], s["k_r"]) if j == 0 else (s["q_r1"], s["q_r"])
                m = 1 if j == 0 else j - 1
                dst = kr[:] if j == 0 else qr[:, j % 2, :]
                if j == 0:
                    dve.wait_ge(s["q_r"].sem, s["q_r"].before(g))
                else:
                    dve.wait_ge(s["k_r"].sem, s["k_r"].at(g))
                    dve.wait_ge(s["q_r"].sem, s["q_r"].at(g, j - 2))
                V.tensor_tensor(tokB[:, 0, :], tokA[:, 0, :], cos, ALU.mult)
                V.tensor_tensor(tokB[:, 1, :], tokA[:, 1, :], sin, ALU.mult).then_inc(r1.sem, 1)
                dve.wait_ge(r1.sem, r1.at(g, m))
                if j == 0:
                    dve.wait_ge(s["sc"].sem, s["sc"].before(g))
                elif j >= 4:
                    dve.wait_ge(s["sc"].sem, s["sc"].at(g, j - 3))
                V.tensor_tensor(dst, tokB[:, 0, :], tokB[:, 1, :], ALU.add).then_inc(r2.sem, 1)

            def gate_product(j, i):
                dve.wait_ge(d_evac.sem, d_evac.n(4 * i + U_GA + j + 1))
                dve.wait_ge(s["o_ev"].sem, s["o_ev"].n(4 if isinstance(i, int) else 16))
                m = mrg[:, bass.ds(j + 4 * i, 1), :].rearrange("p a t -> p (a t)")
                V.scalar_tensor_tensor(m, tokA[:, j % 2, :], 1.0, m, ALU.add, ALU.mult).then_inc(s["ga_m"].sem, 1)

            def maxima(g, h):
                dve.wait_ge(s["sc"].sem, s["sc"].at(g, h + 1))
                dve.wait_ge(s["esink"].sem, s["esink"].at(g, h) if h else s["esink"].before(g))
                V.tensor_tensor(scm[:].rearrange("p a b -> p (a b)"), PB[3 + h % 2][:, :], wmask, ALU.add).then_inc(s["sc_m"].sem, 1)
                dve.wait_ge(s["sc_m"].sem, s["sc_m"].at(g, h + 1))
                V.tensor_reduce(sm[:, 0:2], scm[:], AX.X, ALU.max).then_inc(s["mx"].sem, 1)
                dve.wait_ge(s["mx"].sem, s["mx"].at(g, h + 1))
                sink = sinkb[:, bass.ds(4 * g + h, 1)]
                V.tensor_scalar(sm[:, 2:4], sm[:, 0:2], float(HD) ** -0.5, sink, ALU.mult, ALU.max).then_inc(s["mx2"].sem, 1)
                dve.wait_ge(s["mx2"].sem, s["mx2"].at(g, h + 1))
                V.tensor_scalar(sm[:, 6:8], sm[:, 2:4], -1.0, None, ALU.mult)
                V.tensor_scalar(sm[:, 4:6], sm[:, 2:4], -1.0, sink, ALU.mult, ALU.add).then_inc(s["neg"].sem, 1)

            def normalise(g, h):
                dve.wait_ge(s["ex"].sem, s["ex"].at(g, h + 1))
                dve.wait_ge(s["esink"].sem, s["esink"].at(g, h + 1))
                V.tensor_tensor(sm[:, 12:14], sm[:, 8:10], sm[:, 10:12], ALU.add).then_inc(s["den"].sem, 1)
                dve.wait_ge(s["den"].sem, s["den"].at(g, h + 1))
                V.reciprocal(sm[:, 14:16], sm[:, 12:14]).then_inc(s["rden"].sem, 1)
                dve.wait_ge(s["rden"].sem, s["rden"].at(g, h + 1))
                for qb in range(2):
                    x = V.tensor_scalar(prb[:, h % 2, qb, :], prb[:, h % 2, qb, :], sm[:, 14 + qb:15 + qb], None, ALU.mult)
                x.then_inc(s["prn"].sem, 1)

            def cut_attention(u_static, i=0):
                slot = u_static % 3 if u_static < U_GA else u_static % 4
                dve.wait_ge(w_hi.sem, w_hi.n(u_static + 6 * i + 1))
                V.tensor_tensor(wlo[:, u_static % 2, :], raw[:, slot, :], whi[:, u_static % 2, :].bitcast(f32), ALU.subtract)\
                    .then_inc(w_lo.sem, 1)

            def step(j, g, hg, u_static, i=0):
                u = u_static + 6 * i
                h = (j + 3) % 6
                if hg is not None and h < 4:
                    maxima(hg, h)
                if g is None:
                    gate_product(j, 0)
                elif j != 1:
                    dve.wait_ge(d_evac.sem, d_evac.n(u + 1))
                    rotate(j, g)
                cut_attention(u_static + 2, i)
                if hg is not None and h < 4:
                    normalise(hg, h)

            for j in (0, 1, 2):
                step(j, 0, None, j)
            with dve.Fori(0, KVH - 1, 1) as i:
                for j in (3, 4, 5):
                    step(j, i, i, j, i)
                for j in (0, 1, 2):
                    step(j, i + 1, i, 6 + j, i)
            for j in (3, 4, 5):
                step(j, KVH - 1, KVH - 1, 18 + j)
            for j in (0, 1, 2):
                step(j, None, KVH - 1, U_GA + j)
            gate_product(3, 0)
            cut_lo(U_GA + 5, U_GA + 5)
            with dve.Fori(0, 3, 1) as i:
                for j in range(4):
                    gate_product(j, i + 1)
                    cut_lo(U_GA + j + 2, 4 * i + 4 + U_GA + j + 2)
            dve.wait_ge(s["ga_m"].sem, s["ga_m"].n(16))
            V.memset(raw4[:], 0.0).then_inc(s["zr"].sem, 1)
            V.memset(lact[:], 0.0).then_inc(s["zr"].sem, 1)
            for d in range(2):
                V.memset(G[d][:], 0.0).then_inc(s["zr"].sem, 1)
            dve.wait_ge(s["zr"].sem, s["zr"].n(4))
            for d in range(2):
                V.tensor_copy(G[d][:, :, 0, :], ident.unsqueeze(1).to_broadcast([P, 4, P])).then_inc(s["drv"].sem, 1)
            V.memset(zero[:], 0.0).then_inc(s["zr"].sem, 1)
            V.memset(Pd[0][:, :, 0:1], P0SCALE).then_inc(s["zr"].sem, 1)
            V.memset(Pd[1][:, :, P:P + 1], P0SCALE).then_inc(s["zr"].sem, 1)
            V.tensor_scalar(der[:, 0:64], pA[:, 48:112], 0.5, None, ALU.mult).then_inc(s["drv"].sem, 1)
            V.tensor_scalar(der[:, 64:80], pB[:, 16:32], 0.5, None, ALU.mult).then_inc(s["drv"].sem, 1)
            V.tensor_scalar(der[:, 80:96], pB[:, 16:32], -0.5, 1.0, ALU.mult, ALU.add).then_inc(s["drv"].sem, 1)
            dve.wait_ge(s["zr"].sem, s["zr"].n(7))
            V.tensor_scalar(der[:, 96:112], pB[:, 0:16], -1.0, None, ALU.mult).then_inc(s["drv"].sem, 1)
            dve.wait_ge(s["drv"].sem, s["drv"].n(6))
            for j in range(6):
                u = U_LO + j
                n = DL if j < 4 else P
                dst = lact[0:n, j, :] if j < 4 else gact[:, j - 4, :]
                dve.wait_ge(d_evac.sem, d_evac.n(u + 1))
                V.tensor_tensor(nb[0:n, 0, :], raw4[0:n, 0, 0:T], raw4[0:n, 0, 2:T + 2], ALU.add).then_inc(s["lo_nb"].sem, 1)
                dve.wait_ge(s["lo_nb"].sem, s["lo_nb"].n(j + 1))
                V.scalar_tensor_tensor(nb[0:n, 1, :], nb[0:n, 0, :], 0.5, raw4[0:n, 0, 1:T + 1], ALU.mult, ALU.subtract).then_inc(s["lo_df"].sem, 1)
                dve.wait_ge(s["lo_df"].sem, s["lo_df"].n(j + 1))
                V.scalar_tensor_tensor(dst, nb[0:n, 1, :], muL[0:n, j:j + 1], raw4[0:n, 0, 1:T + 1], ALU.mult, ALU.add).then_inc(s["lo_sh"].sem, 1)
                cut_lo(u + 2, u + 2)
            dve.wait_ge(s["lo_act"].sem, s["lo_act"].n(4))
            V.tensor_scalar(gact[:], gact[:], 0.5, 0.5, ALU.mult, ALU.add).then_inc(s["lo_fin"].sem, 1)

            def cut_pair(j, i, half=None):
                if i is not None:
                    cut_lo(U_RW + j + 2, 4 * i + U_RW + j + 2, half)

            blocks = lambda t: t.rearrange("p (a b) -> p a b", a=2)
            r, k, v = sh[:, 0, :], sh[:, 1, :], sh[:, 2, :]
            inc = lambda x, name: x.then_inc(s[name].sem, 1)

            class Prep:

                def __init__(self, n):
                    self.n = n
                    self.w = lambda name, k=None: dve.wait_ge(s[name].sem, s[name].at(n, k))
                    self.col = lambda t, c: t[:, bass.ds(c + n, 1)]

                def neighbours(self):
                    n, w = self.n, self.w
                    dve.wait_ge(d_evac.sem, d_evac.n(U_RW + 3 + 4 * n))
                    inc(V.tensor_tensor(nb[:], raw4[:, 0:3, 0:T], raw4[:, 0:3, 2:T + 2], ALU.add), "sh_nb")
                    w("sh_nb")
                    inc(V.scalar_tensor_tensor(nb[:], nb[:], 0.5, raw4[:, 0:3, 1:T + 1], ALU.mult, ALU.subtract), "sh_df")

                def shift(self):
                    w, col = self.w, self.col
                    w("sh_df")
                    for c in (1, 0, 2):
                        x = V.scalar_tensor_tensor(sh[:, c, :], nb[:, c, :], col(pA, 16 * c), raw4[:, c, 1:T + 1], ALU.mult, ALU.add)
                    inc(x, "shifted")

                def keys(self):
                    w = self.w
                    w("ss")
                    inc(V.tensor_scalar(st[:, 0:4], PB[7][:, 0:4], 1e-24, None, ALU.max), "ssm")

                def norm(self):
                    w = self.w
                    w("rs")
                    for tb in range(2):
                        x = V.tensor_copy(rep[:, tb, :].rearrange("p (h f) -> p h f", h=2),
                                          st[:, 4 + 2 * tb:6 + 2 * tb].unsqueeze(2).to_broadcast([P, 2, 64]))
                    inc(x, "rrep")

                def products(self, d):
                    w = self.w
                    w("decs", d + 1)
                    for tb in range(2):
                        src = dec[d][:, P * tb:P * tb + P]
                        if d == 0:
                            x = V.tensor_tensor_scan(Pd[0][:, tb, 1:P + 1], src, zero[:], P0SCALE, ALU.mult, ALU.add)
                        else:
                            x = V.tensor_tensor_scan(Pd[1][:, tb, 0:P][:, ::-1], src[:, ::-1], zero[:], P0SCALE, ALU.mult, ALU.add)
                    inc(x, "scan")

                def modified(self):
                    w = self.w
                    w("rbc")
                    inc(V.scalar_tensor_tensor(kk[:], k, self.col(der, 96), PB[7][:, 0:T], ALU.mult, ALU.mult), "nkk")
                    w("tas")
                    w("kAB")
                    for d in range(2):
                        inc(V.tensor_tensor(km[d][:], kA[:], ta[d][:], ALU.mult), "km1")
                    w("nkk")
                    for d in range(2):
                        w("km1", d + 1)
                        inc(V.tensor_tensor(km[d][:], km[d][:], kB[:], ALU.add), "km2")
                        inc(V.scalar_tensor_tensor(ta[d][:], ta[d][:], 1.0, kk[:], ALU.add, ALU.mult), "tt")

                def inverse(self, d):
                    incl = Pd[d][:, :, 1:P + 1] if d == 0 else Pd[d][:, :, 0:P]
                    self.w("scan", d + 1)
                    inc(V.reciprocal(blocks(dec[d][:]), incl), "inv")

                def hats(self, d):
                    w = self.w
                    w("tt", d + 1)
                    w("inv", d + 1)
                    inc(V.scalar_tensor_tensor(bh[d][:], ta[d][:], -0.5, dec[d][:], ALU.mult, ALU.mult), "bhs")
                    w("km2", d + 1)
                    w("kbs")
                    inc(V.tensor_tensor(kh[d][:], km[d][:], dec[d][:], ALU.mult), "khs")

            class Gram:

                def __init__(self, n):
                    self.n = n
                    self.w = lambda name, k=None: dve.wait_ge(s[name].sem, s[name].at(n, k))

                def keep(self, m):
                    d, q = m // 4, m % 4
                    self.w("gram", m + 1)
                    V.memset(cells[0:1, m:m + 1], 0.0)
                    mask = cst[:, C_GM + 256 * d:C_GM + 256 * d + 256].bitcast(i32).unsqueeze(1).to_broadcast([P, 2, 256])
                    inc(V.copy_predicated(G[d][:, q, :, :].rearrange("p (a b) c -> p a (b c)", a=2), mask,
                                          PB[3 - q % 2][:, :].rearrange("p (a b) -> p a b", a=2)), "gmask")

                def lasts(self):
                    V.tensor_copy(pl[:, 0:1], Pd[0][:, 0, P:P + 1])
                    inc(V.tensor_copy(pl[:, 1:2], Pd[1][:, 1, 0:1]), "plc")

                def bonus(self):
                    dve.wait_ge(s["y3"].sem, s["y3"].before(self.n))
                    self.w("bonm")
                    inc(V.tensor_tensor(bon[:], PB[6][:, 0:T], v, ALU.mult), "bonv")

            class Tail:

                def __init__(self, i):
                    self.i = i
                    self.w = lambda name, k=None: dve.wait_ge(s[name].sem, s[name].at(i, k))
                    self.col = lambda t, c: t[:, bass.ds(c + i, 1)]

                def centre(self):
                    self.w("ye")
                    self.w("mean")
                    inc(V.tensor_tensor(yc[:], ysb[:], PB[7][:, 0:T], ALU.subtract), "ycs")

                def variance(self):
                    self.w("var")
                    inc(V.tensor_scalar(st[:, 0:4], PB[7][:, 0:4], 1.0 / 64, GN_EPS, ALU.mult, ALU.add), "vars")

                def spread(self):
                    self.w("vpow")
                    for tb in range(2):
                        x = V.tensor_copy(rep[:, tb, :].rearrange("p (h f) -> p h f", h=2),
                                          st[:, 4 + 2 * tb:6 + 2 * tb].unsqueeze(2).to_broadcast([P, 2, 64]))
                    inc(x, "vrep")

                def scale(self):
                    w = self.w
                    w("vbc")
                    inc(V.tensor_tensor(yc[:], yc[:], PB[7][:, 0:T], ALU.mult), "y1")

                def add_bonus(self):
                    w = self.w
                    w("y2")
                    w("bonv")
                    inc(V.tensor_tensor(yc[:], yc[:], bon[:], ALU.add), "y3")

                def gate(self):
                    w = self.w
                    w("y3")
                    w("gg")
                    inc(V.tensor_tensor(yc[:], yc[:], gt[:], ALU.mult), "y4")

                def merge(self):
                    i = self.i
                    self.w("y4")
                    m = mrg[:, bass.ds(i, 1), :].rearrange("p a t -> p (a t)") if not isinstance(i, int) else mrg[:, i, :]
                    inc(V.tensor_tensor(m, m, yc[:], ALU.add), "y5")

            def pair(i, n, d1, d2):
                w = lambda name, k=None: dve.wait_ge(s[name].sem, s[name].at(i, k))
                nx = Prep(n) if n is not None else None
                cut_pair(1, d1, 0)
                for l in range(1, LV):
                    m = 1 << l
                    part = lambda t, par: t[:].rearrange("p g (n two m) -> p (g n) two m", two=2, m=m)[:, :, par, :]
                    small_ = lambda bank: bank[:, 0:T].rearrange("p (n m) -> p n m", m=m)
                    for d in range(2):
                        nn = 2 * (l - 1) + d + 1
                        if l < LV - 1:
                            w("ddm", nn)
                            inc(V.tensor_tensor(part(Dm[d], d), part(Dm[d], d).bitcast(f32), small_(PB[5 if d == 0 else 2]), ALU.add), "dup")
                        w("dtm", nn)
                        inc(V.tensor_tensor(part(DT[d], 1 - d), part(DT[d], 1 - d).bitcast(f32), small_(PB[6 if d == 0 else 7]), ALU.add), "dtup")
                        if l == 1 and d == 0:
                            cut_pair(1, d1, 1)
                        if l in (4, 5) and d == 1:
                            cut_pair(2, d1, l - 4)
                for c in range(2):
                    if nx and c == 0:
                        nx.neighbours()
                    elif nx:
                        nx.inverse(0)
                    w("ue", c + 1)
                    w("resm", c + 1)
                    inc(V.scalar_tensor_tensor(rhs[:].rearrange("p a b -> p (a b)"), U[:, c, :, :].rearrange("p a b -> p (a b)"), -2.0,
                                               PB[4][:, 0:T], ALU.mult, ALU.add), "rese")
                    if nx and c == 0:
                        nx.shift()
                    elif nx:
                        nx.inverse(1)
                    w("dum", c + 1)
                    u2 = U[:, c, :, :].rearrange("p a b -> p (a b)")
                    inc(V.tensor_tensor(u2, PB[5][:, T:2 * T], u2, ALU.add), "due")
                    if c == 0:
                        if nx:
                            nx.keys()
                        cut_pair(3, d1, 0)
                        w("smm")
                        for d in range(2):
                            x = V.scalar_tensor_tensor(Sm[:, d, :], PB[6][:, P * d:P * d + P], pl[:, d:d + 1], cst[:, C_SM:C_SM + P], ALU.mult, ALU.mult)
                        inc(x, "sme")
                        if nx:
                            nx.norm()
                        cut_pair(3, d1, 1)
                        if nx:
                            nx.products(0)
                            nx.products(1)
                            nx.modified()
                if nx:
                    nx.hats(0)
                tail = Tail(i)
                if nx is None:
                    tail.centre()
                    tail.variance()
                    tail.spread()
                    tail.scale()
                    tail.add_bonus()
                    tail.gate()
                    tail.merge()
                    return
                gram = Gram(n)
                cut_pair(0, d2, 0)
                nx.hats(1)
                gram.keep(0)
                tail.centre()
                gram.keep(1)
                tail.variance()
                gram.keep(2)
                gram.lasts()
                tail.spread()
                gram.keep(3)
                cut_pair(0, d2, 1)
                gram.keep(4)
                tail.scale()
                gram.keep(5)
                tail.add_bonus()
                gram.bonus()
                tail.gate()
                gram.keep(6)
                tail.merge()
                gram.keep(7)

            for j in range(4):
                cut_pair(j, 0)
            p0 = Prep(0)
            p0.neighbours()
            p0.shift()
            p0.keys()
            p0.norm()
            p0.products(0)
            p0.products(1)
            p0.modified()
            for d in range(2):
                p0.inverse(d)
                p0.hats(d)
            g0 = Gram(0)
            g0.lasts()
            for m in range(8):
                g0.keep(m)
                if m == 3:
                    g0.bonus()
            cut_pair(0, 1)
            with dve.Fori(0, PAIRS - 2, 1) as i:
                pair(i, i + 1, i + 1, i + 2)
            pair(PAIRS - 2, PAIRS - 1, PAIRS - 1, None)
            pair(PAIRS - 1, None, None, None)

            dve.wait_ge(s["y5"].sem, s["y5"].n(16))
            for k in range(KT):
                dve.wait_ge(s["mg_hi"].sem, s["mg_hi"].n(k + 1))
                V.tensor_tensor(xT[:, k, 1, :], mrg[:, k, :], xT[:, k, 0, :].bitcast(f32), ALU.subtract).then_inc(s["mg_lo"].sem, 1)
            with dve.Fori(0, 2, 1) as i:
                for j in range(8):
                    cut_lo(U_OUT + j + 2, 8 * i + U_OUT + j + 2)
                    if j % 4 == 3:
                        n = j // 4
                        dve.wait_ge(s["n_sq"].sem, s["n_sq"].n(8 + 4 * i + 2 * n + 2))
                        dve.wait_ge(s["ld_g"].sem, s["ld_g"].n(16))
                        chunk_cols = bass.ds(512 * n + 1024 * i, 512)
                        for b in range(2):
                            x = V.tensor_tensor(acc[:, b, chunk_cols], PB[2 * n + b][:, :], gain[:, chunk_cols], ALU.mult)
                        x.then_inc(s["o_cp"].sem, 1)

            rstd(16, 1, 4 * EPS)
            dve.wait_ge(s["n_pow"].sem, s["n_pow"].at(1))
            dve.wait_ge(s["ld_h"].sem, s["ld_h"].n(16))
            dve.wait_ge(s["o_cp"].sem, s["o_cp"].n(4))
            for b in range(2):
                for half in range(2):
                    hs = slice(1024 * half, 1024 * half + 1024)
                    V.scalar_tensor_tensor(hres[:, b, hs], acc[:, b, hs], small[:, 28 + b:29 + b], hres[:, b, hs], ALU.mult, ALU.add)\
                        .then_inc(s["m_h"].sem, 1)
            rstd(32, 2)
            diagonals(2, 32, "h_n")
            lo_parts("h_hi", "h_lo", PB[4:8], 96)
            V.memset(acc[:], 0.0).then_inc(s["acc0"].sem, 1)
            dve.wait_ge(s["acc0"].sem, s["acc0"].n(1))
            def chunk(i, last):
                for j in range(16):
                    u = U_FF + j
                    if not (last and j >= 14):
                        cut_lo(u + 2, 16 * i + u + 2)
                    if j < 8:
                        dve.wait_ge(s["up_re"].sem, s["up_re"].at(i, j + 1))
                        V.tensor_tensor(fs[:, j % 2, :], fa[:, j % 2, :], fa[:, j % 2, :], ALU.mult).then_inc(s["up_sq"].sem, 1)
                        dve.wait_ge(s["up_sq"].sem, s["up_sq"].at(i, j + 1))
                        dve.wait_ge(s["up_hi"].sem, s["up_hi"].at(i, j + 1))
                        V.tensor_tensor(ft[:, j, 1, :], fs[:, j % 2, :], ft[:, j, 0, :].bitcast(f32), ALU.subtract).then_inc(s["up_lo"].sem, 1)
                    elif j % 2 == 1:
                        n = (j - 9) // 2
                        dve.wait_ge(s["dn"].sem, s["dn"].at(i, n + 1))
                        for b in range(2):
                            x = V.tensor_tensor(acc[:, b, 512 * n:512 * n + 512], acc[:, b, 512 * n:512 * n + 512], PB[2 + 2 * (n % 3) + b][:, :], ALU.add)
                        x.then_inc(s["dn_acc"].sem, 1)

            with dve.Fori(0, FCH - 1, 1) as i:
                chunk(i, False)
            chunk(FCH - 1, True)
            rstd(48, 3)
            dve.wait_ge(s["n_pow"].sem, s["n_pow"].at(3))
            dve.wait_ge(s["ld_g2"].sem, s["ld_g2"].n(16))
            for b in range(2):
                V.scalar_tensor_tensor(acc[:, b, :], acc[:, b, :], small[:, 60 + b:61 + b], gain[:], ALU.mult, ALU.mult).then_inc(s["f_n"].sem, 1)
                dve.wait_ge(s["f_n"].sem, s["f_n"].n(b + 1))
                V.tensor_tensor(acc[:, b, :], hres[:, b, :], acc[:, b, :], ALU.add).then_inc(s["f_o"].sem, 1)

        @block.gpsimd
        def _(pool):
            Gp = nc.gpsimd

            def power(norm, col):
                pool.wait_ge(s["n_st"].sem, s["n_st"].at(norm))
                Gp.tensor_tensor(small[:, col + 12:col + 14], small[:, col + 10:col + 12], epsh[:, 0:2], ALU.pow).then_inc(s["n_pow"].sem, 1)

            pool.wait_ge(s["exp_ms"].sem, s["exp_ms"].n(1))
            power(0, 0)
            pool.wait_ge(s["ld_c2"].sem, s["ld_c2"].n(32))

            blocks = lambda t: t.rearrange("p (a b) -> p a b", a=2)

            def prep(n):
                w = lambda name, k=None: pool.wait_ge(s[name].sem, s[name].at(n, k))
                w("ssm")
                Gp.tensor_tensor(st[:, 4:8], st[:, 0:4], epsh[:, 0:4], ALU.pow).then_inc(s["rs"].sem, 1)
                incl = (Pd[0][:, :, 1:P + 1], Pd[1][:, :, 0:P])
                excl = (Pd[0][:, :, 0:P], Pd[1][:, :, 1:P + 1])
                pool.wait_ge(s["asc"].sem, s["asc"].before(n))
                for d in range(2):
                    w("scan", d + 1)
                    Gp.tensor_tensor(blocks(AR[d][:, 1, :]), blocks(sh[:, 0, :]), incl[d], ALU.mult)
                w("nkk")
                for d in range(2):
                    Gp.tensor_tensor(blocks(AR[d][:, 0, :]), blocks(kk[:]), excl[d], ALU.mult).then_inc(s["ar"].sem, 1)
                w("km2", 2)
                w("ss")
                Gp.tensor_tensor(nb[:, 1, :], km[0][:], km[1][:], ALU.add).then_inc(s["kbs"].sem, 1)
                w("kbs")
                w("rkd")
                Gp.tensor_tensor(rk[:], rk[:], nb[:, 1, :], ALU.mult).then_inc(s["t2"].sem, 1)

            def pair(i, n):
                w = lambda name, k=None: pool.wait_ge(s[name].sem, s[name].at(i, k))
                lm = lambda d, l: lmk[:, d, l, :].unsqueeze(1).to_broadcast([P, 4, P])
                for d in range(2):
                    w("gmask", 4 * d + 4)
                    pool.wait_ge(s["dum"].sem, s["dum"].before(i))
                    Gp.tensor_tensor(DT[d][:], G[d][:, :, 0, :], lm(d, 0), ALU.mult).then_inc(s["dt0"].sem, 1)
                    Gp.tensor_tensor(CT[d][:], G[d][:, :, 0, :], lm(d, 1), ALU.mult).then_inc(s["ctm"].sem, 1)
                for l in range(2, LV):
                    for d in range(2):
                        w("wmm", 2 * (l - 2) + d + 1)
                        Gp.tensor_tensor(CT[d][:], G[d][:, :, 0, :], lm(d, l), ALU.mult).then_inc(s["ctm"].sem, 1)
                    if l == 2:
                        pool.wait_ge(s["ym"].sem, s["ym"].before(i))
                        for d in range(2):
                            x = Gp.tensor_tensor(AS[:, d, :, :], AR[d][:, :, P * (1 - d):P * (1 - d) + P],
                                                 zero[:].unsqueeze(1).to_broadcast([P, 2, P]), ALU.add)
                        x.then_inc(s["asc"].sem, 1)
                    if l == 3:
                        w("gate_t")
                        Gp.tensor_tensor(gt[:], gt[:], gup[:], ALU.mult).then_inc(s["gg"].sem, 1)
                        w("gg", 1)
                        Gp.tensor_tensor(gt[:], gt[:], gup[:], ALU.add).then_inc(s["gg"].sem, 1)
                if n is not None:
                    prep(n)
                w("vars")
                Gp.tensor_tensor(st[:, 4:8], st[:, 0:4], epsh[:, 0:4], ALU.pow).then_inc(s["vpow"].sem, 1)

            prep(0)
            with pool.Fori(0, PAIRS - 1, 1) as i:
                pair(i, i + 1)
            pair(PAIRS - 1, None)
            for norm in (1, 2, 3):
                power(norm, 16 * norm)

        @block.tensor
        def _(pe):
            M = nc.tensor.matmul

            def unit_b(u_static, u, k0=0, k1=KT):
                if k0 == 0:
                    pe.wait_ge(w_lo.sem, w_lo.n(u + 1))
                bank = PB[u_static % 2]
                hi, lo = whi[:, u_static % 2, :], wlo[:, u_static % 2, :]
                for k in range(k0, k1):
                    h, l = hi[:, P * k:P * k + P], lo[:, P * k:P * k + P]
                    M(bank[:, 0:T], h, xT[:, k, 0, :], start=k == 0, stop=False)
                    M(bank[:, 0:T], h, xT[:, k, 1, :], start=False, stop=False)
                    x = M(bank[:, 0:T], l, xT[:, k, 0, :], start=False, stop=k == KT - 1)
                if k1 == KT:
                    x.then_inc(w_used.sem, 1)

            def unit_a(u_static, u, act_tiles, banks, first, last, done=None):
                pe.wait_ge(w_lo.sem, w_lo.n(u + 1))
                hi, lo = whi[:, u_static % 2, :], wlo[:, u_static % 2, :]
                for k in range(4):
                    t = act_tiles[k]
                    for b in range(2):
                        ah, al = t[:, 0, P * b:P * b + P], t[:, 1, P * b:P * b + P]
                        wh, wl = hi[:, 512 * k:512 * k + 512], lo[:, 512 * k:512 * k + 512]
                        f, e = first and k == 0, last and k == 3
                        M(banks[b][:, :], ah, wh, start=f, stop=False)
                        M(banks[b][:, :], ah, wl, start=False, stop=False)
                        x = M(banks[b][:, :], al, wh, start=False, stop=e)
                x.then_inc(w_used.sem, 1)
                return x

            pe.wait_ge(s["ld_c"].sem, s["ld_c"].n(16))
            pe.wait_ge(s["ld_p"].sem, s["ld_p"].n(16 * (len(PARAMS_A) + len(PARAMS_B) + 3)))
            for q in range(3):
                nc.tensor.transpose(PB[7][:, P * q:P * q + P], prow[:, q, :], ident).then_inc(s["prm_tp"].sem, 1)

            def token_tiles(src, banks, ready, free, done, u_static, u):
                products = lambda k2: (pe.wait_ge(s[free].sem, 2 * k2 + 2), unit_b(u_static, u, 2 * k2, 2 * k2 + 2))
                pe.wait_ge(s[ready].sem, 2)
                for k2 in range(KT // 2):
                    if k2 >= 4:
                        pe.wait_ge(s[free].sem, 2 * (k2 - 3))
                    for kk_ in range(2):
                        for b in range(2):
                            k = 2 * k2 + kk_
                            x = M(banks[k2 % 4][:, T * kk_ + P * b:T * kk_ + P * b + P], src[:, b, P * k:P * k + P], diag[:, b, :],
                                  start=True, stop=True)
                    x.then_inc(s[done].sem, 1)
                    if k2 >= 3:
                        products(k2 - 3)
                for k2 in range(5, 8):
                    products(k2)

            def scores(g, h):
                pe.wait_ge(s["k_r"].sem, s["k_r"].at(g))
                pe.wait_ge(s["q_r"].sem, s["q_r"].at(g, h + 1))
                pe.wait_ge(s["sc_m"].sem, s["sc_m"].at(g, h - 1) if h >= 2 else s["sc_m"].before(g))
                for qb in range(2):
                    x = M(PB[3 + h % 2][:, T * qb:T * qb + T], qr[:, h % 2, P * qb:P * qb + P], kr[:], start=True, stop=True)
                x.then_inc(s["sc"].sem, 1)

            def turn(g, h):
                pe.wait_ge(s["prn"].sem, s["prn"].at(g, h + 1))
                pe.wait_ge(s["p_T"].sem, s["p_T"].at(g, h) if h else s["p_T"].before(g))
                for sbk in range(2):
                    for qb in range(2):
                        x = nc.tensor.transpose(PB[5][:, T * sbk + P * qb:T * sbk + P * qb + P], prb[:, h % 2, qb, P * sbk:P * sbk + P], ident)
                x.then_inc(s["p_tp"].sem, 1)

            def weigh(g, h):
                pe.wait_ge(s["p_T"].sem, s["p_T"].at(g, h + 1))
                pe.wait_ge(s["v_tok"].sem, s["v_tok"].at(g))
                pe.wait_ge(s["o_ev"].sem, s["o_ev"].at(g, h) if h else s["o_ev"].before(g))
                for sbk in range(2):
                    x = M(PB[6][:, 0:T], vtok[:, sbk, :], prT[:, sbk, :], start=sbk == 0, stop=sbk == 1)
                x.then_inc(s["pv"].sem, 1)

            def step(j, g, hg, u_static, i=0):
                u = u_static + 6 * i
                if u_static >= 2:
                    pe.wait_ge(d_evac.sem, d_evac.n(u - 1))
                h = (j + 1) % 6
                if hg is not None and h < 4:
                    unit_b(u_static, u, 0, 4)
                    weigh(hg, h)
                    unit_b(u_static, u, 4, 8)
                else:
                    unit_b(u_static, u, 0, 8)
                if j == 2 and g is not None:
                    pe.wait_ge(d_evac.sem, d_evac.n(u))
                    for tb in range(2):
                        x = nc.tensor.transpose(PB[2][:, P * tb:P * tb + P], vf[:, P * tb:P * tb + P], ident)
                    x.then_inc(s["v_tp"].sem, 1)
                h = (j + 3) % 6
                if hg is not None and h < 4:
                    scores(hg, h)
                unit_b(u_static, u, 8, KT)
                h = (j + 2) % 6
                if hg is not None and h < 4:
                    turn(hg, h)

            token_tiles(xtok, PB[2:6], "x_n", "x_lo", "x_tp", 0, 0)
            for j in (1, 2):
                step(j, 0, None, j)
            with pe.Fori(0, KVH - 1, 1) as i:
                for j in (3, 4, 5):
                    step(j, i, i, j, i)
                for j in (0, 1, 2):
                    step(j, i + 1, i, 6 + j, i)
            for j in (3, 4, 5):
                step(j, KVH - 1, KVH - 1, 18 + j)
            for j in (0, 1, 2):
                step(j, None, KVH - 1, U_GA + j)
            pe.wait_ge(d_evac.sem, d_evac.n(U_GA + 2))
            unit_b(U_GA + 3, U_GA + 3)
            with pe.Fori(0, 3, 1) as i:
                for j in range(4):
                    pe.wait_ge(d_evac.sem, d_evac.n(4 * i + 4 + U_GA + j - 1))
                    unit_b(U_GA + j, 4 * i + 4 + U_GA + j)
            for j in range(6):
                pe.wait_ge(d_evac.sem, d_evac.n(U_LO + j - 1))
                unit_b(U_LO + j, U_LO + j)

            def dense(j, n, k0=0, k1=KT):
                if n is None:
                    return
                if k0 == 0:
                    pe.wait_ge(d_evac.sem, d_evac.n(4 * n + U_RW + j - 1))
                unit_b(U_RW + j, 4 * n + U_RW + j, k0, k1)

            inc = lambda x, name: x.then_inc(s[name].sem, 1)

            class Prep:

                def __init__(self, n):
                    self.n = n
                    self.w = lambda name, k=None: pe.wait_ge(s[name].sem, s[name].at(n, k))

                def lora_w(self):
                    n = self.n
                    pe.wait_ge(s["up_ld"].sem, s["up_ld"].n(16 * 5 * n + 80))
                    for q in range(2):
                        x = M(PB[2][:, T * q:T * q + T], upw[0:DL, q, :], lact[0:DL, q, :], start=True, stop=True)
                    inc(x, "lw")

                def lora_a(self):
                    for q in range(2):
                        x = M(PB[3][:, T * q:T * q + T], upw[0:DL, 2 + q, :], lact[0:DL, 2 + q, :], start=True, stop=True)
                    inc(x, "la")

                def squares(self):
                    self.w("sqd")
                    for tb in range(2):
                        x = M(PB[7][:, 2 * tb:2 * tb + 2], sq[:, P * tb:P * tb + P], hsel, start=True, stop=True)
                    inc(x, "ss")

                def norms(self):
                    self.w("rrep")
                    for tb in range(2):
                        x = M(PB[7][:, P * tb:P * tb + P], rep[:, tb, :], ident, start=True, stop=True)
                    inc(x, "rbc")

            class Gram:

                def __init__(self, n):
                    self.n = n
                    self.w = lambda name, k=None: pe.wait_ge(s[name].sem, s[name].at(n, k))

                def values(self):
                    pe.wait_ge(s["due"].sem, s["due"].before(self.n))
                    self.w("shifted")
                    for tb in range(2):
                        x = nc.tensor.transpose(PB[5][:, P * tb:P * tb + P], sh[:, 2, P * tb:P * tb + P], ident)
                    inc(x, "vtp")

                def gate(self):
                    pe.wait_ge(s["rese"].sem, s["rese"].before(self.n))
                    for q in range(2):
                        x = M(PB[4][:, 0:T], upg[:, q, :], gact[:, q, :], start=q == 0, stop=q == 1)
                    inc(x, "lg")

                def gram(self, m):
                    w = self.w
                    d, q = m // 4, m % 4
                    tb, h = q // 2, q % 2
                    if q == 0:
                        w("khs", d + 1)
                        w("bhs", d + 1)
                        w("ar", d + 1)
                    if m >= 2:
                        w("gmask", m - 1)
                    elif m == 0:
                        w("tas")
                    else:
                        w("tws")
                        pe.wait_ge(s["ye"].sem, s["ye"].before(self.n))
                    hp, ts = slice(64 * h, 64 * h + 64), slice(P * tb, P * tb + P)
                    for a, src in enumerate((bh[d], kh[d])):
                        x = M(PB[3 - q % 2][:, T * a:T * a + T], src[hp, ts], AR[d][hp, :, ts], start=True, stop=True)
                    inc(x, "gram")

                def bonus(self):
                    self.w("t2")
                    pe.wait_ge(s["sme"].sem, s["sme"].before(self.n))
                    x = M(PB[6][:, 0:T], ones_half, rk[:], start=True, stop=True)
                    inc(x, "bonm")

            def pair(i, n, d1, d2):
                w = lambda name, k=None: pe.wait_ge(s[name].sem, s[name].at(i, k))
                nx = Prep(n) if n is not None else None
                at = [0]

                def filler(count):
                    k = at[0]
                    at[0] = k + count
                    if k < KT:
                        dense(2, d1, k, min(k + count, KT))
                    if k + count > KT:
                        dense(3, d1, max(k - KT, 0), k + count - KT)

                filler(3)
                for d in range(2):
                    w("dt0", d + 1)
                    if d == 0:
                        w("vts")
                    else:
                        w("bonv")
                    for q in range(4):
                        x = nc.tensor.transpose(PB[5 + d][:, P * q:P * q + P], DT[d][:, q, :].bitcast(f32), ident)
                    inc(x, "d0p")
                    filler(4 if d == 0 else 2)

                def blocks_w(l, d):
                    nn = 2 * (l - 1) + d + 1
                    w("ctm", nn)
                    if l == 1:
                        w("d0", d + 1)
                        if d == 0:
                            w("gups")
                            w("gmask", 8)
                    else:
                        w("dup", nn - 2)
                        w("wev", nn - 2)
                    for q in range(4):
                        x = M(PB[4 - d][:, P * q:P * q + P], CT[d][:, q, :], Dm[d][:, q, :], start=True, stop=True)
                    inc(x, "wmm")

                def blocks_d(l, d):
                    m = 1 << l
                    part = lambda t, q, par: t[:, q, :].rearrange("p (n two m) -> p n two m", two=2, m=m)[:, :, par, :]
                    nn = 2 * (l - 1) + d + 1
                    w("wev", nn)
                    if l == 1:
                        w("d0", 2)
                        if d == 1:
                            pe.wait_ge(s["y1"].sem, s["y1"].before(i))
                    else:
                        w("dtup", nn - 2)
                    bd, bt = (PB[5], PB[6]) if d == 0 else (PB[2], PB[7])
                    if l < LV - 1:
                        for q in range(4):
                            x = M(bd[:, 64 * q:64 * q + 64].rearrange("p (n m) -> p n m", m=m), DT[d][:, q, :], part(W[d], q, d), start=True, stop=True)
                        inc(x, "ddm")
                    for q in range(4):
                        x = M(bt[:, 64 * q:64 * q + 64].rearrange("p (n m) -> p n m", m=m), W[d][:, q, :], part(DT[d], q, 1 - d), start=True, stop=True)
                    inc(x, "dtm")

                for l in range(1, LV):
                    blocks_w(l, 0)
                    if l > 1:
                        blocks_d(l - 1, 1)
                    filler(1 if l == LV - 1 else 2)
                    blocks_d(l, 0)
                    blocks_w(l, 1)
                    filler(2)
                blocks_d(LV - 1, 1)
                w("wev")
                for d in range(2):
                    ts = slice(P * d, P * d + P)
                    for a, src in enumerate((kh[d], bh[d])):
                        x = nc.tensor.transpose(PB[3][:, P * (2 * d + a):P * (2 * d + a) + P], src[:, ts], ident)
                inc(x, "kbtp")
                w("dup")
                w("asc")
                if nx:
                    nx.lora_w()
                for c in range(2):
                    if c == 1:
                        w("rese", 1)
                        w("due", 1)
                        w("sme")
                    first = True
                    for d in range(2):
                        tb = c if d == 0 else 1 - c
                        if c == 1:
                            M(PB[4][:, P * d:P * d + P], AS[:, d, 0, :], Sm[:, d, :], start=first, stop=False, skip_group_check=True)
                            first = False
                        for h in range(2):
                            q, o = 2 * tb + h, slice(64 * (2 * d + h), 64 * (2 * d + h) + 64)
                            x = M(PB[4][:, o], G[d][:, q, 2, :], Vt[:, tb, 64 * h:64 * h + 64], start=first, stop=False, skip_group_check=True)
                            first = False
                    inc(x, "rhsm")
                    cuts = ((0, 3), (3, 6), (6, 9), (9, 12)) if c == 0 else ((0, 4), (4, 8), (8, 12), (12, KT))
                    dense(c, d2, *cuts[0])
                    w("rhsc", c + 1)
                    if c == 0:
                        w("dtup")
                    for d in range(2):
                        tb = c if d == 0 else 1 - c
                        for h in range(2):
                            q, e = 2 * tb + h, 2 * d + h
                            x = M(PB[5][:, 64 * e:64 * e + 64], DT[d][:, q, :], rhs[:, e, :], start=True, stop=True)
                    inc(x, "um")
                    dense(c, d2, *cuts[1])
                    w("ue", c + 1)
                    for d in range(2):
                        tb = c if d == 0 else 1 - c
                        for h in range(2):
                            q, e = 2 * tb + h, 2 * d + h
                            x = M(PB[4][:, 64 * e:64 * e + 64], G[d][:, q, 0, :], U[:, c, e, :], start=False, stop=True, skip_group_check=True)
                    inc(x, "resm")
                    if nx and c == 0:
                        w("kbs2")
                        nx.lora_a()
                    dense(c, d2, *cuts[2])
                    w("rese", c + 1)
                    for d in range(2):
                        tb = c if d == 0 else 1 - c
                        for h in range(2):
                            q, e = 2 * tb + h, 2 * d + h
                            x = M(PB[5][:, T + 64 * e:T + 64 * e + 64], DT[d][:, q, :], rhs[:, e, :], start=True, stop=True)
                    inc(x, "dum")
                    dense(c, d2, *cuts[3])
                    if c == 0:
                        if nx:
                            nx.squares()
                        w("due", c + 1)
                        w("kbs2")
                        for d in range(2):
                            o = PB[6][:, P * d:P * d + P]
                            M(o, KB[:, 2 * d, :], Vt[:, d, :], start=True, stop=False)
                            x = M(o, KB[:, 2 * d + 1, :], U[:, 0, 2 * d:2 * d + 2, :].rearrange("p a b -> p (a b)"), start=False, stop=True)
                        inc(x, "smm")
                        dense(c, d2, 12, KT)
                        if nx:
                            nx.norms()
                    else:
                        w("due", 2)
                gram = Gram(n) if n is not None else None
                if gram:
                    gram.values()
                    nx.w("tws")
                for tb in range(2):
                    ts = slice(P * tb, P * tb + P)
                    d2nd = 1 if tb == 0 else 0
                    M(PB[2][:, ts], Sm[:, d2nd, :], AS[:, d2nd, 1, :], start=True, stop=False, skip_group_check=True)
                    for h in range(2):
                        hp, q = slice(64 * h, 64 * h + 64), 2 * tb + h
                        for d in range(2):
                            c = tb if d == 0 else 1 - tb
                            M(PB[2][hp, ts], Vt[:, tb, hp], G[d][:, q, 3, :], start=False, stop=False, skip_group_check=True)
                            x = M(PB[2][hp, ts], U[:, c, 2 * d + h, :], G[d][:, q, 1, :], start=False, stop=d == 1, skip_group_check=True)
                inc(x, "ym")
                if gram:
                    gram.gate()
                    gram.gram(0)
                    nx.w("nkk")
                w("ye")
                x = M(PB[7][:, 0:T], ones_mean, ysb[:], start=True, stop=True)
                inc(x, "mean")
                if gram:
                    gram.gram(1)
                    gram.gram(2)
                w("ysqs")
                for tb in range(2):
                    x = M(PB[7][:, 2 * tb:2 * tb + 2], ysq[:, P * tb:P * tb + P], hsel, start=True, stop=True)
                inc(x, "var")
                if gram:
                    gram.gram(3)
                    gram.gram(4)
                    gram.bonus()
                w("vrep")
                for tb in range(2):
                    x = M(PB[7][:, P * tb:P * tb + P], rep[:, tb, :], ident, start=True, stop=True)
                inc(x, "vbc")
                if gram:
                    for m in range(5, 8):
                        gram.gram(m)

            for j in range(4):
                dense(j, 0)
            pe.wait_ge(s["lo_fin"].sem, s["lo_fin"].n(1))
            pe.wait_ge(s["lo_sh"].sem, s["lo_sh"].n(6))
            p0 = Prep(0)
            p0.lora_w()
            p0.lora_a()
            p0.squares()
            p0.norms()
            g0 = Gram(0)
            g0.values()
            g0.gate()
            for m in range(8):
                g0.gram(m)
                if m == 3:
                    g0.bonus()
            for j in range(2):
                dense(j, 1)
            with pe.Fori(0, PAIRS - 2, 1) as i:
                pair(i, i + 1, i + 1, i + 2)
            pair(PAIRS - 2, PAIRS - 1, PAIRS - 1, None)
            pair(PAIRS - 1, None, None, None)

            pe.wait_ge(s["mg_lo"].sem, s["mg_lo"].n(16))
            with pe.Fori(0, 2, 1) as i:
                for j in range(8):
                    n, kc = j // 4, j % 4
                    if kc == 0:
                        pe.wait_ge(s["o_cp"].sem, s["o_cp"].n(2 * i))
                    x = unit_a(U_OUT + j, 8 * i + U_OUT + j, [xT[:, 4 * kc + k, :, :] for k in range(4)], PB[2 * n:2 * n + 2], kc == 0, kc == 3)
                    if kc == 3:
                        pe.wait_ge(w_used.sem, w_used.n(8 * i + U_OUT + j + 1))
                        pe.sem_inc(s["om"].sem, 1)
            pe.wait_ge(s["o_cp"].sem, s["o_cp"].n(4))
            token_tiles(hres, PB[4:8], "h_n", "h_lo", "h_tp", U_FF, U_FF)
            def ffn_chunk(i, first_unit):
                for j in range(first_unit, 8):
                    pe.wait_ge(s["up_re"].sem, s["up_re"].at(i, j - 1) if j >= 2 else s["up_re"].before(i))
                    unit_b(U_FF + j, 16 * i + U_FF + j)
                for j in range(8):
                    n, kc = j // 2, j % 2
                    pe.wait_ge(s["up_lo"].sem, s["up_lo"].at(i, 4 * kc + 4))
                    if kc == 0:
                        pe.wait_ge(s["dn_acc"].sem, s["dn_acc"].at(i, n - 2) if n >= 3 else s["dn_acc"].before(i))
                    x = unit_a(U_FF + 8 + j, 16 * i + U_FF + 8 + j, [ft[:, 4 * kc + k, :, :] for k in range(4)],
                               PB[2 + 2 * (n % 3):4 + 2 * (n % 3)], kc == 0, kc == 1)
                    if kc == 1:
                        pe.wait_ge(w_used.sem, w_used.n(16 * i + U_FF + 8 + j + 1))
                        pe.sem_inc(s["dn"].sem, 1)

            ffn_chunk(0, 1)
            with pe.Fori(0, FCH - 1, 1) as i:
                ffn_chunk(i + 1, 0)


INS = ["x", "norm_pre_mix", "w_in", "mu_shift", "attn_sink", "w0_fwd", "w_up_fwd", "w0_bwd", "w_up_bwd", "a0_fwd", "a_up_fwd",
       "a0_bwd", "a_up_bwd", "g_up", "k_k", "k_a", "r_k", "ln_x_gain", "ln_x_bias", "w_out", "norm_post_mix", "norm_pre_ffn",
       "w_ffn_up", "w_ffn_down", "norm_post_ffn"]


def kernel(**inputs):
    import numpy as _np
    import concourse.bacc as _bacc
    from concourse import mybir as _mybir
    from concourse.bass_utils import run_bass_kernel_spmd as _run

    nc = _bacc.Bacc("TRN2", target_bir_lowering=False, num_devices=1)
    arrays, aps = {}, {}
    c, a, lm = constants()
    for name, arr in [(n, _np.ascontiguousarray(inputs[n])) for n in INS] + [("constants", c), ("attn_constants", a), ("level_masks", lm)]:
        arrays[f"in_{name}"] = arr
        aps[name] = nc.dram_tensor(f"in_{name}", arr.shape, _mybir.dt.from_np(arr.dtype), kind="ExternalInput").ap()
    out = nc.dram_tensor("out", (1, T, D), _mybir.dt.float32, kind="ExternalOutput").ap()
    block_kernel(nc, aps, aps["constants"], aps["attn_constants"], aps["level_masks"], out)
    r = _run(nc, [arrays], core_ids=[0])
    return r.results[0]["out"]
```
